# Optimizing a Trainium2 kernel written in Bass

```python
import math
import jax, jax.numpy as jnp
from jax import lax
import numpy as np
import jax
import jax.numpy as jnp

D_MODEL = 1024
BATCH = 1
SEQ = 512
DEPTH = 2

GRID_W = 64
CTX_LEN = 256
HEAD_DIM = 64
ROPE_THETA = 10000.0
Q_BLOCK = 128
EPS = 1e-6

B_WIDTH = D_MODEL // 4
B_GROUPS = 4
B_GROUP_DIM = B_WIDTH // B_GROUPS
POOL_WINDOWS = (2, 4, 8, 16)
A_WIDTH = D_MODEL - B_WIDTH
A_Q_HEADS = A_WIDTH // HEAD_DIM
A_KV_HEADS = A_Q_HEADS // 3
A_GROUP = A_Q_HEADS // A_KV_HEADS
A_KV_WIDTH = A_KV_HEADS * HEAD_DIM
A_IN_WIDTH = A_WIDTH + 2 * A_KV_WIDTH + B_WIDTH
D_CH = D_MODEL // 4
C_QK_DIM = HEAD_DIM
C_V_DIM = 2 * HEAD_DIM
C_WIDTH = D_MODEL - D_CH
C_HEADS = C_WIDTH // C_V_DIM
CONV_WIDTH = 31
C_IN_WIDTH = 3 * C_WIDTH + 2 * D_CH
FFN_HIDDEN = -(-8 * D_MODEL // (3 * 256)) * 256
ALPHA = (2.0 * DEPTH) ** 0.25
BETA = (8.0 * DEPTH) ** -0.25

F32 = jnp.float32


def layer_norm(x, g, b):
    xf = x.astype(F32)
    mu = jnp.mean(xf, axis=-1, keepdims=True)
    var = jnp.mean(jnp.square(xf - mu), axis=-1, keepdims=True)
    return ((xf - mu) * lax.rsqrt(var + EPS) * g.astype(F32) + b.astype(F32)).astype(x.dtype)

def rms_norm(x, g):
    xf = x.astype(F32)
    return (xf * lax.rsqrt(jnp.mean(jnp.square(xf), axis=-1, keepdims=True) + EPS) * g.astype(F32)).astype(x.dtype)

def axial_rope_tables(n_tokens):
    rows = n_tokens // GRID_W
    row = jnp.repeat(jnp.arange(rows, dtype=F32), GRID_W)
    col = jnp.tile(jnp.arange(GRID_W, dtype=F32), rows)
    axis_dim = HEAD_DIM // 2
    freqs = ROPE_THETA ** (-jnp.arange(0, axis_dim, 2, dtype=F32) / axis_dim)
    ang = jnp.concatenate([row[:, None] * freqs, col[:, None] * freqs], axis=-1)
    return jnp.cos(ang), jnp.sin(ang)

def apply_axial_rope(x, cos, sin):
    q = HEAD_DIM // 4
    xf = x.astype(F32)

    def rot(xa, c, s):
        x1, x2 = xa[..., :q], xa[..., q:]
        return jnp.concatenate([x1 * c - x2 * s, x2 * c + x1 * s], axis=-1)

    out = jnp.concatenate([rot(xf[..., :2 * q], cos[:, :q], sin[:, :q]),
                           rot(xf[..., 2 * q:], cos[:, q:], sin[:, q:])], axis=-1)
    return out.astype(x.dtype)

def map_query_blocks(fn, q):
    t = q.shape[-2]
    nb = t // Q_BLOCK
    qb = jnp.moveaxis(q.reshape(q.shape[:-2] + (nb, Q_BLOCK, q.shape[-1])), -3, 0)
    out = jnp.moveaxis(lax.map(fn, qb), 0, -3)
    return out.reshape(out.shape[:-3] + (t, out.shape[-1]))

def gqa_attend(q, k, v):
    s = jnp.einsum('bkgqd,bksd->bkgqs', q, k, preferred_element_type=F32) * (HEAD_DIM ** -0.5)
    p = jax.nn.softmax(s, axis=-1)
    return jnp.einsum('bkgqs,bksd->bkgqd', p.astype(v.dtype), v)

def diff_attend(q, k, v, lam):
    s = jnp.einsum('bhiqd,bhisd->bhiqs', q, k, preferred_element_type=F32) * (C_QK_DIM ** -0.5)
    p = jax.nn.softmax(s, axis=-1)
    a = p[:, :, 0] - lam * p[:, :, 1]
    return jnp.einsum('bhqs,bhsd->bhqd', a.astype(v.dtype), v)

def centred_window_mean(x, w):
    t_len = x.shape[1]
    cs = jnp.pad(jnp.cumsum(x.astype(F32), axis=1), ((0, 0), (1, 0), (0, 0)))
    t = jnp.arange(t_len)
    lo = jnp.clip(t - w // 2, 0, t_len)
    hi = jnp.clip(t + (w - 1 - w // 2) + 1, 0, t_len)
    s = jnp.take(cs, hi, axis=1) - jnp.take(cs, lo, axis=1)
    return (s / (hi - lo).astype(F32)[None, :, None]).astype(x.dtype)

def pool_mixer(u, w_pool, pool_scale):
    bsz, n, _ = u.shape
    ug = u.reshape(bsz, n, B_GROUPS, B_GROUP_DIM)
    pooled = jnp.stack([centred_window_mean(ug[:, :, g], w) - ug[:, :, g]
                        for g, w in enumerate(POOL_WINDOWS)], axis=2)
    mixed = jnp.einsum('bngc,gcd->bngd', pooled, w_pool)
    return mixed.reshape(bsz, n, B_WIDTH) * pool_scale

def conformer_conv(u, conv_w, conv_b, ln_g, ln_b):
    a, g = jnp.split(u, 2, axis=-1)
    z = a * jax.nn.sigmoid(g)
    z = lax.conv_general_dilated(z, conv_w[:, None, :].astype(z.dtype), window_strides=(1,),
                                 padding=[(CONV_WIDTH // 2, CONV_WIDTH // 2)],
                                 dimension_numbers=('NWC', 'WIO', 'NWC'),
                                 feature_group_count=D_CH) + conv_b
    return jax.nn.silu(layer_norm(z, ln_g, ln_b))

def swiglu(h, w_in, w_out):
    a, g = jnp.split(h @ w_in, 2, axis=-1)
    return (jax.nn.silu(g) * a) @ w_out

def mixer_ab(h, hc, w_in, q_gain, k_gain, w_pool, pool_scale, w_out, cos, sin, with_ctx_out):
    bsz, n_lat, _ = h.shape
    n_ctx = hc.shape[1]
    n = n_ctx + n_lat
    p = jnp.concatenate([hc, h], axis=1) @ w_in
    q, k, v, u = jnp.split(p, [A_WIDTH, A_WIDTH + A_KV_WIDTH, A_WIDTH + 2 * A_KV_WIDTH], axis=-1)
    q = rms_norm(q.reshape(bsz, n, A_KV_HEADS, A_GROUP, HEAD_DIM), q_gain).transpose(0, 2, 3, 1, 4)
    k = rms_norm(k.reshape(bsz, n, A_KV_HEADS, HEAD_DIM), k_gain).transpose(0, 2, 1, 3)
    v = v.reshape(bsz, n, A_KV_HEADS, HEAD_DIM).transpose(0, 2, 1, 3)
    k_all = jnp.concatenate([k[..., :n_ctx, :], apply_axial_rope(k[..., n_ctx:, :], cos, sin)], axis=-2)
    q_lat = apply_axial_rope(q[..., n_ctx:, :], cos, sin)
    o_lat = map_query_blocks(lambda qb: gqa_attend(qb, k_all, v), q_lat)

    def finish(o, uu):
        o = o.transpose(0, 3, 1, 2, 4).reshape(o.shape[0], o.shape[3], A_WIDTH)
        return jnp.concatenate([o, pool_mixer(uu, w_pool, pool_scale)], axis=-1) @ w_out

    y = finish(o_lat, u[:, n_ctx:])
    yc = None
    if with_ctx_out:
        o_ctx = gqa_attend(q[..., :n_ctx, :], k[..., :n_ctx, :], v[:, :, :n_ctx])
        yc = finish(o_ctx, u[:, :n_ctx])
    return y, yc

def mixer_cd(h, hc, w_in, lq1, lk1, lq2, lk2, subln_gain, conv_w, conv_b, conv_ln_g, conv_ln_b,
             w_out, cos, sin, lam_init, with_ctx_out):
    bsz, n_lat, _ = h.shape
    n_ctx = hc.shape[1]
    n = n_ctx + n_lat
    p = jnp.concatenate([hc, h], axis=1) @ w_in
    q, k, v, u = jnp.split(p, [C_WIDTH, 2 * C_WIDTH, 3 * C_WIDTH], axis=-1)
    q = q.reshape(bsz, n, C_HEADS, 2, C_QK_DIM).transpose(0, 2, 3, 1, 4)
    k = k.reshape(bsz, n, C_HEADS, 2, C_QK_DIM).transpose(0, 2, 3, 1, 4)
    v = v.reshape(bsz, n, C_HEADS, C_V_DIM).transpose(0, 2, 1, 3)
    lam = (jnp.exp(jnp.sum(lq1.astype(F32) * lk1.astype(F32)))
           - jnp.exp(jnp.sum(lq2.astype(F32) * lk2.astype(F32))) + lam_init)
    k_all = jnp.concatenate([k[..., :n_ctx, :], apply_axial_rope(k[..., n_ctx:, :], cos, sin)], axis=-2)
    q_lat = apply_axial_rope(q[..., n_ctx:, :], cos, sin)
    o_lat = map_query_blocks(lambda qb: diff_attend(qb, k_all, v, lam), q_lat)

    def finish(o, uu):
        o = rms_norm(o, subln_gain) * (1.0 - lam_init)
        o = o.transpose(0, 2, 1, 3).reshape(o.shape[0], o.shape[2], C_WIDTH)
        conv = conformer_conv(uu, conv_w, conv_b, conv_ln_g, conv_ln_b)
        return jnp.concatenate([o, conv], axis=-1) @ w_out

    y = finish(o_lat, u[:, n_ctx:])
    yc = None
    if with_ctx_out:
        o_ctx = diff_attend(q[..., :n_ctx, :], k[..., :n_ctx, :], v[:, :, :n_ctx], lam)
        yc = finish(o_ctx, u[:, :n_ctx])
    return y, yc

def first_inputs(seed: int = 0) -> dict:
    key = jax.random.key(seed)
    ks = iter(jax.random.split(key, 32))
    n_even = (DEPTH + 1) // 2
    n_odd = DEPTH // 2

    def nrm(shape, scale):
        return jax.random.normal(next(ks), shape, F32) * scale

    def gain(shape):
        return 1.0 + nrm(shape, 0.05)

    return {
        'x': nrm((BATCH, SEQ, D_MODEL), 1.0),
        'c': nrm((BATCH, D_MODEL), 1.0),
        'ctx': nrm((BATCH, CTX_LEN, D_MODEL), 1.0),
        'c_ctx': nrm((D_MODEL,), 1.0),
        'ab_w_in': nrm((n_even, D_MODEL, A_IN_WIDTH), D_MODEL ** -0.5),
        'ab_q_gain': gain((n_even, HEAD_DIM)),
        'ab_k_gain': gain((n_even, HEAD_DIM)),
        'ab_w_pool': nrm((n_even, B_GROUPS, B_GROUP_DIM, B_GROUP_DIM), B_GROUP_DIM ** -0.5),
        'ab_pool_scale': gain((n_even, B_WIDTH)),
        'ab_w_out': nrm((n_even, D_MODEL, D_MODEL), BETA * D_MODEL ** -0.5),
        'cd_w_in': nrm((n_odd, D_MODEL, C_IN_WIDTH), D_MODEL ** -0.5),
        'cd_lambda_q1': nrm((n_odd, C_QK_DIM), 0.1),
        'cd_lambda_k1': nrm((n_odd, C_QK_DIM), 0.1),
        'cd_lambda_q2': nrm((n_odd, C_QK_DIM), 0.1),
        'cd_lambda_k2': nrm((n_odd, C_QK_DIM), 0.1),
        'cd_subln_gain': gain((n_odd, C_V_DIM)),
        'cd_conv_w': nrm((n_odd, CONV_WIDTH, D_CH), CONV_WIDTH ** -0.5),
        'cd_conv_b': nrm((n_odd, D_CH), 0.02),
        'cd_conv_ln_g': gain((n_odd, D_CH)),
        'cd_conv_ln_b': nrm((n_odd, D_CH), 0.02),
        'cd_w_out': nrm((n_odd, D_MODEL, D_MODEL), BETA * D_MODEL ** -0.5),
        'ada_w': nrm((DEPTH, D_MODEL, 6 * D_MODEL), 0.5 * D_MODEL ** -0.5),
        'ada_b': nrm((DEPTH, 6 * D_MODEL), 0.02),
        'ln1_g': gain((DEPTH, D_MODEL)),
        'ln1_b': nrm((DEPTH, D_MODEL), 0.02),
        'ln2_g': gain((DEPTH, D_MODEL)),
        'ln2_b': nrm((DEPTH, D_MODEL), 0.02),
        'ffn_w_in': nrm((DEPTH, D_MODEL, 2 * FFN_HIDDEN), D_MODEL ** -0.5),
        'ffn_w_out': nrm((DEPTH, FFN_HIDDEN, D_MODEL), BETA * FFN_HIDDEN ** -0.5),
    }

def first_block(x, c, ctx, c_ctx, ab_w_in, ab_q_gain, ab_k_gain, ab_w_pool, ab_pool_scale, ab_w_out,
              cd_w_in, cd_lambda_q1, cd_lambda_k1, cd_lambda_q2, cd_lambda_k2, cd_subln_gain,
              cd_conv_w, cd_conv_b, cd_conv_ln_g, cd_conv_ln_b, cd_w_out,
              ada_w, ada_b, ln1_g, ln1_b, ln2_g, ln2_b, ffn_w_in, ffn_w_out):
    cos, sin = axial_rope_tables(x.shape[1])
    xc = ctx
    for l in range(DEPTH):
        with_ctx_out = l < DEPTH - 1
        mod = (jax.nn.silu(c) @ ada_w[l] + ada_b[l])[:, None, :]
        mod_c = (jax.nn.silu(c_ctx) @ ada_w[l] + ada_b[l])[None, None, :]
        sh1, sc1, g1, sh2, sc2, g2 = jnp.split(mod, 6, axis=-1)
        csh1, csc1, cg1, csh2, csc2, cg2 = jnp.split(mod_c, 6, axis=-1)
        h = x * (1.0 + sc1) + sh1
        hc = xc * (1.0 + csc1) + csh1
        i = l // 2
        if l % 2 == 0:
            y, yc = mixer_ab(h, hc, ab_w_in[i], ab_q_gain[i], ab_k_gain[i], ab_w_pool[i], ab_pool_scale[i],
                             ab_w_out[i], cos, sin, with_ctx_out)
        else:
            lam_init = 0.8 - 0.6 * math.exp(-0.3 * l)
            y, yc = mixer_cd(h, hc, cd_w_in[i], cd_lambda_q1[i], cd_lambda_k1[i], cd_lambda_q2[i], cd_lambda_k2[i],
                             cd_subln_gain[i], cd_conv_w[i], cd_conv_b[i], cd_conv_ln_g[i], cd_conv_ln_b[i],
                             cd_w_out[i], cos, sin, lam_init, with_ctx_out)
        x = layer_norm(ALPHA * x + g1 * y, ln1_g[l], ln1_b[l])
        x = layer_norm(ALPHA * x + g2 * swiglu(x * (1.0 + sc2) + sh2, ffn_w_in[l], ffn_w_out[l]), ln2_g[l], ln2_b[l])
        if with_ctx_out:
            xc = layer_norm(ALPHA * xc + cg1 * yc, ln1_g[l], ln1_b[l])
            xc = layer_norm(ALPHA * xc + cg2 * swiglu(xc * (1.0 + csc2) + csh2, ffn_w_in[l], ffn_w_out[l]),
                            ln2_g[l], ln2_b[l])
    return x


RET_HEADS = 4
RET_HEAD_DIM = D_MODEL // 2 // RET_HEADS
RET_VALUE_DIM = D_MODEL // 2 // RET_HEADS
RET_CHUNK = 128
RET_WIDTH = RET_HEADS * RET_VALUE_DIM
WIN_Q_HEADS = 8
WIN_KV_HEADS = 2
WIN_HEAD_DIM = D_MODEL // 2 // WIN_Q_HEADS
WINDOW = 128
WIN_BLOCK = WINDOW
WIN_WIDTH = WIN_Q_HEADS * WIN_HEAD_DIM
FOURIER_GROUPS = 4
N_GROUPS = 4
EXPERTS_PER_GROUP = 8
N_EXPERTS = N_GROUPS * EXPERTS_PER_GROUP
TOP_K = 2
EXPERT_HIDDEN = D_MODEL // 2
LN_EPS = 1e-5
GN_EPS = 1e-6
DEEPNORM_ALPHA = (2.0 * DEPTH) ** 0.25
DEEPNORM_BETA = (8.0 * DEPTH) ** -0.25
N_EVEN = (DEPTH + 1) // 2
N_ODD = DEPTH // 2
RET_QK = RET_HEADS * RET_HEAD_DIM
WIN_KV = WIN_KV_HEADS * WIN_HEAD_DIM
EVEN_SPLITS = tuple(np.cumsum([RET_QK, RET_QK, RET_WIDTH, RET_WIDTH, WIN_WIDTH, WIN_KV])[:].tolist())
IN_EVEN = 2 * RET_QK + 2 * RET_WIDTH + WIN_WIDTH + 2 * WIN_KV


def layer_norm_2(x, gain, bias):
    xf = x.astype(jnp.float32)
    mu = jnp.mean(xf, axis=-1, keepdims=True)
    var = jnp.mean(jnp.square(xf - mu), axis=-1, keepdims=True)
    y = (xf - mu) * lax.rsqrt(var + LN_EPS) * gain.astype(jnp.float32) + bias.astype(jnp.float32)
    return y.astype(x.dtype)

def rope(x, pos):
    d = x.shape[-1]
    half = d // 2
    inv = ROPE_THETA ** (-jnp.arange(half, dtype=jnp.float32) / half)
    ang = pos.astype(jnp.float32)[:, None] * inv[None, :]
    cos = jnp.cos(ang)[None, :, None, :]
    sin = jnp.sin(ang)[None, :, None, :]
    xf = x.astype(jnp.float32)
    x1, x2 = xf[..., :half], xf[..., half:]
    return jnp.concatenate([x1 * cos - x2 * sin, x1 * sin + x2 * cos], axis=-1).astype(x.dtype)

def retention_one_direction(q, k, v, log_gamma, include_diag):
    B, H, S, dk = q.shape
    dv = v.shape[-1]
    C = RET_CHUNK
    NC = S // C
    qc = q.reshape(B, H, NC, C, dk)
    kc = k.reshape(B, H, NC, C, dk)
    vc = v.reshape(B, H, NC, C, dv)
    pos = jnp.arange(C, dtype=jnp.float32)
    lg = log_gamma[:, None, None]
    diff = pos[:, None] - pos[None, :]
    mask = diff >= 0 if include_diag else diff > 0
    dmat = jnp.where(mask[None], jnp.exp(lg * jnp.maximum(diff, 0.0)[None]), 0.0)
    scores = jnp.einsum('bhncd,bhnmd->bhncm', qc, kc) * dmat[None, :, None]
    y_inner = jnp.einsum('bhncm,bhnmv->bhncv', scores, vc)
    zeta = jnp.exp(log_gamma[:, None] * (C - 1.0 - pos)[None])
    kv = jnp.einsum('bhnmd,bhnmv->nbhdv', kc * zeta[None, :, None, :, None], vc)
    chunk_decay = jnp.exp(log_gamma * C)[None, :, None, None]

    def step(state, kv_n):
        return state * chunk_decay + kv_n, state

    _, r_prev = lax.scan(step, jnp.zeros((B, H, dk, dv), jnp.float32), kv)
    xi = jnp.exp(log_gamma[:, None] * (pos + 1.0)[None])
    y_cross = jnp.einsum('bhncd,nbhdv->bhncv', qc * xi[None, :, None, :, None], r_prev)
    return (y_inner + y_cross).reshape(B, H, S, dv)

def bidirectional_retention(q, k, v, decay_logit):
    qf = jnp.transpose(q.astype(jnp.float32), (0, 2, 1, 3))
    kf = jnp.transpose(k.astype(jnp.float32), (0, 2, 1, 3))
    vf = jnp.transpose(v.astype(jnp.float32), (0, 2, 1, 3))
    log_gamma = jax.nn.log_sigmoid(decay_logit.astype(jnp.float32))
    fwd = retention_one_direction(qf, kf, vf, log_gamma[0], True)
    bwd = jnp.flip(retention_one_direction(jnp.flip(qf, 2), jnp.flip(kf, 2), jnp.flip(vf, 2),
                                           log_gamma[1], False), 2)
    return jnp.transpose(fwd + bwd, (0, 2, 1, 3))

def banded_keys(t):
    B, S, Hkv, d = t.shape
    NB = S // WIN_BLOCK
    tp = jnp.pad(t, ((0, 0), (WINDOW, WINDOW), (0, 0), (0, 0))).reshape(B, NB + 2, WIN_BLOCK, Hkv, d)
    return jnp.concatenate([tp[:, :-2], tp[:, 1:-1], tp[:, 2:]], axis=2)

def window_attention_with_sink(q, k, v, sink_logit):
    B, S, Hq, d = q.shape
    Hkv = k.shape[2]
    G = Hq // Hkv
    NB = S // WIN_BLOCK
    qb = q.reshape(B, NB, WIN_BLOCK, Hkv, G, d)
    kb = banded_keys(k)
    vb = banded_keys(v)
    s = jnp.einsum('bnqhgd,bnkhd->bnhgqk', qb, kb).astype(jnp.float32)
    i = jnp.arange(WIN_BLOCK)[:, None]
    j = jnp.arange(3 * WIN_BLOCK)[None, :]
    rel_ok = jnp.abs(i - j + WINDOW) <= WINDOW
    kpos = jnp.arange(NB)[:, None] * WIN_BLOCK + jnp.arange(3 * WIN_BLOCK)[None, :] - WINDOW
    in_ok = (kpos >= 0) & (kpos < S)
    mask = rel_ok[None] & in_ok[:, None, :]
    s = jnp.where(mask[None, :, None, None], s, -1e30)
    sink = jnp.broadcast_to(sink_logit.astype(jnp.float32).reshape(1, 1, Hkv, G, 1, 1), s.shape[:-1] + (1,))
    p = jax.nn.softmax(jnp.concatenate([s, sink], axis=-1), axis=-1)[..., :-1]
    o = jnp.einsum('bnhgqk,bnkhd->bnqhgd', p.astype(v.dtype), vb)
    return o.reshape(B, S, Hq * d)

def even_mixer(x, w_in, decay_logit, gn_gain, sink_logit, w_out, pos):
    B, S, _ = x.shape
    h = x @ w_in
    qa, ka, va, ga, qb, kb, vb = jnp.split(h, EVEN_SPLITS, axis=-1)
    qa = rope(qa.reshape(B, S, RET_HEADS, RET_HEAD_DIM), pos)
    ka = rope(ka.reshape(B, S, RET_HEADS, RET_HEAD_DIM), pos) * (RET_HEAD_DIM ** -0.5)
    va = va.reshape(B, S, RET_HEADS, RET_VALUE_DIM)
    ya = bidirectional_retention(qa, ka, va, decay_logit)
    mu = jnp.mean(ya, axis=-1, keepdims=True)
    var = jnp.mean(jnp.square(ya - mu), axis=-1, keepdims=True)
    ya = ((ya - mu) * lax.rsqrt(var + GN_EPS)).reshape(B, S, RET_WIDTH) * gn_gain.astype(jnp.float32)
    ya = jax.nn.silu(ga) * ya.astype(x.dtype)
    qb = rope(qb.reshape(B, S, WIN_Q_HEADS, WIN_HEAD_DIM), pos) * (WIN_HEAD_DIM ** -0.5)
    kb = rope(kb.reshape(B, S, WIN_KV_HEADS, WIN_HEAD_DIM), pos)
    vb = vb.reshape(B, S, WIN_KV_HEADS, WIN_HEAD_DIM)
    yb = window_attention_with_sink(qb, kb, vb, sink_logit)
    return jnp.concatenate([ya, yb], axis=-1) @ w_out

def fourier_mixer(x, w_out):
    B, S, D = x.shape
    xg = x.astype(jnp.float32).reshape(B, S, FOURIER_GROUPS, D // FOURIER_GROUPS)
    y = jnp.fft.fft2(xg, axes=(1, 3), norm='ortho').real.reshape(B, S, D)
    return y.astype(x.dtype) @ w_out

def hierarchical_moe(x, w_coarse, b_coarse, w_fine, b_fine, w_gate, w_up, w_down):
    B, S, D = x.shape
    xt = x.reshape(B * S, D)
    T = B * S
    coarse = (xt @ w_coarse + b_coarse).astype(jnp.float32)
    p_group, g_idx = lax.top_k(jax.nn.softmax(coarse, axis=-1), 1)
    fine = (xt @ w_fine + b_fine).astype(jnp.float32).reshape(T, N_GROUPS, EXPERTS_PER_GROUP)
    fine_g = jnp.take_along_axis(fine, g_idx[:, :, None], axis=1)[:, 0]
    top_val, top_idx = lax.top_k(fine_g, TOP_K)
    gate = jax.nn.softmax(top_val, axis=-1) * p_group
    expert_id = (g_idx * EXPERTS_PER_GROUP + top_idx).reshape(-1)
    order = jnp.argsort(expert_id)
    tok = order // TOP_K
    sizes = jnp.bincount(expert_id, length=N_EXPERTS).astype(jnp.int32)
    xs = xt[tok]
    hid = jax.nn.silu(lax.ragged_dot(xs, w_gate, sizes)) * lax.ragged_dot(xs, w_up, sizes)
    ys = lax.ragged_dot(hid, w_down, sizes) * gate.reshape(-1)[order][:, None].astype(x.dtype)
    out = jax.ops.segment_sum(ys, tok, num_segments=T)
    return out.reshape(B, S, D)

def second_inputs(seed: int = 0) -> dict:
    key = jax.random.key(seed)
    ks = jax.random.split(key, 20)
    f32 = jnp.float32
    nrm = lambda k, shape: jax.random.normal(k, shape, f32)
    base_logit = jnp.log(2.0 ** (5.0 + jnp.arange(RET_HEADS, dtype=f32)) - 1.0)
    return {
        "x": nrm(ks[0], (BATCH, SEQ, D_MODEL)),
        "w_in_even": nrm(ks[1], (N_EVEN, D_MODEL, IN_EVEN)) * D_MODEL ** -0.5,
        "ret_decay_logit": base_logit[None, None, :] + 0.1 * nrm(ks[2], (N_EVEN, 2, RET_HEADS)),
        "ret_gn_gain": 1.0 + 0.02 * nrm(ks[3], (N_EVEN, RET_WIDTH)),
        "sink_logit": 0.5 * nrm(ks[4], (N_EVEN, WIN_Q_HEADS)),
        "w_out_even": nrm(ks[5], (N_EVEN, D_MODEL, D_MODEL)) * D_MODEL ** -0.5 * DEEPNORM_BETA,
        "w_out_fourier": nrm(ks[6], (N_ODD, D_MODEL, D_MODEL)) * D_MODEL ** -0.5 * DEEPNORM_BETA,
        "ln1_gain": 1.0 + 0.02 * nrm(ks[7], (DEPTH, D_MODEL)),
        "ln1_bias": 0.02 * nrm(ks[8], (DEPTH, D_MODEL)),
        "ln2_gain": 1.0 + 0.02 * nrm(ks[9], (DEPTH, D_MODEL)),
        "ln2_bias": 0.02 * nrm(ks[10], (DEPTH, D_MODEL)),
        "router_coarse_w": nrm(ks[11], (DEPTH, D_MODEL, N_GROUPS)) * D_MODEL ** -0.5,
        "router_coarse_b": 0.01 * nrm(ks[12], (DEPTH, N_GROUPS)),
        "router_fine_w": nrm(ks[13], (DEPTH, D_MODEL, N_EXPERTS)) * D_MODEL ** -0.5,
        "router_fine_b": 0.01 * nrm(ks[14], (DEPTH, N_EXPERTS)),
        "expert_w_gate": nrm(ks[15], (DEPTH, N_EXPERTS, D_MODEL, EXPERT_HIDDEN)) * D_MODEL ** -0.5,
        "expert_w_up": nrm(ks[16], (DEPTH, N_EXPERTS, D_MODEL, EXPERT_HIDDEN)) * D_MODEL ** -0.5,
        "expert_w_down": nrm(ks[17], (DEPTH, N_EXPERTS, EXPERT_HIDDEN, D_MODEL)) * EXPERT_HIDDEN ** -0.5 * DEEPNORM_BETA,
    }

def second_block(x, w_in_even, ret_decay_logit, ret_gn_gain, sink_logit, w_out_even, w_out_fourier,
              ln1_gain, ln1_bias, ln2_gain, ln2_bias, router_coarse_w, router_coarse_b,
              router_fine_w, router_fine_b, expert_w_gate, expert_w_up, expert_w_down):
    pos = jnp.arange(x.shape[1], dtype=jnp.int32)
    for layer in range(DEPTH):
        if layer % 2 == 0:
            e = layer // 2
            mix = even_mixer(x, w_in_even[e], ret_decay_logit[e], ret_gn_gain[e], sink_logit[e],
                             w_out_even[e], pos)
        else:
            mix = fourier_mixer(x, w_out_fourier[layer // 2])
        x = layer_norm_2(DEEPNORM_ALPHA * x + mix, ln1_gain[layer], ln1_bias[layer])
        ffn = hierarchical_moe(x, router_coarse_w[layer], router_coarse_b[layer], router_fine_w[layer],
                               router_fine_b[layer], expert_w_gate[layer], expert_w_up[layer],
                               expert_w_down[layer])
        x = layer_norm_2(DEEPNORM_ALPHA * x + ffn, ln2_gain[layer], ln2_bias[layer])
    return x


def setup_inputs(seed=0):
    out = dict(first_inputs(seed))
    for name, value in second_inputs(seed + 1).items():
        if name != "x":
            out[name + "_2"] = value
    return out


def reference(
    x, c, ctx, c_ctx, ab_w_in, ab_q_gain, ab_k_gain, ab_w_pool, ab_pool_scale, ab_w_out,
    cd_w_in, cd_lambda_q1, cd_lambda_k1, cd_lambda_q2, cd_lambda_k2, cd_subln_gain, cd_conv_w,
    cd_conv_b, cd_conv_ln_g, cd_conv_ln_b, cd_w_out, ada_w, ada_b, ln1_g, ln1_b, ln2_g, ln2_b,
    ffn_w_in, ffn_w_out, w_in_even_2, ret_decay_logit_2, ret_gn_gain_2, sink_logit_2,
    w_out_even_2, w_out_fourier_2, ln1_gain_2, ln1_bias_2, ln2_gain_2, ln2_bias_2,
    router_coarse_w_2, router_coarse_b_2, router_fine_w_2, router_fine_b_2, expert_w_gate_2,
    expert_w_up_2, expert_w_down_2,
):
    x = first_block(
        x, c, ctx, c_ctx, ab_w_in, ab_q_gain, ab_k_gain, ab_w_pool, ab_pool_scale, ab_w_out,
        cd_w_in, cd_lambda_q1, cd_lambda_k1, cd_lambda_q2, cd_lambda_k2, cd_subln_gain,
        cd_conv_w, cd_conv_b, cd_conv_ln_g, cd_conv_ln_b, cd_w_out, ada_w, ada_b, ln1_g, ln1_b,
        ln2_g, ln2_b, ffn_w_in, ffn_w_out,
    )
    return second_block(
        x, w_in_even_2, ret_decay_logit_2, ret_gn_gain_2, sink_logit_2, w_out_even_2,
        w_out_fourier_2, ln1_gain_2, ln1_bias_2, ln2_gain_2, ln2_bias_2, router_coarse_w_2,
        router_coarse_b_2, router_fine_w_2, router_fine_b_2, expert_w_gate_2, expert_w_up_2,
        expert_w_down_2,
    )


_drawn_inputs = setup_inputs


def setup_inputs(seed=0):
    import zlib

    import numpy as np

    out = dict(_drawn_inputs(seed))
    spreads = {}
    factors = {'ctx': 2.786,
     'ab_q_gain': 8.0,
     'ab_k_gain': 8.0,
     'ab_pool_scale': 7.62,
     'cd_lambda_q1': 3.876,
     'cd_lambda_k1': 8.0,
     'cd_lambda_q2': 8.0,
     'cd_lambda_k2': 8.0,
     'cd_subln_gain': 6.868,
     'cd_conv_b': 8.0,
     'cd_conv_ln_g': 8.0,
     'cd_conv_ln_b': 25.54,
     'ada_b': 3.278,
     'ret_gn_gain_2': 7.971,
     'sink_logit_2': 21.692,
     'router_coarse_b_2': 20.701,
     'router_fine_b_2': 7.745}
    for name, (base, spread) in spreads.items():
        noise = np.random.default_rng([zlib.crc32(name.encode()), seed]).standard_normal(out[name].shape)
        drawn = base * np.exp(spread * noise) if base else spread * noise
        out[name] = jnp.asarray(drawn.astype(out[name].dtype))
    for name, factor in factors.items():
        out[name] = (out[name] * factor).astype(out[name].dtype)
    return out
```

```python
import math
from contextlib import ExitStack

import numpy as np
import concourse.bass as bass
from concourse import mybir

F32, I32, U32 = mybir.dt.float32, mybir.dt.int32, mybir.dt.uint32
ACT, ALU, AX = mybir.ActivationFunctionType, mybir.AluOpType, mybir.AxisListType

P = 128
D = 1024
KD = D // P
SEQ, CTX = 512, 256
NT_C, NT_X = CTX // P, SEQ // P
NT = NT_C + NT_X
HD = 64
GRID_W = 64
FFN = 2816
KF = FFN // P
EPS, LN_EPS2, GN_EPS = 1e-6, 1e-5, 1e-6
ALPHA = (2.0 * 2) ** 0.25
LAM_INIT = 0.8 - 0.6 * math.exp(-0.3)
NE = 32
BIG_IDX = 4096.0
NEG = -1e30
DVE_PER_PASS = 8


def constants():
    f = np.float32
    c = {}
    c["ident"] = np.eye(P, dtype=f)
    t = np.arange(SEQ)
    row, col = (t // GRID_W).astype(f), (t % GRID_W).astype(f)
    fr = (10000.0 ** (-np.arange(0, 32, 2, dtype=f) / 32)).astype(f)
    cs, sn = [], []
    for pos in (row, col):
        a = (pos[:, None] * fr[None]).astype(f).astype(np.float64)
        cs += [np.cos(a), np.cos(a)]
        sn += [-np.sin(a), np.sin(a)]
    c["rope_ax"] = np.concatenate([np.concatenate(cs, 1), np.concatenate(sn, 1)], 1).astype(f)
    for name, half in (("rope_ret", 64), ("rope_win", 32)):
        inv = (10000.0 ** (-np.arange(half, dtype=f) / half)).astype(f)
        a = (t.astype(f)[:, None] * inv[None]).astype(f).astype(np.float64)
        c[name] = np.concatenate([np.cos(a), np.cos(a), -np.sin(a), np.sin(a)], 1).astype(f)

    def pool(n):
        out = np.zeros((4, n, n), np.float64)
        for g, w in enumerate((2, 4, 8, 16)):
            for i in range(n):
                lo, hi = max(i - w // 2, 0), min(i + (w - 1 - w // 2) + 1, n)
                out[g, lo:hi, i] += 1.0 / (hi - lo)
                out[g, i, i] -= 1.0
        return out

    c["pool_x"] = np.ascontiguousarray(pool(SEQ).reshape(4, NT_X, P, SEQ).transpose(2, 0, 1, 3)).astype(f)
    c["pool_c"] = np.ascontiguousarray(pool(CTX).reshape(4, NT_C, P, CTX).transpose(2, 0, 1, 3)).astype(f)
    j, p = np.arange(896)[None] - 384, np.arange(P)[:, None]
    c["dist"] = np.stack([np.maximum(j - p, 0), np.maximum(p - j, 0)], 1).astype(f)
    i, k = np.arange(P)[:, None], np.arange(P)[None]
    c["band"] = np.stack([np.where(i <= k, 0, NEG), np.zeros((P, P)), np.where(k <= i, 0, NEG)], 1).astype(f)
    kk = np.outer(np.arange(256), np.arange(256)) % 256 * (2 * np.pi / 256)
    c["dft_c"] = np.ascontiguousarray(
        np.concatenate([np.cos(kk), np.sin(kk)], 1).reshape(2, P, 512).transpose(1, 0, 2)).astype(f)
    kk = np.outer(np.arange(SEQ), np.arange(SEQ)) % SEQ * (2 * np.pi / SEQ)
    s = 1.0 / math.sqrt(SEQ * 256)
    c["dft_s"] = np.ascontiguousarray(
        np.stack([np.cos(kk) * s, -np.sin(kk) * s]).reshape(2, NT_X, P, SEQ).transpose(2, 0, 1, 3)).astype(f)
    c["before"] = np.concatenate([np.triu(np.ones((P, P)), 1), np.ones((P, P))], 1).astype(f)
    c["iota"] = np.tile(np.arange(P, dtype=f), (P, 1))
    c["tok"] = (np.arange(NT_X)[None] * P + np.arange(P)[:, None]).astype(f)
    return c


def build(nc, A, stop):
    ctx = ExitStack()
    with ctx:
        KB = 256
        arena = ctx.enter_context(nc.sbuf_tensor("arena", [P, 206 * KB], F32))

        def region(kb, *shape, parts=P):
            n = int(np.prod(shape))
            at = int(round(kb * KB))
            assert at + n <= 206 * KB, (kb, shape)
            v = arena[0:parts, at:at + n]
            if len(shape) == 1:
                return v
            names = "abcde"[:len(shape)]
            return v.rearrange(f"p ({' '.join(names)}) -> p {' '.join(names)}",
                               **{n_: s for n_, s in zip(names[1:], shape[1:])})

        RING_KB = [0, 16, 32, 48, 64]
        MOE_RING_KB = RING_KB + [128]
        X = region(80, NT, D)
        HT = region(104, KD, NT * P)
        BIG, MISC = 128, 200

        ident = ctx.enter_context(nc.sbuf_tensor("ident", [P, P], F32))[:, :]
        mod_cols = region(MISC, 48, 2)
        stat = region(MISC + 0.5, NT, 2, 6)
        mv = region(MISC + 1, NT, 2)
        rstd = region(MISC + 1.25, NT, 16)
        nmx = region(MISC + 3.5, 8)
        esum = region(MISC + 3.75, 8)
        rsum = region(MISC + 4, 8)
        lam = region(MISC + 4.25, 8)
        psum = ctx.enter_context(nc.psum_tensor("psum", [P, 8, 512], F32))

        sems = {}

        def sem(name):
            if name not in sems:
                sems[name] = ctx.enter_context(nc.semaphore(name))
            return sems[name]

        psum_full, psum_free = sem("psum_full"), sem("psum_free")
        w_used = sem("w_used")
        act_chain, dve_chain = sem("act_chain"), sem("dve_chain")
        stage_act, stage_dve = sem("stage_act"), sem("stage_dve")
        gate_done = sem("gate_done")
        stat_ready, sqrt_done = sem("stat_ready"), sem("sqrt_done")
        w_ready = [sem(f"w_ready{i}") for i in range(5)]

        mod_rows, ada_bias = region(BIG, 6 * D, parts=2), region(BIG + 24, 6 * D, parts=2)
        c_cols, c_silu = region(BIG + 48, 2, KD), region(BIG + 49, KD, 2)
        ab_qk, ab_vu = region(BIG, NT, 1024), region(BIG + 24, NT, 512)
        ab_qT, ab_kT = region(BIG + 36, 6, NT * P), region(BIG + 54, 4, NT * P)
        ab_kd = region(104, NT, 512)
        tmp_a, tmp_b = region(116, 1024), region(120, 1024)
        qk_gain = region(124, 2, HD)
        rope_ax = region(125, NT_X, 128)
        att_P, att_PT = region(BIG, 2, 768), region(BIG + 6, 2, 768)
        pooledT, w_pool = region(BIG + 12, 4, 512, parts=64), region(BIG + 20, 4, 64, parts=64)
        pool_scale = region(BIG + 21, 256)
        O_all = region(104, NT, D)
        cd_conv = region(BIG, NT_X, 256)
        cd_qT, cd_kT, cd_v = region(BIG + 4, 6, SEQ), region(BIG + 16, 6, NT * P), region(BIG + 34, NT, 768)
        cd_tmp = region(BIG + 52, NT, 768)
        cd_z, cd_acc, cd_sg = region(BIG + 52, 2, 544), region(BIG + 57, 2, SEQ), region(BIG + 61, 2, SEQ)
        cd_wrow, cd_wcol = region(BIG + 65, 256, parts=32), region(BIG + 66, 2, 32)
        cd_lng, cd_lnb = region(BIG + 67, 256), region(BIG + 68, 256)
        cd_ta, cd_tb = region(BIG + 34, 768), region(BIG + 37, 768)
        cd_rope = region(BIG + 40, NT_X, 128)
        cd_P, cd_A, cd_PT = region(BIG + 52, 4, 768), region(BIG + 64, 2, 768), region(120, 2, 768)
        cd_sq = region(BIG + 52, 768)
        O4 = region(104, NT_X, D)
        lam_in, sub_gain = region(BIG + 70, 4, HD), region(BIG + 71, 128)
        ev_qa, ev_ka, ev_va, ev_ga, ev_qb = (region(BIG + 8 * i, NT_X, 512) for i in range(5))
        ev_kv = region(BIG + 40, NT_X, 256)
        ev_qaT, ev_kaT = region(BIG + 44, 4, SEQ), region(BIG + 52, 4, SEQ)
        ev_qbT, ev_kbT = region(BIG + 60, 4, SEQ), region(BIG + 68, 2, SEQ)
        rope_ret, rope_win = region(104, NT_X, 256), region(108, NT_X, 128)
        ev_ta, ev_tb, ev_kbd = region(110, 512), region(112, 512), region(114, NT_X, 256)
        ev_D, ev_ST = region(BIG, 4, SEQ), region(BIG + 8, 4, SEQ)
        dist = region(BIG + 32, 2, 896)
        gn_row = region(120, 512)
        decay = region(122, 2, 4)
        lg = region(122.25, 8, 2, 4)
        sinks = region(122.75, 8)
        ev_Sm, ev_P, ev_PT = region(BIG, 2, 388), region(BIG + 4, 2, 384), region(BIG + 8, 2, 384)
        band = region(BIG + 12, 3, P)
        fo_AB, fo_YT = region(BIG, NT_X, 4, 512), region(BIG + 32, KD, SEQ)
        ffn_hT, ffn_sg = region(BIG, KF, SEQ), region(BIG + 44, 2, SEQ)
        OT_ab, OT_cd, OT_ev = region(BIG + 36, KD, NT * P), region(BIG + 4, KD, SEQ), region(BIG + 44, KD, SEQ)

        class Rows:

            def __init__(self, kb, gates):
                self.gate = [region(kb + 4 * i, D) for i in range(gates)]
                kb += 4 * gates
                self.g, self.b, self.tmp = region(kb, D), region(kb + 4, D), region(kb + 8, 2, 512)

        rows_ab, rows_cd, rows_ev, rows_fo = Rows(BIG, 2), Rows(BIG + 24, 1), Rows(BIG, 0), Rows(BIG + 48, 0)
        rows_ffn = Rows(BIG + 48, 1)
        mo_xg, mo_xgT = region(144, 2, D), region(152, KD, P)
        mo_sg, mo_h, mo_hT, mo_y = region(156, 512), region(158, 512), region(160, 4, P), region(162, 2, D)
        mo_sel, mo_F = region(170, 8, P), region(174, NT_X, NE, 4)
        mo_RK, mo_cnt = region(176, NT_X, NE), region(176.5, 8)
        mo_idxf, mo_gate = region(176.75, 2, NE + 1), region(177.25, NE)
        mo_idx = region(177.5, 2, NE + 1).bitcast(I32)
        mo_np, mo_npi = region(178, 8), region(178.125, 8).bitcast(I32)
        mo_L, mo_C8 = region(178.25, NT_X, 36), region(179, NT_X, 8)
        mo_m8, mo_ix, mo_ixf = region(179.25, NT_X, 8), region(179.5, NT_X, 8).bitcast(U32), region(179.75, NT_X, 8)
        mo_G, mo_FS, mo_t8 = region(180, NT_X, 4), region(180.25, NT_X, 8), region(180.5, NT_X, 8)
        mo_A1, mo_A2, mo_A = region(180.75, NT_X, NE), region(181.25, NT_X, NE), region(181.75, NT_X, NE)
        mo_s = region(182.25, 16, NT_X)
        mo_wr, mo_bias = region(183, KD, 36), region(184.25, 36)
        mo_before, mo_iota, mo_tok = region(184.5, 2, P), region(185.5, P), region(186, NT_X)
        mo_meta = region(186.25, NE, 4)
        mo_y12 = region(144, 2, NT_X, D)
        rows_moe = Rows(187, 0)

        def ffn_stages(f):
            return [f"{f}_ht", f"{f}_in", f"{f}_out", f"{f}_norm"]

        def moe_stages(m):
            return [f"r{m}_ht", f"r{m}_route", f"r{m}_experts", f"r{m}_norm"]

        STAGES = (["mod0", "modT0", "ab_ht", "ab_in", "ab_rope", "ab_tr", "ab_att", "ab_pool", "ab_ot", "ab_out",
                   "ab_norm"] + ffn_stages("f0x") + ffn_stages("f0c")
                  + ["mod1", "modT1", "cd_ht", "cd_u", "cd_conv", "cd_q", "cd_qrope", "cd_qt", "cd_k", "cd_krope",
                     "cd_kt", "cd_v", "cd_att", "cd_sub", "cd_ot", "cd_out", "cd_norm"] + ffn_stages("f1x")
                  + ["ev_ht", "ev_in", "ev_rope", "ev_tr", "ev_ret", "ev_win", "ev_ot", "ev_out", "ev_norm"]
                  + moe_stages(0) + ["fo_ht", "fo_dft", "fo_seq", "fo_out", "fo_norm"] + moe_stages(1))
        if stop:
            STAGES = STAGES[:STAGES.index(stop) + 1]

        TILES_X, TILES_C = list(range(NT_C, NT)), list(range(NT_C))
        ALL = TILES_C + TILES_X

        def row(v):
            return v.partition_broadcast(P)

        def norm_rows(rows, l, n, gates=()):
            out = [(rows.gate[i], row(A["mod"][l, who, at * D:at * D + D])) for i, (who, at) in enumerate(gates)]
            sfx = "" if n[:2] == "ln" else ""
            g, b = (f"{n}_g", f"{n}_b") if not n.endswith("_2") else (n.replace("_2", "_gain_2"), n.replace("_2", "_bias_2"))
            return out + [(rows.g, row(A[g][l])), (rows.b, row(A[b][l]))]

        def mod_loads(l):
            return [(c_cols[:, 0], A["c"][0].rearrange("(k p) -> p k", p=P)),
                    (c_cols[:, 1], A["c_ctx"].rearrange("(k p) -> p k", p=P)),
                    (ada_bias, A["ada_b"][l].partition_broadcast(2))]

        def route_loads(m):
            return [(mo_wr[:, :, 0:4], A["router_coarse_w_2"][m].rearrange("(k p) n -> p k n", p=P)),
                    (mo_wr[:, :, 4:36], A["router_fine_w_2"][m].rearrange("(k p) n -> p k n", p=P)),
                    (mo_bias[:, 0:4], row(A["router_coarse_b_2"][m])), (mo_bias[:, 4:36], row(A["router_fine_b_2"][m])),
                    (mo_before, A["before"].rearrange("p (a n) -> p a n", a=2)), (mo_iota, A["iota"]),
                    (mo_tok, A["tok"])]

        LOADS = {
            "mod0": mod_loads(0), "mod1": mod_loads(1),
            "ab_rope": [(qk_gain[:, 0], row(A["ab_q_gain"][0])), (qk_gain[:, 1], row(A["ab_k_gain"][0])),
                        (rope_ax, A["rope_ax"].rearrange("(t p) n -> p t n", p=P))],
            "ab_pool": [(w_pool, A["ab_w_pool"][0].rearrange("g c d -> c g d")),
                        (pool_scale, row(A["ab_pool_scale"][0]))],
            "ab_out": norm_rows(rows_ab, 0, "ln1", [(0, 2), (1, 2)]),
            "f0x_out": norm_rows(rows_ffn, 0, "ln2", [(0, 5)]),
            "f0c_out": norm_rows(rows_ffn, 0, "ln2", [(1, 5)]),
            "cd_u": [(cd_wrow[0:31], A["cd_conv_w"][0]), (cd_wrow[31:32], A["cd_conv_b"]),
                     (cd_lng, row(A["cd_conv_ln_g"][0])), (cd_lnb, row(A["cd_conv_ln_b"][0]))],
            "cd_q": [(cd_rope, A["rope_ax"].rearrange("(t p) n -> p t n", p=P))],
            "cd_v": [(lam_in[:, i], row(A[n][0])) for i, n in
                     enumerate(("cd_lambda_q1", "cd_lambda_k1", "cd_lambda_q2", "cd_lambda_k2"))]
            + [(sub_gain, row(A["cd_subln_gain"][0]))],
            "cd_out": norm_rows(rows_cd, 1, "ln1", [(0, 2)]),
            "f1x_out": norm_rows(rows_ffn, 1, "ln2", [(0, 5)]),
            "ev_rope": [(rope_ret, A["rope_ret"].rearrange("(t p) n -> p t n", p=P)),
                        (rope_win, A["rope_win"].rearrange("(t p) n -> p t n", p=P))],
            "ev_ret": [(dist, A["dist"]), (gn_row, row(A["ret_gn_gain_2"][0])),
                       (decay[:, 0], row(A["ret_decay_logit_2"][0, 0])), (decay[:, 1], row(A["ret_decay_logit_2"][0, 1])),
                       (sinks, row(A["sink_logit_2"][0]))],
            "ev_win": [(band, A["band"])],
            "ev_out": norm_rows(rows_ev, 0, "ln1_2"),
            "fo_out": norm_rows(rows_fo, 1, "ln1_2"),
        }
        for m in range(2):
            LOADS[f"r{m}_ht"] = route_loads(m)
            LOADS[f"r{m}_norm"] = norm_rows(rows_moe, m, "ln2_2") + [
                (mo_y12[:, j, t], A[f"y{m}"][j * SEQ + t * P:j * SEQ + t * P + P]) for j in range(2) for t in range(NT_X)]

        def wait_loads(eng, stage):
            eng.wait_ge(sem("loads_" + stage), 16 * len(LOADS[stage]))

        chunks, by_name = [], {}

        def add_chunk(name, parts, k, n):
            i = len(chunks)
            chunks.append(dict(parts=parts, k=k, n=n, slot=i % 5, use=i // 5 + 1, name=name))
            by_name.setdefault(name, []).append(i)

        def kpn(w, c0, c1, k0, k):
            return w[k0 * P:(k0 + k) * P, c0:c1].rearrange("(k p) n -> p k n", p=P)

        def weight_chunks(name, w, bounds, kblocks=KD):
            for c0, c1 in bounds:
                for k0 in range(0, kblocks, 8):
                    k = min(8, kblocks - k0)
                    add_chunk(name, [(0, kpn(w, c0, c1, k0, k))], k, c1 - c0)

        def ffn_chunks(f, l):
            w = A["ffn_w_in"][l]
            for j in range(0, FFN, 256):
                add_chunk(f"{f}_in", [(0, kpn(w, j, j + 256, 0, KD)), (256, kpn(w, FFN + j, FFN + j + 256, 0, KD))],
                          KD, 512)
            weight_chunks(f"{f}_out", A["ffn_w_out"][l], HALVES, KF)

        HALVES = [(0, 512), (512, 1024)]
        weight_chunks("mod0", A["ada_w"][0], [(i * 512, i * 512 + 512) for i in range(12)])
        weight_chunks("ab_in", A["ab_w_in"][0], [(0, 512), (512, 1024), (1024, 1536)])
        for i in range(2):
            add_chunk("ab_pool", [(0, A["pool_x"][:, 2 * i:2 * i + 2].rearrange("p g t n -> p (g t) n"))], 8, 512)
        add_chunk("ab_pool", [(0, A["pool_c"].rearrange("p g t n -> p (g t) n"))], 8, 256)
        weight_chunks("ab_out", A["ab_w_out"][0], HALVES)
        ffn_chunks("f0x", 0)
        ffn_chunks("f0c", 0)
        weight_chunks("mod1", A["ada_w"][1], [(i * 512, i * 512 + 512) for i in range(12)])
        cw = A["cd_w_in"][0]
        weight_chunks("cd_u", cw, [(2304, 2816)])
        weight_chunks("cd_q", cw, [(0, 512), (512, 768)])
        weight_chunks("cd_k", cw, [(768, 1280), (1280, 1536)])
        weight_chunks("cd_v", cw, [(1536, 2048), (2048, 2304)])
        weight_chunks("cd_out", A["cd_w_out"][0], HALVES)
        ffn_chunks("f1x", 1)
        weight_chunks("ev_in", A["w_in_even_2"][0], [(i * 512, min(i * 512 + 512, 2816)) for i in range(6)])
        weight_chunks("ev_out", A["w_out_even_2"][0], HALVES)
        before_experts0 = len(chunks)
        add_chunk("fo_dft", [(0, A["dft_c"])], 2, 512)
        add_chunk("fo_seq", [(0, A["dft_s"].rearrange("p s t n -> p (s t) n"))], 8, 512)
        weight_chunks("fo_out", A["w_out_fourier_2"][0], HALVES)
        chunk_read = {}
        groups = {}

        def slot(i):
            ch = chunks[i]
            return region(RING_KB[ch["slot"]], ch["k"], ch["n"])

        class Link:

            def __init__(self, eng, chain):
                self.eng, self.chain, self.n, self.at = eng, chain, {}, {}

            def __call__(self, ins, s=None, upto=None):
                s = self.chain if s is None else s
                self.n[s.name] = self.n.get(s.name, 0) + 1
                ins.then_inc(s, 1)
                self.eng.wait_ge(s, upto if upto is not None else self.at.get(s.name, 0) + self.n[s.name])

        def run(eng, steps, me=None):
            for n, name in enumerate(STAGES):
                if name in ("ab_ht", "cd_ht"):
                    eng.wait_ge(sem("mod_stored"), 16 if name == "ab_ht" else 32)
                if name in ("r0_norm", "r1_norm"):
                    eng.wait_ge(M(int(name[1]), "x_stored"), 16 * NT_X)
                if name in steps:
                    steps[name]()
                if me is not None:
                    eng.sem_inc(me, 1)
                eng.wait_ge(stage_act, n + 1)
                eng.wait_ge(stage_dve, n + 1)

        def tiles(t, n=1):
            return slice(t * P, (t + n) * P)

        def flat(bank, n):
            return psum[:, bank:bank + -(-n // 512), :].rearrange("p b n -> p (b n)")[:, 0:n]

        AB_UNITS = [(h, t) for h in range(12) for t in TILES_X] + [(h, t) for h in range(12) for t in TILES_C]
        CD_UNITS = [(h, t) for h in range(6) for t in range(NT_X)]
        WIN_UNITS = [(h, t) for h in range(8) for t in range(NT_X)]

        def win_keys(t):
            return [k for k in (t - 1, t, t + 1) if 0 <= k < NT_X]

        def ab_keys(t):
            return NT if t >= NT_C else NT_C

        A_, C_ = {}, {}
        for nm in ("score_full", "max_done", "exp_done", "pt_full", "pt_copied", "o_full", "o_done", "diff_done"):
            A_[nm], C_[nm] = sem("ab_" + nm), sem("cd_" + nm)

        ret_mv = region(MISC + 4.5, NT_X, 4, 2)

        def M(m, name):
            return sem(f"moe{m}_{name}")

        def more_passes(eng, m, one_pass):
            eng.wait_ge(stage_dve, STAGES.index(f"r{m}_experts"))
            n = eng.value_load(mo_npi[0:1, 0:1], min_val=1, max_val=NT_X)
            with eng.If(n > 1):
                with eng.Fori(1, n) as p:
                    one_pass(p)

        block = ctx.enter_context(nc.Block())

        @block.tensor
        def _(pe):
            state = dict(g=0, bank=0, mid=0)
            last_group = [-1] * 8

            def open_group(name, nb=1):
                if state["bank"] + nb > 8:
                    state["bank"] = 0
                b = state["bank"]
                state["bank"] = (b + nb) % 8
                before = max(last_group[b:b + nb])
                if before >= 0:
                    pe.wait_ge(psum_free, before + 1)
                for i in range(b, b + nb):
                    last_group[i] = state["g"]
                groups[name] = (state["g"], b)
                state["g"] += 1
                return b

            def close(ins):
                ins.then_inc(psum_full, 1)
                return ins

            def await_chunk(i):
                pe.wait_ge(w_ready[chunks[i]["slot"]], 16 * sum(
                    len(c["parts"]) for c in chunks[:i + 1] if c["slot"] == chunks[i]["slot"]))

            def read_group(name):
                pe.wait_ge(psum_free, groups[name][0] + 1)

            def products(name, tl, lhs):
                for c, i in enumerate(by_name[name]):
                    await_chunk(i)
                    w, k, n = slot(i), chunks[i]["k"], chunks[i]["n"]
                    for t in tl:
                        b = open_group((name, c, t))
                        for kk in range(k):
                            ins = nc.tensor.matmul(psum[:, b, 0:n], lhs(t, kk), w[:, kk, :],
                                                   start=kk == 0, stop=kk == k - 1)
                        close(ins)
                    chunk_read[i] = (psum_full, state["g"])

            def transposes(name, tl, src, n, per=8):
                for t in tl:
                    b = open_group((name, t), -(-n // 4))
                    for k in range(n):
                        ins = nc.tensor.transpose(flat(b, n * P)[:, tiles(k)], src(t, k), ident)
                    close(ins)

            def mod(l):
                def go():
                    pe.wait_ge(gate_ready := sem("c_ready"), l + 1)
                    for c, i in enumerate(by_name[f"mod{l}"]):
                        await_chunk(i)
                        b = open_group(("mod", l, c))
                        for k in range(KD):
                            ins = nc.tensor.matmul(psum[0:2, b, :], c_silu[:, k], slot(i)[:, k],
                                                   start=k == 0, stop=k == KD - 1)
                        close(ins)
                        chunk_read[i] = (psum_full, state["g"])
                return go

            def mod_t(l):
                def go():
                    b = open_group(("modT", l))
                    for j in range(48):
                        ins = nc.tensor.transpose(psum[:, b, 2 * j:2 * j + 2], mod_rows[:, tiles(j)], ident[0:2, 0:2])
                    close(ins)
                return go

            def gated(name, w_cols, ntok, col0):
                for c, i in enumerate(by_name[name]):
                    await_chunk(i)
                    w = slot(i)
                    for j in range(2):
                        b = open_group((name, 2 * c + j), 2)
                        for part in range(2):
                            for k in range(KD):
                                ins = nc.tensor.matmul(psum[:, b + part, 0:ntok],
                                                       w[:, k, part * 256 + j * P:part * 256 + j * P + P],
                                                       HT[:, k, col0:col0 + ntok], start=k == 0, stop=k == KD - 1)
                        close(ins)
                    chunk_read[i] = (psum_full, state["g"])

            def summed(name, tl):
                ids = by_name[name]
                per = len(ids) // 2
                for half in range(2):
                    banks = {t: open_group((name, half, t)) for t in tl}
                    k0 = 0
                    for j in range(per):
                        i = ids[half * per + j]
                        await_chunk(i)
                        w, k = slot(i), chunks[i]["k"]
                        for t in tl:
                            for kk in range(k):
                                ins = nc.tensor.matmul(psum[:, banks[t], :], ffn_hT[:, k0 + kk, tiles(t - tl[0])],
                                                       w[:, kk, :], start=k0 + kk == 0, stop=k0 + kk == KF - 1)
                            if j == per - 1:
                                close(ins)
                        if j == per - 1:
                            chunk_read[i] = (psum_full, state["g"])
                        else:
                            ins.then_inc(w_used, 1)
                            state["mid"] += 1
                            chunk_read[i] = (w_used, state["mid"])
                        k0 += k

            def ffn(f, tl):
                return {
                    f"{f}_ht": lambda: transposes(f"{f}_ht", tl, lambda t, k: X[:, t, tiles(k)], KD),
                    f"{f}_in": lambda: gated(f"{f}_in", None, len(tl) * P, tl[0] * P),
                    f"{f}_out": lambda: summed(f"{f}_out", tl),
                }

            def ab_tr():
                transposes("ab_q", ALL, lambda t, k: ab_qk[:, t, tiles(k)], 6)
                transposes("ab_k", ALL, lambda t, k: ab_kd[:, t, tiles(k)], 4)

            def ab_att():
                s, n = A_, len(AB_UNITS)

                def scores(u):
                    if u >= n:
                        return
                    h, t = AB_UNITS[u]
                    lo, kv, nk = 64 * (h % 2), h // 3, ab_keys(t) * P
                    if u >= 2:
                        pe.wait_ge(s["exp_done"], u - 1)
                    for c0 in range(0, nk, 512):
                        c1 = min(c0 + 512, nk)
                        ins = nc.tensor.matmul(flat(2 * (u % 2), nk)[:, c0:c1], ab_qT[lo:lo + 64, h // 2, tiles(t)],
                                               ab_kT[lo:lo + 64, kv, c0:c1], start=True, stop=True)
                    ins.then_inc(s["score_full"], 1)

                scores(0)
                scores(1)
                for u, (h, t) in enumerate(AB_UNITS):
                    nk = ab_keys(t)
                    pe.wait_ge(s["exp_done"], u + 1)
                    if u >= 1:
                        pe.wait_ge(s["pt_copied"], u)
                    for k in range(nk):
                        ins = nc.tensor.transpose(flat(4, 768)[:, tiles(k)], att_P[:, u % 2, tiles(k)], ident)
                    ins.then_inc(s["pt_full"], 1)
                    scores(u + 2)
                    pe.wait_ge(s["pt_copied"], u + 1)
                    if u >= 2:
                        pe.wait_ge(s["o_done"], u - 1)
                    for k in range(nk):
                        ins = nc.tensor.matmul(psum[:, 6 + u % 2, 0:HD], att_PT[:, u % 2, tiles(k)],
                                               ab_vu[:, k, HD * (h // 3):HD * (h // 3) + HD],
                                               start=k == 0, stop=k == nk - 1)
                    ins.then_inc(s["o_full"], 1)

            def ab_pool():
                wait_loads(pe, "ab_pool")
                ids = by_name["ab_pool"]
                for who, tl, cs in (("x", TILES_X, ids[:2]), ("c", TILES_C, ids[2:])):
                    nt = len(tl)
                    for g in range(4):
                        i = cs[g * len(cs) // 4]
                        if g % (4 // len(cs)) == 0:
                            await_chunk(i)
                        b = open_group(("pooled", who, g))
                        for kt in range(nt):
                            ins = nc.tensor.matmul(psum[0:64, b, 0:nt * P],
                                                   ab_vu[:, tl[0] + kt, 256 + g * 64:320 + g * 64],
                                                   slot(i)[:, (g % (4 // len(cs))) * nt + kt, :],
                                                   start=kt == 0, stop=kt == nt - 1)
                        close(ins)
                        chunk_read[i] = (psum_full, state["g"])
                    for g in range(4):
                        read_group(("pooled", who, g))
                    for t in tl:
                        b = open_group(("mixed", t))
                        for g in range(4):
                            ins = nc.tensor.matmul(psum[:, b, g * 64:g * 64 + 64], pooledT[:, g, tiles(t - tl[0])],
                                                   w_pool[:, g], start=True, stop=True)
                        close(ins)

            def cd_u():
                wait_loads(pe, "cd_u")
                b = open_group("conv_w")
                for j in range(2):
                    ins = nc.tensor.transpose(psum[:, b, 32 * j:32 * j + 32], cd_wrow[:, tiles(j)], ident[0:32, 0:32])
                close(ins)
                gated("cd_u", None, SEQ, NT_C * P)

            def cd_conv_t():
                pe.wait_ge(sem("conv_done"), 1)
                for t in range(NT_X):
                    b = open_group(("conv", t))
                    for j in range(2):
                        ins = nc.tensor.transpose(psum[:, b, tiles(j)], cd_acc[:, j, tiles(t)], ident)
                    close(ins)

            def cd_att():
                s, n = C_, 2 * len(CD_UNITS)
                NK = NT * P

                def scores(v):
                    if v >= n:
                        return
                    h, t = CD_UNITS[v // 2]
                    lo = 64 * (v % 2)
                    if v >= 2:
                        pe.wait_ge(s["exp_done"], v - 1)
                    for c0 in range(0, NK, 512):
                        c1 = min(c0 + 512, NK)
                        ins = nc.tensor.matmul(flat(2 * (v % 2), NK)[:, c0:c1], cd_qT[lo:lo + 64, h, tiles(t)],
                                               cd_kT[lo:lo + 64, h, c0:c1], start=True, stop=True)
                    ins.then_inc(s["score_full"], 1)

                scores(0)
                scores(1)
                for u, (h, t) in enumerate(CD_UNITS):
                    pe.wait_ge(s["diff_done"], u + 1)
                    if u >= 1:
                        pe.wait_ge(s["pt_copied"], u)
                    for k in range(NT):
                        ins = nc.tensor.transpose(flat(4, 768)[:, tiles(k)], cd_A[:, u % 2, tiles(k)], ident)
                    ins.then_inc(s["pt_full"], 1)
                    scores(2 * u + 2)
                    pe.wait_ge(s["pt_copied"], u + 1)
                    if u >= 2:
                        pe.wait_ge(s["o_done"], u - 1)
                    for k in range(NT):
                        ins = nc.tensor.matmul(psum[:, 6 + u % 2, 0:P], cd_PT[:, u % 2, tiles(k)],
                                               cd_v[:, k, tiles(h)], start=k == 0, stop=k == NT - 1)
                    ins.then_inc(s["o_full"], 1)
                    scores(2 * u + 3)

            def ev_tr():
                R = range(NT_X)
                transposes("ev_qa", R, lambda t, k: ev_qa[:, t, tiles(k)], 4)
                transposes("ev_ka", R, lambda t, k: ev_ka[:, t, tiles(k)], 4)
                transposes("ev_qb", R, lambda t, k: ev_qb[:, t, tiles(k)], 4)
                transposes("ev_kb", R, lambda t, k: ev_kbd[:, t, tiles(k)], 2)

            def ev_ret():
                for h in range(4):
                    for mt in range(NT_X):
                        b = open_group(("ret_s", h, mt))
                        close(nc.tensor.matmul(psum[:, b, :], ev_kaT[:, h, tiles(mt)], ev_qaT[:, h, :],
                                               start=True, stop=True))
                    read_group(("ret_s", h, NT_X - 1))
                    for t in range(NT_X):
                        b = open_group(("ret_y", h, t))
                        for mt in range(NT_X):
                            ins = nc.tensor.matmul(psum[:, b, 0:P], ev_ST[:, mt, tiles(t)], ev_va[:, mt, tiles(h)],
                                                   start=mt == 0, stop=mt == NT_X - 1)
                        close(ins)

            def ev_win():
                def scores(u):
                    if u >= len(WIN_UNITS):
                        return
                    h, t = WIN_UNITS[u]
                    ks, lo = win_keys(t), 64 * (h % 2)
                    b = open_group(("win_s", u))
                    close(nc.tensor.matmul(psum[:, b, 0:len(ks) * P], ev_qbT[lo:lo + 64, h // 2, tiles(t)],
                                           ev_kbT[lo:lo + 64, h // 4, tiles(ks[0], len(ks))], start=True, stop=True))

                scores(0)
                for u, (h, t) in enumerate(WIN_UNITS):
                    ks = win_keys(t)
                    scores(u + 1)
                    pe.wait_ge(sem("win_exp_done"), u + 1)
                    b = open_group(("win_pt", u))
                    for k in range(len(ks)):
                        ins = nc.tensor.transpose(psum[:, b, tiles(k)], ev_P[:, u % 2, tiles(k)], ident)
                    close(ins)
                    read_group(("win_pt", u))
                    b = open_group(("win_o", u))
                    for k, kt in enumerate(ks):
                        ins = nc.tensor.matmul(psum[:, b, 0:HD], ev_PT[:, u % 2, tiles(k)],
                                               ev_kv[:, kt, P + HD * (h // 4):P + HD * (h // 4) + HD],
                                               start=k == 0, stop=k == len(ks) - 1)
                    close(ins)

            def fo_dft():
                i = by_name["fo_dft"][0]
                await_chunk(i)
                for t in range(NT_X):
                    for g in range(4):
                        b = open_group(("fo_dft", t, g))
                        for k in range(2):
                            ins = nc.tensor.matmul(psum[:, b, :], HT[:, 2 * g + k, tiles(NT_C + t)], slot(i)[:, k],
                                                   start=k == 0, stop=k == 1)
                        close(ins)
                chunk_read[i] = (psum_full, state["g"])

            def fo_seq():
                i = by_name["fo_seq"][0]
                await_chunk(i)
                for d in range(KD):
                    b = open_group(("fo_seq", d))
                    for part in range(2):
                        for t in range(NT_X):
                            ins = nc.tensor.matmul(
                                psum[:, b, :], fo_AB[:, t, d // 2, part * 256 + (d % 2) * P:part * 256 + (d % 2) * P + P],
                                slot(i)[:, part * NT_X + t], start=part + t == 0, stop=part + t == NT_X)
                    close(ins)
                chunk_read[i] = (psum_full, state["g"])

            def route(m):
                def go():
                    wait_loads(pe, f"r{m}_ht")
                    b = open_group(("logits", m))
                    for t in range(NT_X):
                        for k in range(KD):
                            ins = nc.tensor.matmul(psum[:, b, 36 * t:36 * t + 36], HT[:, k, tiles(NT_C + t)],
                                                   mo_wr[:, k], start=k == 0, stop=k == KD - 1)
                    close(ins)
                    pe.wait_ge(M(m, "picked"), 1)
                    b = open_group(("rank", m))
                    for t in range(NT_X):
                        for s in range(t + 1):
                            ins = nc.tensor.matmul(psum[:, b, NE * t:NE * t + NE], mo_before[:, int(s < t)],
                                                   mo_A[:, s], start=s == 0, stop=s == t)
                    for s in range(NT_X):
                        ins = nc.tensor.matmul(psum[:, b, NE * NT_X:NE * NT_X + NE], mo_before[:, 1], mo_A[:, s],
                                               start=s == 0, stop=s == NT_X - 1)
                    close(ins)
                return go

            def experts(m):
                def one_pass(p):
                    for e in range(NE):
                        pe.wait_ge(M(m, "sel_ready"), NE * p + e + 1)
                        for t in range(NT_X):
                            ins = nc.tensor.matmul(psum[:, 7, 4 * e:4 * e + 4], mo_sel[:, 4 * (e % 2) + t],
                                                   mo_F[:, t, e], start=t == 0, stop=t == NT_X - 1)
                        ins.then_inc(M(m, "sel_used"), 1)

                    def turn_x(xg_n, b):
                        pe.wait_ge(M(m, f"xg_ready{b}"), xg_n * 16)
                        for k in range(KD):
                            ins = nc.tensor.transpose(flat(2, D)[:, tiles(k)], mo_xg[:, b, tiles(k)], ident)
                        ins.then_inc(M(m, "xt_full"), 1)

                    turn_x(17 * p + 1, 0)
                    with pe.Fori(0, NE // 2) as i:
                        for b in range(2):
                            e = NE * p + i * 2 + b
                            pe.wait_ge(M(m, "xgT_ready"), (NE + 1) * p + i * 2 + b + 1)
                            pe.wait_ge(M(m, "gu_free"), e + 1)
                            for part in range(2):
                                w = region(MOE_RING_KB[3 * b + part], KD, 512)
                                pe.wait_ge(M(m, f"w_ready{3 * b + part}"), ((NE // 2) * p + i + 1) * 16)
                                for k in range(KD):
                                    ins = nc.tensor.matmul(psum[:, part, :], mo_xgT[:, k], w[:, k],
                                                           start=k == 0, stop=k == KD - 1)
                            ins.then_inc(M(m, "gu_full"), 1)
                            turn_x((17 * p + i + 2) if b == 1 else (16 * p + i + 1), 1 - b)
                            pe.wait_ge(M(m, "h_ready"), e + 1)
                            for k in range(4):
                                ins = nc.tensor.transpose(psum[:, 4, tiles(k)], mo_h[:, tiles(k)], ident)
                            ins.then_inc(M(m, "ht_full"), 1)
                            pe.wait_ge(M(m, "hT_ready"), e + 1)
                            pe.wait_ge(M(m, "y_free"), e + 1)
                            pe.wait_ge(M(m, f"w_ready{3 * b + 2}"), ((NE // 2) * p + i + 1) * 16)
                            w = region(MOE_RING_KB[3 * b + 2], 4, D)
                            for half in range(2):
                                for k in range(4):
                                    ins = nc.tensor.matmul(psum[:, 5 + half, :], mo_hT[:, k],
                                                           w[:, k, half * 512:half * 512 + 512],
                                                           start=k == 0, stop=k == 3)
                            ins.then_inc(M(m, "y_full"), 1)

                def go():
                    one_pass(0)
                    more_passes(pe, m, one_pass)
                return go

            steps = {
                "mod0": mod(0), "modT0": mod_t(0), "mod1": mod(1), "modT1": mod_t(1),
                "ab_ht": lambda: transposes("ab_ht", ALL, lambda t, k: X[:, t, tiles(k)], KD),
                "ab_in": lambda: products("ab_in", ALL, lambda t, k: HT[:, k, tiles(t)]),
                "ab_tr": ab_tr, "ab_att": ab_att, "ab_pool": ab_pool,
                "ab_ot": lambda: transposes("ab_ot", ALL, lambda t, k: O_all[:, t, tiles(k)], KD),
                "ab_out": lambda: products("ab_out", ALL, lambda t, k: OT_ab[:, k, tiles(t)]),
                **ffn("f0x", TILES_X), **ffn("f0c", TILES_C), **ffn("f1x", TILES_X),
                "cd_ht": lambda: transposes("cd_ht", ALL, lambda t, k: X[:, t, tiles(k)], KD),
                "cd_u": cd_u, "cd_conv": cd_conv_t,
                "cd_q": lambda: products("cd_q", TILES_X, lambda t, k: HT[:, k, tiles(t)]),
                "cd_k": lambda: products("cd_k", ALL, lambda t, k: HT[:, k, tiles(t)]),
                "cd_v": lambda: products("cd_v", ALL, lambda t, k: HT[:, k, tiles(t)]),
                "cd_qt": lambda: transposes("cd_qt", TILES_X, lambda t, k: cd_tmp[:, t, tiles(k)], 6),
                "cd_kt": lambda: transposes("cd_kt", ALL, lambda t, k: cd_tmp[:, t, tiles(k)], 6),
                "cd_att": cd_att,
                "cd_ot": lambda: transposes("cd_ot", TILES_X, lambda t, k: O4[:, t - NT_C, tiles(k)], KD),
                "cd_out": lambda: products("cd_out", TILES_X, lambda t, k: OT_cd[:, k, tiles(t - NT_C)]),
                "ev_ht": lambda: transposes("ev_ht", TILES_X, lambda t, k: X[:, t, tiles(k)], KD),
                "ev_in": lambda: products("ev_in", TILES_X, lambda t, k: HT[:, k, tiles(t)]),
                "ev_tr": ev_tr, "ev_ret": ev_ret, "ev_win": ev_win,
                "ev_ot": lambda: transposes("ev_ot", TILES_X, lambda t, k: O4[:, t - NT_C, tiles(k)], KD),
                "ev_out": lambda: products("ev_out", TILES_X, lambda t, k: OT_ev[:, k, tiles(t - NT_C)]),
                "fo_ht": lambda: transposes("fo_ht", TILES_X, lambda t, k: X[:, t, tiles(k)], KD),
                "fo_dft": fo_dft, "fo_seq": fo_seq,
                "fo_out": lambda: products("fo_out", TILES_X, lambda t, k: fo_YT[:, k, tiles(t - NT_C)]),
            }
            for m in range(2):
                steps[f"r{m}_ht"] = (lambda m: lambda: transposes(f"r{m}_ht", TILES_X,
                                                                  lambda t, k: X[:, t, tiles(k)], KD))(m)
                steps[f"r{m}_route"] = route(m)
                steps[f"r{m}_experts"] = experts(m)
            pe.wait_ge(sem("ident_loaded"), 16)
            pe.wait_ge(sem("x_loaded"), 16 * NT)
            run(pe, steps)

        @block.scalar
        def _(act):
            link = Link(act, act_chain)

            def await_group(name):
                act.wait_ge(psum_full, groups[name][0] + 1)
                return groups[name]

            def take(name, dst, n):
                g, b = await_group(name)
                src = flat(b, n)
                if len(dst.shape) == 3:
                    src = src.rearrange("p (a c) -> p a c", a=dst.shape[1])
                link(nc.scalar.activation(dst, src, ACT.Copy), psum_free, g + 1)

            def roots(n, times=1):
                def go():
                    for _ in range(times):
                        k = link.n.get("sqrt_done", 0)
                        act.wait_ge(stat_ready, k + 1)
                        v = n if not callable(n) else n()
                        link(nc.scalar.activation(v, v, ACT.Sqrt), sqrt_done)
                return go

            def mod(l):
                def go():
                    wait_loads(act, f"mod{l}")
                    for who in range(2):
                        link(nc.scalar.activation(c_silu[:, :, who], c_cols[:, who], ACT.Silu),
                             None if who == 0 else sem("c_ready"))
                return go

            def gate(name, func, sg, ntok, n):
                def go():
                    for j in range(n):
                        g, b = await_group((name, j))
                        if j >= 2:
                            act.wait_ge(psum_free, groups[(name, j - 2)][0] + 1)
                        link(nc.scalar.activation(sg[:, j % 2, 0:ntok], psum[:, b + 1, 0:ntok], func), gate_done)
                return go

            def ab_in():
                for c in range(3):
                    for t in ALL:
                        take(("ab_in", c, t), ab_qk[:, t, 512 * c:512 * c + 512] if c < 2 else ab_vu[:, t], 512)

            def ab_att():
                s = A_

                def exps(u):
                    if u >= len(AB_UNITS):
                        return
                    n = ab_keys(AB_UNITS[u][1]) * P
                    act.wait_ge(s["max_done"], u + 1)
                    link(nc.scalar.activation(att_P[:, u % 2, 0:n], flat(2 * (u % 2), n), ACT.Exp,
                                              bias=nmx[:, u % 4:u % 4 + 1], scale=HD ** -0.5,
                                              accum_out=esum[:, u % 4:u % 4 + 1]), s["exp_done"])

                exps(0)
                exps(1)
                for u, (h, t) in enumerate(AB_UNITS):
                    n = ab_keys(t) * P
                    act.wait_ge(s["pt_full"], u + 1)
                    link(nc.scalar.activation(att_PT[:, u % 2, 0:n], flat(4, n), ACT.Copy), s["pt_copied"])
                    exps(u + 2)

            def cd_att():
                s, n = C_, NT * P
                for i in range(2):
                    act.wait_ge(sem("lam_sum"), i + 1)
                    link(nc.scalar.activation(lam[:, i:i + 1], lam[:, i:i + 1], ACT.Exp), sem("lam_exp"))

                def exps(v):
                    if v >= 2 * len(CD_UNITS):
                        return
                    act.wait_ge(s["max_done"], v + 1)
                    link(nc.scalar.activation(cd_P[:, v % 4], flat(2 * (v % 2), n), ACT.Exp,
                                              bias=nmx[:, v % 8:v % 8 + 1], scale=HD ** -0.5,
                                              accum_out=esum[:, v % 8:v % 8 + 1]), s["exp_done"])

                exps(0)
                exps(1)
                for u in range(len(CD_UNITS)):
                    act.wait_ge(s["pt_full"], u + 1)
                    link(nc.scalar.activation(cd_PT[:, u % 2], flat(4, n), ACT.Copy), s["pt_copied"])
                    exps(2 * u + 2)
                    exps(2 * u + 3)

            def cd_conv_():
                roots(rstd[:, 0:NT_X, 0])()
                act.wait_ge(sem("conv_normed"), 1)
                link(nc.scalar.activation(cd_conv, cd_conv, ACT.Silu))

            def cd_proj(name, tl, dst):
                def go():
                    for c, w in enumerate((512, 256)):
                        for t in tl:
                            take((name, c, t), dst[:, t, 512 * c:512 * c + w], w)
                return go

            def ev_in():
                for c, d in enumerate((ev_qa, ev_ka, ev_va, ev_ga, ev_qb, ev_kv)):
                    for t in range(NT_X):
                        take(("ev_in", c, NT_C + t), d[:, t], 512 if c < 5 else 256)

            def ev_ret():
                act.wait_ge(sem("decay_abs"), 1)
                link(nc.scalar.activation(lg[:, 1], lg[:, 0], ACT.Exp, scale=-1.0), sem("decay_exp"))
                for h in range(4):
                    act.wait_ge(sem("decay_arg"), h + 1)
                    link(nc.scalar.activation(ev_D, ev_D, ACT.Exp), sem("decay_done"))
                roots(rstd[:, 0:NT_X, 0:4])()
                link(nc.scalar.activation(ev_ga, ev_ga, ACT.Silu), sem("ret_gate"))

            def ev_win():
                for u, (h, t) in enumerate(WIN_UNITS):
                    n = len(win_keys(t)) * P
                    act.wait_ge(sem("win_max_done"), u + 1)
                    link(nc.scalar.activation(ev_P[:, u % 2, 0:n], ev_Sm[:, u % 2, 0:n], ACT.Exp,
                                              bias=nmx[:, u % 4:u % 4 + 1], accum_out=esum[:, u % 4:u % 4 + 1]))
                    link(nc.scalar.activation(esum[:, 4 + u % 4:5 + u % 4], ev_Sm[:, u % 2, n:n + 1], ACT.Exp,
                                              bias=nmx[:, u % 4:u % 4 + 1]), sem("win_exp_done"))

            def fo_dft():
                for t in range(NT_X):
                    for g in range(4):
                        take(("fo_dft", t, g), fo_AB[:, t, g], 512)

            def fo_seq():
                for d in range(KD):
                    take(("fo_seq", d), fo_YT[:, d], 512)

            def route(m):
                def go():
                    act.wait_ge(M(m, "coarse_shifted"), 1)
                    link(nc.scalar.activation(mo_C8[:, :, 0:4], mo_C8[:, :, 0:4], ACT.Exp), M(m, "coarse_exp"))
                    act.wait_ge(M(m, "fine_diff"), 1)
                    link(nc.scalar.activation(mo_s[:, 3], mo_s[:, 2], ACT.Exp), M(m, "fine_exp"))
                return go

            def experts(m):
                chain = Link(act, M(m, "act_chain"))

                def one_pass(p):
                    def turned_x():
                        chain(nc.scalar.activation(mo_xgT, flat(2, D).rearrange("p (a c) -> p a c", a=KD), ACT.Copy),
                              M(m, "xgT_ready"))

                    chain.n = {}
                    chain.at = {M(m, "xgT_ready").name: p * (NE + 1)}
                    act.wait_ge(M(m, "xt_full"), p * (NE + 1) + 1)
                    turned_x()
                    with act.Fori(0, NE // 2) as i:
                        chain.n = {}
                        chain.at = {M(m, "xgT_ready").name: p * (NE + 1) + i * 2 + 1,
                                    M(m, "sg_done").name: p * NE + i * 2, M(m, "hT_ready").name: p * NE + i * 2}
                        for b in range(2):
                            e = p * NE + i * 2 + b
                            act.wait_ge(M(m, "gu_full"), e + 1)
                            chain(nc.scalar.activation(mo_sg, psum[:, 0, :], ACT.Silu), M(m, "sg_done"))
                            act.wait_ge(M(m, "xt_full"), p * (NE + 1) + i * 2 + b + 2)
                            turned_x()
                            act.wait_ge(M(m, "ht_full"), e + 1)
                            chain(nc.scalar.activation(mo_hT, psum[:, 4, :].rearrange("p (a c) -> p a c", a=4),
                                                       ACT.Copy), M(m, "hT_ready"))

                def go():
                    one_pass(0)
                    more_passes(act, m, one_pass)
                return go

            def norm(stage):
                return roots(rstd[:, 0:NT, 0])

            steps = {
                "mod0": mod(0), "mod1": mod(1), "ab_in": ab_in,
                "ab_rope": roots(rstd), "ab_att": ab_att,
                "f0x_in": gate("f0x_in", ACT.Silu, ffn_sg, SEQ, KF), "f0c_in": gate("f0c_in", ACT.Silu, ffn_sg, CTX, KF),
                "f1x_in": gate("f1x_in", ACT.Silu, ffn_sg, SEQ, KF),
                "cd_u": gate("cd_u", ACT.Sigmoid, cd_sg, SEQ, 2), "cd_conv": cd_conv_,
                "cd_q": cd_proj("cd_q", TILES_X, cd_tmp), "cd_k": cd_proj("cd_k", ALL, cd_tmp),
                "cd_v": cd_proj("cd_v", ALL, cd_v), "cd_att": cd_att,
                "cd_sub": roots(rstd[:, 0:NT_X, 0:6]),
                "ev_in": ev_in, "ev_ret": ev_ret, "ev_win": ev_win,
                "fo_dft": fo_dft, "fo_seq": fo_seq,
                "r0_route": route(0), "r1_route": route(1), "r0_experts": experts(0), "r1_experts": experts(1),
            }
            for f, n in (("ab", NT), ("f0x", NT_X), ("f0c", NT_C), ("cd", NT_X), ("f1x", NT_X), ("ev", NT_X),
                         ("fo", NT_X), ("r0", NT_X), ("r1", NT_X)):
                steps[f"{f}_norm"] = roots(rstd[:, 0:n, 0])
            run(act, steps, stage_act)

        @block.vector
        def _(dve):
            link = Link(dve, dve_chain)
            V = nc.vector

            def await_group(name):
                dve.wait_ge(psum_full, groups[name][0] + 1)
                return groups[name]

            def over(v, n):
                return v.unsqueeze(1).broadcast_to([P, n, v.shape[1]])

            def per(v, n):
                return v.unsqueeze(2).broadcast_to([P, v.shape[1], n])

            def take(name, dst, n, parts=P):
                g, b = await_group(name)
                src = flat(b, n)[0:parts]
                if len(dst.shape) == 3:
                    src = src.rearrange("p (a c) -> p a c", a=dst.shape[1])
                link(V.tensor_copy(dst, src), psum_free, g + 1)

            def mod(l):
                def go():
                    wait_loads(dve, f"mod{l}")
                    for c in range(12):
                        g, b = await_group(("mod", l, c))
                        link(V.tensor_tensor(mod_rows[:, 512 * c:512 * c + 512], psum[0:2, b, :],
                                             ada_bias[:, 512 * c:512 * c + 512], ALU.add), psum_free, g + 1)
                return go

            def mod_t(l):
                def go():
                    take(("modT", l), mod_cols, 96)
                    for k in (8, 32):
                        link(V.tensor_scalar(mod_cols[:, k:k + 8], mod_cols[:, k:k + 8], 1.0, None, ALU.add))
                return go

            def modulated(name, tl, shift):
                def go():
                    for t in tl:
                        g, b = await_group((name, t))
                        who = int(t < NT_C)
                        for k in range(KD):
                            ins = V.tensor_scalar(HT[:, k, tiles(t)], flat(b, D)[:, tiles(k)],
                                                  mod_cols[:, shift + 8 + k, who:who + 1],
                                                  mod_cols[:, shift + k, who:who + 1], ALU.mult, ALU.add)
                        link(ins, psum_free, g + 1)
                return go

            def plain(name, tl, dst, n, t0=0):
                def go():
                    for t in tl:
                        take((name, t), dst[:, :, tiles(t - t0)], n)
                return go

            def root_of(v, count, eps):
                link(V.tensor_scalar(v, v, 1.0 / count, eps, ALU.mult, ALU.add), stat_ready)
                dve.wait_ge(sqrt_done, link.n["stat_ready"])
                link(V.reciprocal(v, v))

            def residual(name, tl, rows, gates=True):
                def go():
                    if name in LOADS:
                        wait_loads(dve, name)
                    n = 0
                    for half in range(2):
                        for t in tl:
                            g, b = await_group((name, half, t))
                            cols = slice(512 * half, 512 * half + 512)
                            if gates:
                                row_ = rows.gate[len(rows.gate) - 1 if t < NT_C else 0]
                                link(V.tensor_tensor(rows.tmp[:, n % 2], psum[:, b, :], row_[:, cols], ALU.mult),
                                     psum_free, g + 1)
                                link(V.scalar_tensor_tensor(X[:, t, cols], X[:, t, cols], ALPHA, rows.tmp[:, n % 2],
                                                            ALU.mult, ALU.add))
                            else:
                                link(V.scalar_tensor_tensor(X[:, t, cols], X[:, t, cols], ALPHA, psum[:, b, :],
                                                            ALU.mult, ALU.add), psum_free, g + 1)
                            n += 1
                return go

            def statistics(src, slot_, n):
                for j in range(-(-n // 512)):
                    link(V.bn_stats(stat[:, slot_, j], src[:, 512 * j:min(512 * j + 512, n)]))
                link(V.bn_aggr(mv[:, slot_], stat[:, slot_, 0:-(-n // 512)]))

            def norm(name, tl, rows, eps):
                def go():
                    for j, t in enumerate(tl):
                        statistics(X[:, t], j, D)
                    n = len(tl)
                    link(V.tensor_copy(rstd[:, 0:n, 0], mv[:, 0:n, 1]))
                    root_of(rstd[:, 0:n, 0], 1.0, eps)
                    for j, t in enumerate(tl):
                        link(V.tensor_scalar(X[:, t], X[:, t], mv[:, j, 0:1], rstd[:, j, 0:1], ALU.subtract, ALU.mult))
                        link(V.tensor_tensor(X[:, t], X[:, t], rows.g, ALU.mult))
                        link(V.tensor_tensor(X[:, t], X[:, t], rows.b, ALU.add))
                return go

            def product(f, n_tok):
                def go():
                    for j in range(KF):
                        g, b = await_group((f"{f}_in", j))
                        dve.wait_ge(gate_done, gate_base[f] + j + 1)
                        link(V.tensor_tensor(ffn_hT[:, j, 0:n_tok], psum[:, b, 0:n_tok], ffn_sg[:, j % 2, 0:n_tok],
                                             ALU.mult), psum_free, g + 1)
                return go

            gate_base = dict(f0x=0, f0c=KF, cd_u=2 * KF, f1x=2 * KF + 2)

            def rotate(x, table, heads, axes, half, ta, tb):
                w = axes * 2 * half
                n = heads * w
                cos, sin = table[:, 0:w], table[:, w:2 * w]
                x3 = x.rearrange("p (h w) -> p h w", w=w)
                a3, b3 = (v[:, 0:n].rearrange("p (h w) -> p h w", w=w) for v in (ta, tb))
                link(V.tensor_tensor(a3, x3, over(cos, heads), ALU.mult))
                for ax in range(axes):
                    for s in range(2):
                        at = ax * 2 * half + s * half
                        of = ax * 2 * half + (1 - s) * half
                        link(V.tensor_tensor(b3[:, :, at:at + half], x3[:, :, of:of + half],
                                             over(sin[:, at:at + half], heads), ALU.mult))
                link(V.tensor_tensor(x, ta[:, 0:n], tb[:, 0:n], ALU.add))

            def ab_rope():
                wait_loads(dve, "ab_rope")
                for t in ALL:
                    link(V.tensor_tensor(tmp_a, ab_qk[:, t], ab_qk[:, t], ALU.mult))
                    link(V.reduce_sum(rstd[:, t], tmp_a.rearrange("p (h d) -> p h d", d=HD), axis=AX.X))
                root_of(rstd, HD, EPS)
                for t in ALL:
                    x3 = ab_qk[:, t].rearrange("p (h d) -> p h d", d=HD)
                    link(V.tensor_tensor(x3, x3, per(rstd[:, t], HD), ALU.mult))
                    link(V.tensor_tensor(x3[:, 0:12], x3[:, 0:12], over(qk_gain[:, 0], 12), ALU.mult))
                    link(V.tensor_tensor(x3[:, 12:16], x3[:, 12:16], over(qk_gain[:, 1], 4), ALU.mult))
                    if t >= NT_C:
                        rotate(ab_qk[:, t], rope_ax[:, t - NT_C], 16, 2, 16, tmp_a, tmp_b)
                    kd = ab_kd[:, t].rearrange("p (h c) -> p h c", h=4)
                    for j in range(2):
                        link(V.tensor_copy(kd[:, :, HD * j:HD * j + HD], x3[:, 12:16]))

            def ab_tr():
                for t in ALL:
                    take(("ab_q", t), ab_qT[:, :, tiles(t)], 768)
                for t in ALL:
                    take(("ab_k", t), ab_kT[:, :, tiles(t)], 512)

            def max_of(s, u, m, n):
                dve.wait_ge(s["score_full"], u + 1)
                link(V.reduce_max(nmx[:, u % m:u % m + 1], flat(2 * (u % 2), n), axis=AX.X))
                link(V.tensor_scalar(nmx[:, u % m:u % m + 1], nmx[:, u % m:u % m + 1], -(HD ** -0.5), None, ALU.mult),
                     s["max_done"])

            def ab_att():
                s = A_

                def mx(u):
                    if u < len(AB_UNITS):
                        max_of(s, u, 4, ab_keys(AB_UNITS[u][1]) * P)

                mx(0)
                mx(1)
                for u, (h, t) in enumerate(AB_UNITS):
                    mx(u + 2)
                    dve.wait_ge(s["o_full"], u + 1)
                    link(V.reciprocal(rsum[:, u % 4:u % 4 + 1], esum[:, u % 4:u % 4 + 1]))
                    link(V.tensor_scalar(O_all[:, t, HD * h:HD * h + HD], psum[:, 6 + u % 2, 0:HD],
                                         rsum[:, u % 4:u % 4 + 1], None, ALU.mult), s["o_done"])

            def ab_pool():
                wait_loads(dve, "ab_pool")
                for who, tl in (("x", TILES_X), ("c", TILES_C)):
                    for g in range(4):
                        take(("pooled", who, g), pooledT[:, g, 0:len(tl) * P], len(tl) * P, 64)
                    for t in tl:
                        g, b = await_group(("mixed", t))
                        link(V.tensor_tensor(O_all[:, t, 768:1024], psum[:, b, 0:256], pool_scale, ALU.mult),
                             psum_free, g + 1)

            def cd_u():
                take("conv_w", cd_wcol, 64)
                link(V.memset(cd_z, 0.0))
                for j in range(2):
                    g, b = await_group(("cd_u", j))
                    dve.wait_ge(gate_done, gate_base["cd_u"] + j + 1)
                    link(V.tensor_tensor(cd_z[:, j, 15:15 + SEQ], psum[:, b, :], cd_sg[:, j], ALU.mult),
                         psum_free, g + 1)

            def cd_conv_():
                wait_loads(dve, "cd_u")
                for j in range(2):
                    link(V.tensor_scalar(cd_acc[:, j], cd_z[:, j, 0:SEQ], cd_wcol[:, j, 0:1], cd_wcol[:, j, 31:32],
                                         ALU.mult, ALU.add))
                    for k in range(1, 31):
                        ins = V.scalar_tensor_tensor(cd_acc[:, j], cd_z[:, j, k:k + SEQ], cd_wcol[:, j, k:k + 1],
                                                     cd_acc[:, j], ALU.mult, ALU.add)
                        link(ins, sem("conv_done") if j == 1 and k == 30 else None)
                for t in range(NT_X):
                    take(("conv", t), cd_conv[:, t], 256)
                    statistics(cd_conv[:, t], t, 256)
                link(V.tensor_copy(rstd[:, 0:NT_X, 0], mv[:, 0:NT_X, 1]))
                root_of(rstd[:, 0:NT_X, 0], 1.0, EPS)
                for t in range(NT_X):
                    link(V.tensor_scalar(cd_conv[:, t], cd_conv[:, t], mv[:, t, 0:1], rstd[:, t, 0:1],
                                         ALU.subtract, ALU.mult))
                    link(V.tensor_tensor(cd_conv[:, t], cd_conv[:, t], cd_lng, ALU.mult))
                    link(V.tensor_tensor(cd_conv[:, t], cd_conv[:, t], cd_lnb, ALU.add),
                         sem("conv_normed") if t == NT_X - 1 else None)

            def cd_rope_(times):
                def go():
                    wait_loads(dve, "cd_q")
                    for t in TILES_X:
                        rotate(cd_tmp[:, t], cd_rope[:, t - NT_C], 12, 2, 16, cd_ta, cd_tb)
                return go

            def cd_att():
                wait_loads(dve, "cd_v")
                for i in range(2):
                    link(V.tensor_tensor(lam_in[:, 2 * i], lam_in[:, 2 * i], lam_in[:, 2 * i + 1], ALU.mult))
                    link(V.reduce_sum(lam[:, i:i + 1], lam_in[:, 2 * i], axis=AX.X), sem("lam_sum"))
                dve.wait_ge(sem("lam_exp"), 2)
                link(V.tensor_tensor(lam[:, 2:3], lam[:, 1:2], lam[:, 0:1], ALU.subtract))
                link(V.tensor_scalar(lam[:, 2:3], lam[:, 2:3], -LAM_INIT, None, ALU.add))
                s, n = C_, 2 * len(CD_UNITS)

                def mx(v):
                    if v < n:
                        max_of(s, v, 8, NT * P)

                mx(0)
                mx(1)
                for u, (h, t) in enumerate(CD_UNITS):
                    v = 2 * u
                    dve.wait_ge(s["exp_done"], v + 2)
                    a = v % 8
                    link(V.reciprocal(rsum[:, a:a + 2], esum[:, a:a + 2]))
                    link(V.tensor_tensor(rsum[:, a + 1:a + 2], rsum[:, a + 1:a + 2], lam[:, 2:3], ALU.mult))
                    link(V.tensor_scalar(cd_A[:, u % 2], cd_P[:, v % 4], rsum[:, a:a + 1], None, ALU.mult))
                    link(V.scalar_tensor_tensor(cd_A[:, u % 2], cd_P[:, v % 4 + 1], rsum[:, a + 1:a + 2], cd_A[:, u % 2],
                                                ALU.mult, ALU.add), s["diff_done"])
                    mx(v + 2)
                    dve.wait_ge(s["o_full"], u + 1)
                    link(V.tensor_copy(O4[:, t, tiles(h)], psum[:, 6 + u % 2, 0:P]), s["o_done"])
                    mx(v + 3)

            def cd_sub():
                for t in range(NT_X):
                    link(V.tensor_tensor(cd_sq, O4[:, t, 0:768], O4[:, t, 0:768], ALU.mult))
                    link(V.reduce_sum(rstd[:, t, 0:6], cd_sq.rearrange("p (h d) -> p h d", h=6), axis=AX.X))
                root_of(rstd[:, 0:NT_X, 0:6], 128.0, EPS)
                link(V.tensor_scalar(sub_gain, sub_gain, 1.0 - LAM_INIT, None, ALU.mult))
                for t in range(NT_X):
                    x3 = O4[:, t, 0:768].rearrange("p (h d) -> p h d", h=6)
                    link(V.tensor_tensor(x3, x3, per(rstd[:, t, 0:6], P), ALU.mult))
                    link(V.tensor_tensor(x3, x3, over(sub_gain, 6), ALU.mult))
                    link(V.tensor_copy(O4[:, t, 768:1024], cd_conv[:, t]))

            def ev_rope():
                wait_loads(dve, "ev_rope")
                for t in range(NT_X):
                    rotate(ev_qa[:, t], rope_ret[:, t], 4, 1, 64, ev_ta, ev_tb)
                    rotate(ev_ka[:, t], rope_ret[:, t], 4, 1, 64, ev_ta, ev_tb)
                    rotate(ev_qb[:, t], rope_win[:, t], 8, 1, 32, ev_ta, ev_tb)
                    rotate(ev_kv[:, t, 0:P], rope_win[:, t], 2, 1, 32, ev_ta, ev_tb)
                    kd = ev_kbd[:, t].rearrange("p (h c) -> p h c", h=2)
                    for j in range(2):
                        link(V.tensor_copy(kd[:, :, HD * j:HD * j + HD],
                                           ev_kv[:, t, 0:P].rearrange("p (h d) -> p h d", h=2)))

            def ev_tr():
                for name, dst, n in (("ev_qa", ev_qaT, 512), ("ev_ka", ev_kaT, 512), ("ev_qb", ev_qbT, 512),
                                     ("ev_kb", ev_kbT, 256)):
                    for t in range(NT_X):
                        take((name, t), dst[:, :, tiles(t)], n)

            def ev_ret():
                wait_loads(dve, "ev_ret")
                link(V.tensor_scalar(lg[:, 2], decay, -1.0, None, ALU.mult))
                link(V.tensor_tensor(lg[:, 0], decay, lg[:, 2], ALU.max), sem("decay_abs"))
                dve.wait_ge(sem("decay_exp"), 1)
                link(V.tensor_scalar(lg[:, 2], lg[:, 1], 2.0, None, ALU.add))
                link(V.reciprocal(lg[:, 2], lg[:, 2]))
                link(V.tensor_tensor(lg[:, 1], lg[:, 1], lg[:, 2], ALU.mult))
                link(V.tensor_tensor(lg[:, 2], lg[:, 1], lg[:, 1], ALU.mult))
                link(V.tensor_scalar(lg[:, 3], lg[:, 2], 1.0 / 17, 1.0 / 15, ALU.mult, ALU.add))
                for d in (13, 11, 9, 7, 5, 3, 1):
                    link(V.tensor_tensor(lg[:, 3], lg[:, 3], lg[:, 2], ALU.mult))
                    link(V.tensor_scalar(lg[:, 3], lg[:, 3], 1.0 / d, None, ALU.add))
                link(V.tensor_tensor(lg[:, 3], lg[:, 3], lg[:, 1], ALU.mult))
                link(V.tensor_scalar(lg[:, 3], lg[:, 3], -2.0, None, ALU.mult))
                link(V.tensor_scalar(lg[:, 2], decay, 0.0, None, ALU.min))
                link(V.tensor_tensor(lg[:, 4], lg[:, 3], lg[:, 2], ALU.add))
                for h in range(4):
                    for mt in range(NT_X):
                        at = 384 - P * mt
                        link(V.tensor_scalar(ev_D[:, mt], dist[:, 0, at:at + SEQ], lg[:, 4, 0, h:h + 1], None, ALU.mult))
                        link(V.scalar_tensor_tensor(ev_D[:, mt], dist[:, 1, at:at + SEQ], lg[:, 4, 1, h:h + 1],
                                                    ev_D[:, mt], ALU.mult, ALU.add),
                             sem("decay_arg") if mt == NT_X - 1 else None)
                    dve.wait_ge(sem("decay_done"), h + 1)
                    for mt in range(NT_X):
                        g, b = await_group(("ret_s", h, mt))
                        link(V.scalar_tensor_tensor(ev_ST[:, mt], psum[:, b, :], P ** -0.5, ev_D[:, mt],
                                                    ALU.mult, ALU.mult), psum_free, g + 1)
                    for t in range(NT_X):
                        take(("ret_y", h, t), O4[:, t, tiles(h)], P)
                for t in range(NT_X):
                    for h in range(4):
                        link(V.bn_stats(stat[:, 0, 0], O4[:, t, tiles(h)]))
                        link(V.bn_aggr(ret_mv[:, t, h], stat[:, 0, 0:1]))
                        link(V.tensor_copy(rstd[:, t, h:h + 1], ret_mv[:, t, h, 1:2]))
                root_of(rstd[:, 0:NT_X, 0:4], 1.0, GN_EPS)
                dve.wait_ge(sem("ret_gate"), 1)
                for t in range(NT_X):
                    for h in range(4):
                        link(V.tensor_scalar(O4[:, t, tiles(h)], O4[:, t, tiles(h)], ret_mv[:, t, h, 0:1],
                                             rstd[:, t, h:h + 1], ALU.subtract, ALU.mult))
                    link(V.tensor_tensor(O4[:, t, 0:512], O4[:, t, 0:512], gn_row, ALU.mult))
                    link(V.tensor_tensor(O4[:, t, 0:512], O4[:, t, 0:512], ev_ga[:, t], ALU.mult))

            def ev_win():
                wait_loads(dve, "ev_win")

                def masked(u):
                    if u >= len(WIN_UNITS):
                        return
                    h, t = WIN_UNITS[u]
                    ks = win_keys(t)
                    n = len(ks) * P
                    g, b = await_group(("win_s", u))
                    first = ks[0] - t + 1
                    link(V.scalar_tensor_tensor(ev_Sm[:, u % 2, 0:n], psum[:, b, 0:n], HD ** -0.5,
                                                band[:, first:first + len(ks)].rearrange("p a c -> p (a c)"),
                                                ALU.mult, ALU.add), psum_free, g + 1)
                    link(V.tensor_copy(ev_Sm[:, u % 2, n:n + 1], sinks[:, h:h + 1]))
                    link(V.reduce_max(nmx[:, u % 4:u % 4 + 1], ev_Sm[:, u % 2, 0:n + 1], axis=AX.X))
                    link(V.tensor_scalar(nmx[:, u % 4:u % 4 + 1], nmx[:, u % 4:u % 4 + 1], -1.0, None, ALU.mult),
                         sem("win_max_done"))

                masked(0)
                for u, (h, t) in enumerate(WIN_UNITS):
                    n = len(win_keys(t)) * P
                    masked(u + 1)
                    take(("win_pt", u), ev_PT[:, u % 2, 0:n], n)
                    g, b = await_group(("win_o", u))
                    a = slice(u % 4, u % 4 + 1)
                    link(V.tensor_tensor(rsum[:, a], esum[:, a], esum[:, 4 + u % 4:5 + u % 4], ALU.add))
                    link(V.reciprocal(rsum[:, a], rsum[:, a]))
                    link(V.tensor_scalar(O4[:, t, 512 + HD * h:576 + HD * h], psum[:, b, 0:HD], rsum[:, a], None,
                                         ALU.mult), psum_free, g + 1)

            def route(m):
                def go():
                    s = [mo_s[:, j] for j in range(16)]
                    wait_loads(dve, f"r{m}_ht")
                    link(V.memset(mo_C8, -3e38))
                    link(V.memset(mo_idxf, BIG_IDX))
                    link(V.memset(mo_xg, 0.0))
                    g, b = await_group(("logits", m))
                    link(V.tensor_tensor(mo_L, psum[:, b, 0:144].rearrange("p (t c) -> p t c", c=36),
                                         over(mo_bias, NT_X), ALU.add), psum_free, g + 1)
                    link(V.tensor_copy(mo_C8[:, :, 0:4], mo_L[:, :, 0:4]))
                    for t in range(NT_X):
                        link(V.max(mo_m8[:, t], mo_C8[:, t]))
                        link(V.max_index(mo_ix[:, t], mo_m8[:, t], mo_C8[:, t]))
                    link(V.tensor_copy(mo_ixf, mo_ix))
                    link(V.tensor_copy(s[0], mo_ixf[:, :, 0]))
                    link(V.tensor_tensor(mo_C8[:, :, 0:4], mo_C8[:, :, 0:4], per(mo_m8[:, :, 0], 4), ALU.subtract),
                         M(m, "coarse_shifted"))
                    for t in range(NT_X):
                        link(V.tensor_scalar(mo_G[:, t], mo_iota[:, 0:4], s[0][:, t:t + 1], None, ALU.is_equal))
                    for q in range(4):
                        fine = mo_L[:, :, 4 + 8 * q:12 + 8 * q]
                        dst = mo_FS if q == 0 else mo_t8
                        link(V.tensor_tensor(dst, fine, per(mo_G[:, :, q], 8), ALU.mult))
                        if q:
                            link(V.tensor_tensor(mo_FS, mo_FS, mo_t8, ALU.add))
                    for t in range(NT_X):
                        link(V.max(mo_m8[:, t], mo_FS[:, t]))
                        link(V.max_index(mo_ix[:, t], mo_m8[:, t], mo_FS[:, t]))
                    link(V.tensor_copy(mo_ixf, mo_ix))
                    for j in range(2):
                        link(V.scalar_tensor_tensor(s[4 + j], s[0], 8.0, mo_ixf[:, :, j], ALU.mult, ALU.add))
                    link(V.tensor_tensor(s[2], mo_m8[:, :, 1], mo_m8[:, :, 0], ALU.subtract), M(m, "fine_diff"))
                    for t in range(NT_X):
                        link(V.tensor_scalar(mo_A1[:, t], mo_iota[:, 0:NE], s[4][:, t:t + 1], None, ALU.is_equal))
                        link(V.tensor_scalar(mo_A2[:, t], mo_iota[:, 0:NE], s[5][:, t:t + 1], None, ALU.is_equal))
                    link(V.tensor_tensor(mo_A, mo_A1, mo_A2, ALU.add), M(m, "picked"))
                    dve.wait_ge(M(m, "coarse_exp"), 1)
                    link(V.reduce_sum(s[6], mo_C8[:, :, 0:4], axis=AX.X))
                    link(V.reciprocal(s[6], s[6]))
                    dve.wait_ge(M(m, "fine_exp"), 1)
                    link(V.tensor_scalar(s[7], s[3], 1.0, None, ALU.add))
                    link(V.reciprocal(s[7], s[7]))
                    link(V.tensor_tensor(s[8], s[7], s[6], ALU.mult))
                    link(V.tensor_tensor(s[9], s[8], s[3], ALU.mult))
                    link(V.memset(mo_F[:, :, :, 0], 1.0))
                    for t in range(NT_X):
                        link(V.tensor_scalar(mo_F[:, t, :, 1], mo_F[:, t, :, 0], mo_tok[:, t:t + 1], None, ALU.mult))
                        link(V.tensor_scalar(mo_F[:, t, :, 2], mo_A2[:, t], float(SEQ), mo_tok[:, t:t + 1],
                                             ALU.mult, ALU.add))
                        link(V.tensor_scalar(mo_F[:, t, :, 3], mo_A1[:, t], s[8][:, t:t + 1], None, ALU.mult))
                        link(V.scalar_tensor_tensor(mo_F[:, t, :, 3], mo_A2[:, t], s[9][:, t:t + 1],
                                                    mo_F[:, t, :, 3], ALU.mult, ALU.add))
                    g, b = await_group(("rank", m))
                    link(V.scalar_tensor_tensor(mo_RK, psum[:, b, 0:P].rearrange("p (t e) -> p t e", t=NT_X), 1.0, mo_A,
                                                ALU.add, ALU.mult))
                    link(V.tensor_scalar(mo_RK, mo_RK, -1.0, None, ALU.add))
                    link(V.reduce_max(mo_np[:, 0:1], psum[:, b, P:P + NE], axis=AX.X), psum_free, g + 1)
                    for j in range(1, NT_X):
                        link(V.tensor_scalar(mo_np[:, j:j + 1], mo_np[:, 0:1], P * j + 0.5, None, ALU.is_ge))
                    for j in range(2, NT_X):
                        link(V.tensor_tensor(mo_np[:, 1:2], mo_np[:, 1:2], mo_np[:, j:j + 1], ALU.add))
                    link(V.tensor_scalar(mo_np[:, 1:2], mo_np[:, 1:2], 1.0, None, ALU.add))
                    link(V.tensor_copy(mo_npi[:, 0:1], mo_np[:, 1:2]))
                return go

            def experts(m):
                chain = Link(dve, M(m, "dve_chain"))

                def one_pass(p):
                    first = isinstance(p, int)
                    chain.n, chain.at = {}, {M(m, "dve_chain").name: p * DVE_PER_PASS,
                                             M(m, "sel_ready").name: p * NE}
                    if not first:
                        dve.wait_ge(M(m, "pass_done"), p)
                        chain(V.tensor_scalar(mo_RK, mo_RK, -float(P), None, ALU.add))
                    else:
                        chain(V.tensor_copy(mo_RK, mo_RK))
                    for e in range(NE):
                        if not first or e >= 2:
                            dve.wait_ge(M(m, "sel_used"), p * NE + e - 1)
                        for t in range(NT_X):
                            ins = V.tensor_scalar(mo_sel[:, 4 * (e % 2) + t], mo_iota, mo_RK[:, t, e:e + 1], None,
                                                  ALU.is_equal)
                        chain(ins, M(m, "sel_ready"))
                    dve.wait_ge(M(m, "sel_used"), p * NE + NE)
                    chain(V.tensor_copy(mo_meta, psum[:, 7, 0:P].rearrange("p (e f) -> p e f", f=4)))
                    for j in range(2):
                        chain(V.tensor_scalar(mo_idxf[:, j, 0:NE], mo_meta[:, :, 0], -BIG_IDX, BIG_IDX,
                                              ALU.mult, ALU.add))
                        chain(V.tensor_tensor(mo_idxf[:, j, 0:NE], mo_idxf[:, j, 0:NE], mo_meta[:, :, 1 + j], ALU.add))
                    chain(V.tensor_copy(mo_gate, mo_meta[:, :, 3]))
                    chain(V.tensor_copy(mo_idx, mo_idxf))
                    V.tensor_copy(mo_cnt[:, 0:1], mo_np[:, 0:1]).then_inc(M(m, "lists_ready"), 1)
                    with dve.Fori(0, NE // 2) as i:
                        chain.n, chain.at = {}, {M(m, n).name: p * NE + i * 2 + c for n, c in
                                                 (("h_ready", 0), ("gu_free", 1), ("y_free", 1), ("y_ready", 0))}
                        for b in range(2):
                            e = p * NE + i * 2 + b
                            dve.wait_ge(M(m, "sg_done"), e + 1)
                            chain(V.tensor_tensor(mo_h, psum[:, 1, :], mo_sg, ALU.mult), M(m, "h_ready"))
                            dve.sem_inc(M(m, "gu_free"), 1)
                            dve.wait_ge(M(m, "y_full"), e + 1)
                            dve.wait_ge(M(m, "y_buf_free"), e + 1)
                            chain(V.tensor_scalar(mo_y[:, b], flat(5, D), mo_gate[:, bass.ds(i * 2 + b, 1)], None,
                                                  ALU.mult), M(m, "y_ready"))
                            dve.sem_inc(M(m, "y_free"), 1)

                def go():
                    dve.sem_inc(M(m, "gu_free"), 1)
                    dve.sem_inc(M(m, "y_free"), 1)
                    one_pass(0)
                    more_passes(dve, m, one_pass)
                return go

            def moe_norm(m):
                def go():
                    wait_loads(dve, f"r{m}_norm")
                    for t in range(NT_X):
                        link(V.tensor_tensor(mo_y12[:, 0, t], mo_y12[:, 0, t], mo_y12[:, 1, t], ALU.add))
                        link(V.scalar_tensor_tensor(X[:, NT_C + t], X[:, NT_C + t], ALPHA, mo_y12[:, 0, t],
                                                    ALU.mult, ALU.add))
                    norm(f"r{m}", TILES_X, rows_moe, LN_EPS2)()
                return go

            steps = {
                "mod0": mod(0), "modT0": mod_t(0), "mod1": mod(1), "modT1": mod_t(1),
                "ab_ht": modulated("ab_ht", ALL, 0), "ab_rope": ab_rope, "ab_tr": ab_tr, "ab_att": ab_att,
                "ab_pool": ab_pool, "ab_ot": plain("ab_ot", ALL, OT_ab, D),
                "ab_out": residual("ab_out", ALL, rows_ab), "ab_norm": norm("ab", ALL, rows_ab, EPS),
                "cd_ht": modulated("cd_ht", ALL, 0), "cd_u": cd_u, "cd_conv": cd_conv_,
                "cd_qrope": cd_rope_(0), "cd_qt": plain("cd_qt", TILES_X, cd_qT, 768, NT_C),
                "cd_krope": cd_rope_(1), "cd_kt": plain("cd_kt", ALL, cd_kT, 768),
                "cd_att": cd_att, "cd_sub": cd_sub, "cd_ot": plain("cd_ot", TILES_X, OT_cd, D, NT_C),
                "cd_out": residual("cd_out", TILES_X, rows_cd), "cd_norm": norm("cd", TILES_X, rows_cd, EPS),
                "ev_ht": plain("ev_ht", TILES_X, HT, D), "ev_rope": ev_rope, "ev_tr": ev_tr, "ev_ret": ev_ret,
                "ev_win": ev_win, "ev_ot": plain("ev_ot", TILES_X, OT_ev, D, NT_C),
                "ev_out": residual("ev_out", TILES_X, rows_ev, False), "ev_norm": norm("ev", TILES_X, rows_ev, LN_EPS2),
                "fo_ht": plain("fo_ht", TILES_X, HT, D),
                "fo_out": residual("fo_out", TILES_X, rows_fo, False), "fo_norm": norm("fo", TILES_X, rows_fo, LN_EPS2),
            }
            for f, tl in (("f0x", TILES_X), ("f0c", TILES_C), ("f1x", TILES_X)):
                steps[f"{f}_ht"] = modulated(f"{f}_ht", tl, 24)
                steps[f"{f}_in"] = product(f, len(tl) * P)
                steps[f"{f}_out"] = residual(f"{f}_out", tl, rows_ffn)
                steps[f"{f}_norm"] = norm(f, tl, rows_ffn, EPS)
            for m in range(2):
                steps[f"r{m}_ht"] = plain(f"r{m}_ht", TILES_X, HT, D)
                steps[f"r{m}_route"] = route(m)
                steps[f"r{m}_experts"] = experts(m)
                steps[f"r{m}_norm"] = moe_norm(m)
            run(dve, steps, stage_dve)

        @block.gpsimd
        def _(pool):
            def loads(stage):
                for dst, src in LOADS[stage]:
                    pool.dma_start(dst, src, allow_slow_non_contiguous=stage[:3] == "mod").then_inc(sem("loads_" + stage), 16)

            def store_mod(l):
                def go():
                    pool.dma_start(A["mod"][l], mod_rows).then_inc(sem("mod_stored"), 16)
                    pool.wait_ge(sem("mod_stored"), 16 * (l + 1))
                return go

            def route(m):
                def go():
                    for t in range(NT_X):
                        pool.dma_start(A[f"xs{m}"][tiles(t)], X[:, NT_C + t]).then_inc(M(m, "x_stored"), 16)
                    pool.wait_ge(M(m, "x_stored"), 16 * NT_X)
                return go

            def await_count(s, value):
                pool.wait_ge(s, value)
                if not isinstance(value, int):
                    pool.sem_inc(sem("pool_steps"), 1)

            def experts(m):
                def one_pass(p):
                    await_count(M(m, "lists_ready"), p + 1)

                    def gather(e):
                        if e > NE:
                            return
                        if e >= 2:
                            await_count(M(m, "xt_full"), p * (NE + 1) + e - 1)
                        pool.indirect_dma_start(
                            out=mo_xg[:, e % 2], out_offset=None, in_=A[f"xs{m}"][:, :],
                            in_offset=bass.IndirectOffsetOnAxis(ap=mo_idx[:, 0, e:e + 1], axis=0),
                            bounds_check=SEQ - 1, oob_is_err=False).then_inc(M(m, f"xg_ready{e % 2}"), 16)

                    def buffer_free(e):
                        await_count(M(m, f"y_stored{e % 2}"), (p * (NE // 2) + e // 2 + 1) * 16)
                        pool.sem_inc(M(m, "y_buf_free"), 1)

                    gather(0)
                    gather(1)
                    for e in range(NE):
                        gather(e + 2)
                        await_count(M(m, "y_ready"), p * NE + e + 1)
                        pool.indirect_dma_start(
                            out=A[f"y{m}"][:, :], out_offset=bass.IndirectOffsetOnAxis(ap=mo_idx[:, 1, e:e + 1], axis=0),
                            in_=mo_y[:, e % 2], in_offset=None,
                            bounds_check=2 * SEQ - 1, oob_is_err=False).then_inc(M(m, f"y_stored{e % 2}"), 16)
                        if e >= 1:
                            buffer_free(e - 1)
                    buffer_free(NE - 1)
                    await_count(M(m, "xg_ready0"), p * (17 * 16) + 17 * 16)
                    pool.sem_inc(M(m, "pass_done"), 1)

                def go():
                    pool.sem_inc(M(m, "y_buf_free"), 2)
                    one_pass(0)
                    more_passes(pool, m, one_pass)
                return go

            steps = {s: (lambda s: lambda: loads(s))(s) for s in LOADS}
            steps["modT0"], steps["modT1"] = store_mod(0), store_mod(1)
            for m in range(2):
                steps[f"r{m}_route"], steps[f"r{m}_experts"] = route(m), experts(m)
            run(pool, steps)
            for t in range(NT_X):
                pool.dma_start(A["out"][0, tiles(t)], X[:, NT_C + t]).then_inc(sem("stored"), 16)
            pool.wait_ge(sem("stored"), 16 * NT_X)

        @block.sync
        def _(sp):
            sp.dma_start(ident, A["ident"]).then_inc(sem("ident_loaded"), 16)
            for t in range(NT_C):
                sp.dma_start(X[:, t], A["ctx"][0, tiles(t)]).then_inc(sem("x_loaded"), 16)
            for t in range(NT_X):
                sp.dma_start(X[:, NT_C + t], A["x"][0, tiles(t)]).then_inc(sem("x_loaded"), 16)
            used = [c for c in range(len(chunks)) if c in chunk_read]
            last_user = {}

            def load(i):
                ch = chunks[i]
                if ch["slot"] in last_user:
                    sp.wait_ge(*chunk_read[last_user[ch["slot"]]])
                last_user[ch["slot"]] = i
                for c0, src in ch["parts"]:
                    n = src.shape[2]
                    sp.dma_start(slot(i)[:, :, c0:c0 + n], src).then_inc(w_ready[ch["slot"]], 16)

            def expert_weights(m):
                first = STAGES.index(f"r{m}_experts")

                def one(p, i, b, part, wait=True):
                    if wait:
                        e1 = p * NE + i * 2 + b - 1
                        sp.wait_ge(M(m, "gu_full" if part < 2 else "y_full"), e1)
                    name = ("expert_w_gate_2", "expert_w_up_2", "expert_w_down_2")[part]
                    src = A[name][m, bass.ds(i * 2 + b, 1)].rearrange("o (k p) n -> p (o k) n", p=P)
                    dst = region(MOE_RING_KB[3 * b + part], KD if part < 2 else 4, 512 if part < 2 else D)
                    sp.dma_start(dst, src).then_inc(M(m, f"w_ready{3 * b + part}"), 16)

                for b in range(2):
                    for part in range(3):
                        s = 3 * b + part
                        if s < 5 and s in last_user:
                            sp.wait_ge(*chunk_read[last_user[s]])
                        else:
                            sp.wait_ge(stage_act, first)
                            sp.wait_ge(stage_dve, first)
                        one(0, 0, b, part, wait=False)
                with sp.Fori(1, NE // 2) as i:
                    for b in range(2):
                        for part in range(3):
                            one(0, i, b, part)

                def one_pass(p):
                    with sp.Fori(0, NE // 2) as i:
                        for b in range(2):
                            for part in range(3):
                                one(p, i, b, part)

                sp.wait_ge(stage_act, first)
                sp.wait_ge(stage_dve, first)
                more_passes(sp, m, one_pass)
                sp.wait_ge(stage_act, first + 1)
                sp.wait_ge(stage_dve, first + 1)
                last_user.clear()

            for i in used:
                if i == before_experts0 and "r0_experts" in STAGES:
                    expert_weights(0)
                load(i)
            if used and used[-1] < before_experts0 and "r0_experts" in STAGES:
                expert_weights(0)
            if "r1_experts" in STAGES:
                expert_weights(1)


_INS = """x c ctx c_ctx ab_w_in ab_q_gain ab_k_gain ab_w_pool ab_pool_scale ab_w_out cd_w_in cd_lambda_q1 cd_lambda_k1
    cd_lambda_q2 cd_lambda_k2 cd_subln_gain cd_conv_w cd_conv_b cd_conv_ln_g cd_conv_ln_b cd_w_out ada_w ada_b ln1_g
    ln1_b ln2_g ln2_b ffn_w_in ffn_w_out w_in_even_2 ret_decay_logit_2 ret_gn_gain_2 sink_logit_2 w_out_even_2
    w_out_fourier_2 ln1_gain_2 ln1_bias_2 ln2_gain_2 ln2_bias_2 router_coarse_w_2 router_coarse_b_2 router_fine_w_2
    router_fine_b_2 expert_w_gate_2 expert_w_up_2 expert_w_down_2""".split()
STOP = None


def kernel(**inputs):
    import concourse.bacc as bacc
    from concourse.bass_utils import run_bass_kernel_spmd

    nc = bacc.Bacc("TRN2", target_bir_lowering=False, num_devices=1)
    arrays = {n: np.ascontiguousarray(inputs[n]) for n in _INS}
    arrays.update(constants())
    aps = {n: nc.dram_tensor(f"in_{n}", a.shape, F32, kind="ExternalInput").ap() for n, a in arrays.items()}
    for n, shape in (("mod", (2, 2, 6 * D)), ("xs0", (SEQ, D)), ("xs1", (SEQ, D)), ("y0", (2 * SEQ, D)),
                     ("y1", (2 * SEQ, D))):
        aps[n] = nc.dram_tensor(n, shape, F32, kind="Internal").ap()
    aps["out"] = nc.dram_tensor("out", (1, SEQ, D), F32, kind="ExternalOutput").ap()
    build(nc, aps, STOP)
    r = run_bass_kernel_spmd(nc, [{f"in_{n}": a for n, a in arrays.items()}], core_ids=[0])
    return r.results[0]["out"]
```

```python
import math
from contextlib import ExitStack

import numpy as np
import concourse.bass as bass
from concourse import mybir

F32, I32, U32 = mybir.dt.float32, mybir.dt.int32, mybir.dt.uint32
ACT, ALU, AX = mybir.ActivationFunctionType, mybir.AluOpType, mybir.AxisListType

P = 128
D = 1024
KD = D // P
SEQ, CTX = 512, 256
NT_C, NT_X = CTX // P, SEQ // P
NT = NT_C + NT_X
HD = 64
GRID_W = 64
FFN = 2816
KF = FFN // P
EPS, LN_EPS2, GN_EPS = 1e-6, 1e-5, 1e-6
ALPHA = (2.0 * 2) ** 0.25
LAM_INIT = 0.8 - 0.6 * math.exp(-0.3)
NE = 32
BIG_IDX = 4096.0
NEG = -1e30
DVE_PER_PASS = 8


def constants():
    f = np.float32
    c = {}
    c["ident"] = np.eye(P, dtype=f)
    t = np.arange(SEQ)
    row, col = (t // GRID_W).astype(f), (t % GRID_W).astype(f)
    fr = (10000.0 ** (-np.arange(0, 32, 2, dtype=f) / 32)).astype(f)
    cs, sn = [], []
    for pos in (row, col):
        a = (pos[:, None] * fr[None]).astype(f).astype(np.float64)
        cs += [np.cos(a), np.cos(a)]
        sn += [-np.sin(a), np.sin(a)]
    c["rope_ax"] = np.concatenate([np.concatenate(cs, 1), np.concatenate(sn, 1)], 1).astype(f)
    for name, half in (("rope_ret", 64), ("rope_win", 32)):
        inv = (10000.0 ** (-np.arange(half, dtype=f) / half)).astype(f)
        a = (t.astype(f)[:, None] * inv[None]).astype(f).astype(np.float64)
        c[name] = np.concatenate([np.cos(a), np.cos(a), -np.sin(a), np.sin(a)], 1).astype(f)

    def pool(n):
        out = np.zeros((4, n, n), np.float64)
        for g, w in enumerate((2, 4, 8, 16)):
            for i in range(n):
                lo, hi = max(i - w // 2, 0), min(i + (w - 1 - w // 2) + 1, n)
                out[g, lo:hi, i] += 1.0 / (hi - lo)
                out[g, i, i] -= 1.0
        return out

    c["pool_x"] = np.ascontiguousarray(pool(SEQ).reshape(4, NT_X, P, SEQ).transpose(2, 0, 1, 3)).astype(f)
    c["pool_c"] = np.ascontiguousarray(pool(CTX).reshape(4, NT_C, P, CTX).transpose(2, 0, 1, 3)).astype(f)
    j, p = np.arange(896)[None] - 384, np.arange(P)[:, None]
    c["dist"] = np.stack([np.maximum(j - p, 0), np.maximum(p - j, 0)], 1).astype(f)
    i, k = np.arange(P)[:, None], np.arange(P)[None]
    c["band"] = np.stack([np.where(i <= k, 0, NEG), np.zeros((P, P)), np.where(k <= i, 0, NEG)], 1).astype(f)
    kk = np.outer(np.arange(256), np.arange(256)) % 256 * (2 * np.pi / 256)
    c["dft_c"] = np.ascontiguousarray(
        np.concatenate([np.cos(kk), np.sin(kk)], 1).reshape(2, P, 512).transpose(1, 0, 2)).astype(f)
    kk = np.outer(np.arange(SEQ), np.arange(SEQ)) % SEQ * (2 * np.pi / SEQ)
    s = 1.0 / math.sqrt(SEQ * 256)
    c["dft_s"] = np.ascontiguousarray(
        np.stack([np.cos(kk) * s, -np.sin(kk) * s]).reshape(2, NT_X, P, SEQ).transpose(2, 0, 1, 3)).astype(f)
    c["before"] = np.concatenate([np.triu(np.ones((P, P)), 1), np.ones((P, P))], 1).astype(f)
    c["iota"] = np.tile(np.arange(P, dtype=f), (P, 1))
    c["tok"] = (np.arange(NT_X)[None] * P + np.arange(P)[:, None]).astype(f)
    return c


def build(nc, A, stop):
    ctx = ExitStack()
    with ctx:
        KB = 256
        arena = ctx.enter_context(nc.sbuf_tensor("arena", [P, 207 * KB], F32))

        def region(kb, *shape, parts=P):
            n = int(np.prod(shape))
            at = int(round(kb * KB))
            assert at + n <= 207 * KB, (kb, shape)
            v = arena[0:parts, at:at + n]
            if len(shape) == 1:
                return v
            names = "abcde"[:len(shape)]
            return v.rearrange(f"p ({' '.join(names)}) -> p {' '.join(names)}",
                               **{n_: s for n_, s in zip(names[1:], shape[1:])})

        RING_KB = [0, 16, 32, 48, 64]
        MOE_RING_KB = RING_KB + [128]
        X = region(80, NT, D)
        HT = region(104, KD, NT * P)
        BIG, MISC = 128, 200

        ident = ctx.enter_context(nc.sbuf_tensor("ident", [P, P], F32))[:, :]
        mod_cols = region(MISC, 48, 2)
        stat = region(MISC + 0.5, NT, 2, 6)
        mv = region(MISC + 1, NT, 2)
        rstd = region(MISC + 1.0625, NT, 16)
        nmx = region(MISC + 3.5, 8)
        esum = region(MISC + 3.75, 8)
        rsum = region(MISC + 4, 8)
        lam = region(MISC + 4.25, 8)
        psum = ctx.enter_context(nc.psum_tensor("psum", [P, 8, 512], F32))

        sems = {}

        def sem(name):
            if name not in sems:
                sems[name] = ctx.enter_context(nc.semaphore(name))
            return sems[name]

        psum_full = sem("psum_full")
        free_by = {"act": sem("psum_free_act"), "dve": sem("psum_free_dve")}
        x_normed = sem("x_normed")
        w_used = sem("w_used")
        act_chain, dve_chain = sem("act_chain"), sem("dve_chain")
        stage_act, stage_dve = sem("stage_act"), sem("stage_dve")
        gate_done = sem("gate_done")
        stat_ready, sqrt_done = sem("stat_ready"), sem("sqrt_done")
        w_ready = [sem(f"w_ready{i}") for i in range(5)]

        mod_rows, ada_bias = region(BIG, 6 * D, parts=2), region(BIG + 24, 6 * D, parts=2)
        c_cols, c_silu = region(BIG + 48, 2, KD), region(BIG + 49, KD, 2)
        ab_qk, ab_vu = region(BIG, NT, 1024), region(BIG + 24, NT, 512)
        ab_qT = region(BIG + 36, 6, NT * P)
        ab_kT = region(BIG, 4, 2, NT * P)
        ab_kd = region(BIG + 60, NT, 512)
        tmp_a, tmp_b = region(BIG + 52, 1024), region(BIG + 56, 1024)
        qk_gain = region(MISC + 5, 2, HD)
        rope_ax = region(MISC + 1.5, NT_X, 128)
        att_P, att_PT = region(BIG + 54, 2, 768), region(BIG + 60, 2, 768)
        pooledT, w_pool = region(BIG + 54, 4, 512, parts=64), region(BIG + 62, 4, 64, parts=64)
        pool_scale = region(BIG + 63, 256)
        O_all = region(104, NT, D)
        cd_conv = region(80, NT_X, 256)
        cd_qT = region(BIG, 6, 2, SEQ)
        cd_kT, cd_v = region(BIG + 24, 6, NT * P), region(BIG + 42, NT, 768)
        cd_tmp = region(BIG + 60, 4, 768)
        cd_z, cd_acc, cd_sg = region(BIG, 2, 544), region(BIG + 5, 2, SEQ), region(BIG + 9, 2, SEQ)
        cd_wrow, cd_wcol = region(BIG + 13, 256, parts=32), region(BIG + 14, 2, 32)
        cd_lng, cd_lnb = region(BIG + 15, 256), region(BIG + 16, 256)
        cd_ta, cd_tb = region(84, 384), region(85.5, 384)
        cd_P, cd_PT = region(BIG + 60, 4, 768), region(120, 2, 768)
        cd_sq = region(BIG + 60, 768)
        O4 = region(104, NT_X, D)
        lam_in, sub_gain = region(126, 4, HD), region(127, 128)
        ev_qa, ev_ka, ev_va, ev_ga, ev_qb = (region(BIG + 8 * i, NT_X, 512) for i in range(5))
        ev_kv = region(BIG + 40, NT_X, 256)
        ev_qaT, ev_kaT = region(BIG + 44, 4, SEQ), region(BIG + 52, 4, SEQ)
        ev_qbT, ev_kbT = region(BIG + 60, 4, SEQ), region(124, 2, SEQ)
        rope_ret, rope_win = region(BIG + 44, NT_X, 256), region(BIG + 48, NT_X, 128)
        ev_ta, ev_tb, ev_kbd = region(BIG + 50, 512), region(BIG + 52, 512), region(BIG + 68, NT_X, 256)
        ev_D, ev_ST = region(BIG, 4, SEQ), region(BIG + 8, 4, SEQ)
        dist = region(BIG + 32, 2, 896)
        gn_row = region(120, 512)
        decay = region(122, 2, 4)
        lg = region(122.25, 8, 2, 4)
        sinks = region(122.75, 8)
        ev_Sm, ev_P, ev_PT = region(BIG, 2, 388), region(BIG + 4, 2, 384), region(BIG + 8, 2, 384)
        band = region(BIG + 12, 3, P)
        fo_AB, fo_YT = region(BIG, NT_X, 4, 512), region(BIG + 32, KD, SEQ)
        ffn_hT, ffn_sg = region(BIG, KF, SEQ), region(BIG + 44, 2, SEQ)
        OT_ab, OT_cd, OT_ev = region(BIG + 36, KD, NT * P), region(BIG, KD, SEQ), region(BIG + 44, KD, SEQ)

        class Rows:

            def __init__(self, kb, gates):
                self.gate = [region(kb + 4 * i, D) for i in range(gates)]
                kb += 4 * gates
                self.g, self.b, self.tmp = region(kb, D), region(kb + 4, D), region(kb + 8, 2, 512)

        rows_ab, rows_cd, rows_ev, rows_fo = Rows(BIG, 2), Rows(BIG + 24, 1), Rows(BIG, 0), Rows(BIG + 48, 0)
        rows_ffn = Rows(BIG + 48, 1)
        mo_xg, mo_xgT = region(144, 2, D), region(152, KD, P)
        mo_sg, mo_h, mo_hT, mo_y = region(156, 512), region(158, 512), region(160, 4, P), region(162, 2, D)
        mo_sel, mo_F = region(170, 8, P), region(174, NT_X, NE, 4)
        mo_RK, mo_cnt = region(176, NT_X, NE), region(176.5, 8)
        mo_idxf, mo_gate = region(176.75, 2, NE + 1), region(177.25, NE)
        mo_idx = region(177.5, 2, NE + 1).bitcast(I32)
        mo_np, mo_npi = region(178, 8), region(178.125, 8).bitcast(I32)
        mo_L, mo_C8 = region(178.25, NT_X, 36), region(179, NT_X, 8)
        mo_m8, mo_ix, mo_ixf = region(179.25, NT_X, 8), region(179.5, NT_X, 8).bitcast(U32), region(179.75, NT_X, 8)
        mo_G, mo_FS, mo_t8 = region(180, NT_X, 4), region(180.25, NT_X, 8), region(180.5, NT_X, 8)
        mo_A1, mo_A2, mo_A = region(180.75, NT_X, NE), region(181.25, NT_X, NE), region(181.75, NT_X, NE)
        mo_s = region(182.25, 16, NT_X)
        mo_wr, mo_bias = region(183, KD, 36), region(184.25, 36)
        mo_before, mo_iota, mo_tok = region(184.5, 2, P), region(185.5, P), region(186, NT_X)
        mo_meta = region(186.25, NE, 4)
        mo_y12 = region(144, 2, NT_X, D)
        rows_moe = Rows(187, 0)

        def ffn_stages(f):
            return [f"{f}_in", f"{f}_out"]

        def moe_stages(m):
            return [f"r{m}_route", f"r{m}_experts", f"r{m}_norm"]

        STAGES = (["mod0", "modT0", "ab_ht", "ab_in", "ab_tr", "ab_att", "ab_pool", "ab_ot", "ab_out"]
                  + ffn_stages("f0x") + ffn_stages("f0c")
                  + ["mod1", "modT1", "cd_ht", "cd_u", "cd_conv", "cd_q", "cd_k", "cd_att", "cd_sub", "cd_ot",
                     "cd_out"] + ffn_stages("f1x")
                  + ["ev_in", "ev_tr", "ev_ret", "ev_win", "ev_ot", "ev_out"]
                  + moe_stages(0) + ["fo_dft", "fo_seq", "fo_out"] + moe_stages(1))
        if stop:
            STAGES = STAGES[:STAGES.index(stop) + 1]

        TILES_X, TILES_C = list(range(NT_C, NT)), list(range(NT_C))
        ALL = TILES_C + TILES_X

        def row(v):
            return v.partition_broadcast(P)

        def norm_rows(rows, l, n, gates=()):
            out = [(rows.gate[i], row(A["mod"][l, who, at * D:at * D + D])) for i, (who, at) in enumerate(gates)]
            sfx = "" if n[:2] == "ln" else ""
            g, b = (f"{n}_g", f"{n}_b") if not n.endswith("_2") else (n.replace("_2", "_gain_2"), n.replace("_2", "_bias_2"))
            return out + [(rows.g, row(A[g][l])), (rows.b, row(A[b][l]))]

        def mod_loads(l):
            return [(c_cols[:, 0], A["c"][0].rearrange("(k p) -> p k", p=P)),
                    (c_cols[:, 1], A["c_ctx"].rearrange("(k p) -> p k", p=P)),
                    (ada_bias, A["ada_b"][l].partition_broadcast(2))]

        def route_loads(m):
            return [(mo_wr[:, :, 0:4], A["router_coarse_w_2"][m].rearrange("(k p) n -> p k n", p=P)),
                    (mo_wr[:, :, 4:36], A["router_fine_w_2"][m].rearrange("(k p) n -> p k n", p=P)),
                    (mo_bias[:, 0:4], row(A["router_coarse_b_2"][m])), (mo_bias[:, 4:36], row(A["router_fine_b_2"][m])),
                    (mo_before, A["before"].rearrange("p (a n) -> p a n", a=2)), (mo_iota, A["iota"]),
                    (mo_tok, A["tok"])]

        LOADS = {
            "mod0": mod_loads(0), "mod1": mod_loads(1),
            "ab_in": [(qk_gain[:, 0], row(A["ab_q_gain"][0])), (qk_gain[:, 1], row(A["ab_k_gain"][0])),
                        (rope_ax, A["rope_ax"].rearrange("(t p) n -> p t n", p=P))],
            "ab_pool": [(w_pool, A["ab_w_pool"][0].rearrange("g c d -> c g d")),
                        (pool_scale, row(A["ab_pool_scale"][0]))],
            "ab_out": norm_rows(rows_ab, 0, "ln1", [(0, 2), (1, 2)]),
            "f0x_out": norm_rows(rows_ffn, 0, "ln2", [(0, 5)]),
            "f0c_out": norm_rows(rows_ffn, 0, "ln2", [(1, 5)]),
            "cd_u": [(cd_wrow[0:31], A["cd_conv_w"][0]), (cd_wrow[31:32], A["cd_conv_b"]),
                     (cd_lng, row(A["cd_conv_ln_g"][0])), (cd_lnb, row(A["cd_conv_ln_b"][0]))],
            "cd_att": [(lam_in[:, i], row(A[n][0])) for i, n in
                     enumerate(("cd_lambda_q1", "cd_lambda_k1", "cd_lambda_q2", "cd_lambda_k2"))]
            + [(sub_gain, row(A["cd_subln_gain"][0]))],
            "cd_out": norm_rows(rows_cd, 1, "ln1", [(0, 2)]),
            "f1x_out": norm_rows(rows_ffn, 1, "ln2", [(0, 5)]),
            "ev_in": [(rope_ret, A["rope_ret"].rearrange("(t p) n -> p t n", p=P)),
                        (rope_win, A["rope_win"].rearrange("(t p) n -> p t n", p=P))],
            "ev_ret": [(dist, A["dist"]), (gn_row, row(A["ret_gn_gain_2"][0])),
                       (decay[:, 0], row(A["ret_decay_logit_2"][0, 0])), (decay[:, 1], row(A["ret_decay_logit_2"][0, 1])),
                       (sinks, row(A["sink_logit_2"][0]))],
            "ev_win": [(band, A["band"])],
            "ev_out": norm_rows(rows_ev, 0, "ln1_2"),
            "fo_out": norm_rows(rows_fo, 1, "ln1_2"),
        }
        for m in range(2):
            LOADS[f"r{m}_route"] = route_loads(m) + norm_rows(rows_moe, m, "ln2_2")
            LOADS[f"r{m}_norm"] = [
                (mo_y12[:, j, t], A[f"y{m}"][j * SEQ + t * P:j * SEQ + t * P + P]) for j in range(2) for t in range(NT_X)]

        def wait_loads(eng, stage):
            eng.wait_ge(sem("loads_" + stage), 16 * len(LOADS[stage]))

        chunks, by_name = [], {}

        def add_chunk(name, parts, k, n):
            i = len(chunks)
            chunks.append(dict(parts=parts, k=k, n=n, slot=i % 5, use=i // 5 + 1, name=name))
            by_name.setdefault(name, []).append(i)

        def kpn(w, c0, c1, k0, k):
            return w[k0 * P:(k0 + k) * P, c0:c1].rearrange("(k p) n -> p k n", p=P)

        def weight_chunks(name, w, bounds, kblocks=KD):
            for c0, c1 in bounds:
                for k0 in range(0, kblocks, 8):
                    k = min(8, kblocks - k0)
                    add_chunk(name, [(0, kpn(w, c0, c1, k0, k))], k, c1 - c0)

        def ffn_chunks(f, l):
            w = A["ffn_w_in"][l]
            for j in range(0, FFN, 256):
                add_chunk(f"{f}_in", [(0, kpn(w, j, j + 256, 0, KD)), (256, kpn(w, FFN + j, FFN + j + 256, 0, KD))],
                          KD, 512)
            weight_chunks(f"{f}_out", A["ffn_w_out"][l], HALVES, KF)

        HALVES = [(0, 512), (512, 1024)]
        weight_chunks("mod0", A["ada_w"][0], [(i * 512, i * 512 + 512) for i in range(12)])
        weight_chunks("ab_in", A["ab_w_in"][0], [(0, 512), (512, 1024), (1024, 1536)])
        for i in range(2):
            add_chunk("ab_pool", [(0, A["pool_x"][:, 2 * i:2 * i + 2].rearrange("p g t n -> p (g t) n"))], 8, 512)
        add_chunk("ab_pool", [(0, A["pool_c"].rearrange("p g t n -> p (g t) n"))], 8, 256)
        weight_chunks("ab_out", A["ab_w_out"][0], HALVES)
        ffn_chunks("f0x", 0)
        ffn_chunks("f0c", 0)
        weight_chunks("mod1", A["ada_w"][1], [(i * 512, i * 512 + 512) for i in range(12)])
        cw = A["cd_w_in"][0]
        weight_chunks("cd_u", cw, [(2304, 2816)])
        weight_chunks("cd_v", cw, [(1536, 2048), (2048, 2304)])
        weight_chunks("cd_q", cw, [(0, 512), (512, 768)])
        weight_chunks("cd_k", cw, [(768, 1280), (1280, 1536)])
        weight_chunks("cd_out", A["cd_w_out"][0], HALVES)
        ffn_chunks("f1x", 1)
        weight_chunks("ev_in", A["w_in_even_2"][0], [(i * 512, min(i * 512 + 512, 2816)) for i in range(6)])
        weight_chunks("ev_out", A["w_out_even_2"][0], HALVES)
        before_experts0 = len(chunks)
        add_chunk("fo_dft", [(0, A["dft_c"])], 2, 512)
        add_chunk("fo_seq", [(0, A["dft_s"].rearrange("p s t n -> p (s t) n"))], 8, 512)
        weight_chunks("fo_out", A["w_out_fourier_2"][0], HALVES)
        chunk_read = {}
        groups = {}

        def slot(i):
            ch = chunks[i]
            return region(RING_KB[ch["slot"]], ch["k"], ch["n"])

        class Link:

            def __init__(self, eng, chain):
                self.eng, self.chain, self.n, self.at = eng, chain, {}, {}

            def __call__(self, ins, s=None, upto=None):
                s = self.chain if s is None else s
                self.n[s.name] = self.n.get(s.name, 0) + 1
                ins.then_inc(s, 1)
                self.eng.wait_ge(s, upto if upto is not None else self.at.get(s.name, 0) + self.n[s.name])

        def run(eng, steps, me=None):
            for n, name in enumerate(STAGES):
                if name in ("ab_ht", "cd_ht"):
                    eng.wait_ge(sem("mod_stored"), 16 if name == "ab_ht" else 32)
                if name in ("r0_norm", "r1_norm"):
                    eng.wait_ge(M(int(name[1]), "x_stored"), 16 * NT_X)
                if name in steps:
                    steps[name]()
                if me is not None:
                    eng.sem_inc(me, 1)
                eng.wait_ge(stage_act, n + 1)
                eng.wait_ge(stage_dve, n + 1)

        def await_read(eng, name):
            _, _, by, n = groups[name]
            eng.wait_ge(free_by[by], n)

        def tiles(t, n=1):
            return slice(t * P, (t + n) * P)

        def flat(bank, n):
            return psum[:, bank:bank + -(-n // 512), :].rearrange("p b n -> p (b n)")[:, 0:n]

        AB_UNITS = [(h, t) for h in range(12) for t in TILES_X] + [(h, t) for h in range(12) for t in TILES_C]
        CD_UNITS = [(h, t) for h in range(6) for t in range(NT_X)]
        WIN_UNITS = [(h, t) for h in range(8) for t in range(NT_X)]

        def win_keys(t):
            return [k for k in (t - 1, t, t + 1) if 0 <= k < NT_X]

        def ab_keys(t):
            return NT if t >= NT_C else NT_C

        A_, C_ = {}, {}
        for nm in ("score_full", "max_done", "exp_done", "pt_full", "pt_copied", "o_full", "o_done", "diff_done"):
            A_[nm], C_[nm] = sem("ab_" + nm), sem("cd_" + nm)

        ret_mv = region(MISC + 4.5, NT_X, 4, 2)

        def M(m, name):
            return sem(f"moe{m}_{name}")

        def more_passes(eng, m, one_pass):
            eng.wait_ge(stage_dve, STAGES.index(f"r{m}_experts"))
            n = eng.value_load(mo_npi[0:1, 0:1], min_val=1, max_val=NT_X)
            with eng.If(n > 1):
                with eng.Fori(1, n) as p:
                    one_pass(p)

        block = ctx.enter_context(nc.Block())

        @block.tensor
        def _(pe):
            state = dict(g=0, bank=0, mid=0, x_normed=0)
            read_n = {"act": 0, "dve": 0}
            last_group = [None] * 8

            def open_group(name, nb=1, by="dve"):
                if state["bank"] + nb > 8:
                    state["bank"] = 0
                b = state["bank"]
                state["bank"] = (b + nb) % 8
                for reader, s in free_by.items():
                    before = [g[1] for g in last_group[b:b + nb] if g and g[0] == reader]
                    if before:
                        pe.wait_ge(s, max(before))
                read_n[by] += 1
                for i in range(b, b + nb):
                    last_group[i] = (by, read_n[by])
                groups[name] = (state["g"], b, by, read_n[by])
                state["g"] += 1
                return b

            def close(ins):
                ins.then_inc(psum_full, 1)
                return ins

            def await_chunk(i):
                pe.wait_ge(w_ready[chunks[i]["slot"]], 16 * sum(
                    len(c["parts"]) for c in chunks[:i + 1] if c["slot"] == chunks[i]["slot"]))

            def read_group(name):
                await_read(pe, name)

            def await_x(n=1):
                state["x_normed"] += n
                pe.wait_ge(x_normed, state["x_normed"])

            def one_product(name, c, i, t, lhs, by):
                w, k, n = slot(i), chunks[i]["k"], chunks[i]["n"]
                b = open_group((name, c, t), 1, by)
                for kk in range(k):
                    ins = nc.tensor.matmul(psum[:, b, 0:n], lhs(t, kk), w[:, kk, :],
                                           start=kk == 0, stop=kk == k - 1)
                close(ins)

            def products(name, tl, lhs, by="dve"):
                for c, i in enumerate(by_name[name]):
                    await_chunk(i)
                    for t in tl:
                        one_product(name, c, i, t, lhs, by)
                    chunk_read[i] = (psum_full, state["g"])

            def tile_products(name, tl, lhs, by="dve", then=None):
                ids = by_name[name]
                for j, t in enumerate(tl):
                    for c, i in enumerate(ids):
                        if j == 0:
                            await_chunk(i)
                        one_product(name, c, i, t, lhs, by)
                        if j == len(tl) - 1:
                            chunk_read[i] = (psum_full, state["g"])
                    if then and j:
                        then(tl[j - 1])
                if then:
                    then(tl[-1])

            def turn_x(name):
                def then(t):
                    await_x()
                    if name:
                        transposes(name, [t], lambda t, k: X[:, t, tiles(k)], KD)
                return then

            def transposes(name, tl, src, n, per=8):
                for t in tl:
                    b = open_group((name, t), -(-n // 4))
                    for k in range(n):
                        ins = nc.tensor.transpose(flat(b, n * P)[:, tiles(k)], src(t, k), ident)
                    close(ins)

            def mod(l):
                def go():
                    pe.wait_ge(gate_ready := sem("c_ready"), l + 1)
                    for c, i in enumerate(by_name[f"mod{l}"]):
                        await_chunk(i)
                        b = open_group(("mod", l, c))
                        for k in range(KD):
                            ins = nc.tensor.matmul(psum[0:2, b, :], c_silu[:, k], slot(i)[:, k],
                                                   start=k == 0, stop=k == KD - 1)
                        close(ins)
                        chunk_read[i] = (psum_full, state["g"])
                return go

            def mod_t(l):
                def go():
                    b = open_group(("modT", l))
                    for j in range(48):
                        ins = nc.tensor.transpose(psum[:, b, 2 * j:2 * j + 2], mod_rows[:, tiles(j)], ident[0:2, 0:2])
                    close(ins)
                return go

            def gated(name, w_cols, ntok, col0):
                for c, i in enumerate(by_name[name]):
                    await_chunk(i)
                    w = slot(i)
                    for j in range(2):
                        b = open_group((name, 2 * c + j), 2)
                        for part in range(2):
                            for k in range(KD):
                                ins = nc.tensor.matmul(psum[:, b + part, 0:ntok],
                                                       w[:, k, part * 256 + j * P:part * 256 + j * P + P],
                                                       HT[:, k, col0:col0 + ntok], start=k == 0, stop=k == KD - 1)
                        close(ins)
                    chunk_read[i] = (psum_full, state["g"])

            def summed(name, tl, then):
                ids = by_name[name]
                per = len(ids) // 2
                for half in range(2):
                    banks = {t: open_group((name, half, t)) for t in tl}
                    k0 = 0
                    for j in range(per):
                        i = ids[half * per + j]
                        await_chunk(i)
                        w, k = slot(i), chunks[i]["k"]
                        for t in tl:
                            for kk in range(k):
                                ins = nc.tensor.matmul(psum[:, banks[t], :], ffn_hT[:, k0 + kk, tiles(t - tl[0])],
                                                       w[:, kk, :], start=k0 + kk == 0, stop=k0 + kk == KF - 1)
                            if j == per - 1:
                                close(ins)
                        if j == per - 1:
                            chunk_read[i] = (psum_full, state["g"])
                        else:
                            ins.then_inc(w_used, 1)
                            state["mid"] += 1
                            chunk_read[i] = (w_used, state["mid"])
                        k0 += k
                for t in tl:
                    then(t)

            def ffn(f, tl, following=None):
                return {
                    f"{f}_in": lambda: gated(f"{f}_in", None, len(tl) * P, tl[0] * P),
                    f"{f}_out": lambda: summed(f"{f}_out", tl, turn_x(following)),
                }

            def ab_tr():
                transposes("ab_q", ALL, lambda t, k: ab_qk[:, t, tiles(k)], 6)
                transposes("ab_k", ALL, lambda t, k: ab_kd[:, t, tiles(k)], 4)

            def ab_att():
                s, n = A_, len(AB_UNITS)

                def scores(u):
                    if u >= n:
                        return
                    h, t = AB_UNITS[u]
                    kv, nk = h // 3, ab_keys(t) * P
                    if u >= 2:
                        pe.wait_ge(s["exp_done"], u - 1)
                    for c0 in range(0, nk, 512):
                        c1 = min(c0 + 512, nk)
                        ins = nc.tensor.matmul(flat(2 * (u % 2), nk)[:, c0:c1], ab_qT[:, h // 2, tiles(t)],
                                               ab_kT[:, kv, h % 2, c0:c1], start=True, stop=True)
                    ins.then_inc(s["score_full"], 1)

                scores(0)
                scores(1)
                for u, (h, t) in enumerate(AB_UNITS):
                    nk = ab_keys(t)
                    pe.wait_ge(s["exp_done"], u + 1)
                    if u >= 1:
                        pe.wait_ge(s["pt_copied"], u)
                    for k in range(nk):
                        ins = nc.tensor.transpose(flat(4, 768)[:, tiles(k)], att_P[:, u % 2, tiles(k)], ident)
                    ins.then_inc(s["pt_full"], 1)
                    scores(u + 2)
                    pe.wait_ge(s["pt_copied"], u + 1)
                    if u >= 2:
                        pe.wait_ge(s["o_done"], u - 1)
                    for k in range(nk):
                        ins = nc.tensor.matmul(psum[:, 6 + u % 2, 0:HD], att_PT[:, u % 2, tiles(k)],
                                               ab_vu[:, k, HD * (h // 3):HD * (h // 3) + HD],
                                               start=k == 0, stop=k == nk - 1)
                    ins.then_inc(s["o_full"], 1)

            def ab_pool():
                wait_loads(pe, "ab_pool")
                ids = by_name["ab_pool"]
                for who, tl, cs in (("x", TILES_X, ids[:2]), ("c", TILES_C, ids[2:])):
                    nt = len(tl)
                    for g in range(4):
                        i = cs[g * len(cs) // 4]
                        if g % (4 // len(cs)) == 0:
                            await_chunk(i)
                        b = open_group(("pooled", who, g))
                        for kt in range(nt):
                            ins = nc.tensor.matmul(psum[0:64, b, 0:nt * P],
                                                   ab_vu[:, tl[0] + kt, 256 + g * 64:320 + g * 64],
                                                   slot(i)[:, (g % (4 // len(cs))) * nt + kt, :],
                                                   start=kt == 0, stop=kt == nt - 1)
                        close(ins)
                        chunk_read[i] = (psum_full, state["g"])
                    for g in range(4):
                        read_group(("pooled", who, g))
                    for t in tl:
                        b = open_group(("mixed", t))
                        for g in range(4):
                            ins = nc.tensor.matmul(psum[:, b, g * 64:g * 64 + 64], pooledT[:, g, tiles(t - tl[0])],
                                                   w_pool[:, g], start=True, stop=True)
                        close(ins)

            def cd_u():
                wait_loads(pe, "cd_u")
                b = open_group("conv_w")
                for j in range(2):
                    ins = nc.tensor.transpose(psum[:, b, 32 * j:32 * j + 32], cd_wrow[:, tiles(j)], ident[0:32, 0:32])
                close(ins)
                gated("cd_u", None, SEQ, NT_C * P)

            def cd_conv_v():
                products("cd_v", ALL, lambda t, k: HT[:, k, tiles(t)], "act")
                pe.wait_ge(sem("conv_done"), 1)
                for t in range(NT_X):
                    b = open_group(("conv", t))
                    for j in range(2):
                        ins = nc.tensor.transpose(psum[:, b, tiles(j)], cd_acc[:, j, tiles(t)], ident)
                    close(ins)

            def cd_att():
                s, n = C_, 2 * len(CD_UNITS)
                NK = NT * P

                def scores(v):
                    if v >= n:
                        return
                    h, t = CD_UNITS[v // 2]
                    if v >= 2:
                        pe.wait_ge(s["exp_done"], v - 1)
                    for c0 in range(0, NK, 512):
                        c1 = min(c0 + 512, NK)
                        ins = nc.tensor.matmul(flat(2 * (v % 2), NK)[:, c0:c1], cd_qT[:, h, v % 2, tiles(t)],
                                               cd_kT[:, h, c0:c1], start=True, stop=True)
                    ins.then_inc(s["score_full"], 1)

                scores(0)
                scores(1)
                for u, (h, t) in enumerate(CD_UNITS):
                    pe.wait_ge(s["diff_done"], u + 1)
                    if u >= 1:
                        pe.wait_ge(s["pt_copied"], u)
                    for k in range(NT):
                        ins = nc.tensor.transpose(flat(4, 768)[:, tiles(k)], cd_P[:, 2 * u % 4, tiles(k)], ident)
                    ins.then_inc(s["pt_full"], 1)
                    scores(2 * u + 2)
                    pe.wait_ge(s["pt_copied"], u + 1)
                    if u >= 2:
                        pe.wait_ge(s["o_done"], u - 1)
                    for k in range(NT):
                        ins = nc.tensor.matmul(psum[:, 6 + u % 2, 0:P], cd_PT[:, u % 2, tiles(k)],
                                               cd_v[:, k, tiles(h)], start=k == 0, stop=k == NT - 1)
                    ins.then_inc(s["o_full"], 1)
                    scores(2 * u + 3)

            def ev_tr():
                R = range(NT_X)
                transposes("ev_qa", R, lambda t, k: ev_qa[:, t, tiles(k)], 4)
                transposes("ev_ka", R, lambda t, k: ev_ka[:, t, tiles(k)], 4)
                transposes("ev_qb", R, lambda t, k: ev_qb[:, t, tiles(k)], 4)
                transposes("ev_kb", R, lambda t, k: ev_kbd[:, t, tiles(k)], 2)

            def ev_ret():
                for h in range(4):
                    for mt in range(NT_X):
                        b = open_group(("ret_s", h, mt))
                        close(nc.tensor.matmul(psum[:, b, :], ev_kaT[:, h, tiles(mt)], ev_qaT[:, h, :],
                                               start=True, stop=True))
                    read_group(("ret_s", h, NT_X - 1))
                    for t in range(NT_X):
                        b = open_group(("ret_y", h, t))
                        for mt in range(NT_X):
                            ins = nc.tensor.matmul(psum[:, b, 0:P], ev_ST[:, mt, tiles(t)], ev_va[:, mt, tiles(h)],
                                                   start=mt == 0, stop=mt == NT_X - 1)
                        close(ins)

            def ev_win():
                def scores(u):
                    if u >= len(WIN_UNITS):
                        return
                    h, t = WIN_UNITS[u]
                    ks, lo = win_keys(t), 64 * (h % 2)
                    b = open_group(("win_s", u))
                    close(nc.tensor.matmul(psum[:, b, 0:len(ks) * P], ev_qbT[lo:lo + 64, h // 2, tiles(t)],
                                           ev_kbT[lo:lo + 64, h // 4, tiles(ks[0], len(ks))], start=True, stop=True))

                scores(0)
                for u, (h, t) in enumerate(WIN_UNITS):
                    ks = win_keys(t)
                    scores(u + 1)
                    pe.wait_ge(sem("win_exp_done"), u + 1)
                    b = open_group(("win_pt", u))
                    for k in range(len(ks)):
                        ins = nc.tensor.transpose(psum[:, b, tiles(k)], ev_P[:, u % 2, tiles(k)], ident)
                    close(ins)
                    read_group(("win_pt", u))
                    b = open_group(("win_o", u))
                    for k, kt in enumerate(ks):
                        ins = nc.tensor.matmul(psum[:, b, 0:HD], ev_PT[:, u % 2, tiles(k)],
                                               ev_kv[:, kt, P + HD * (h // 4):P + HD * (h // 4) + HD],
                                               start=k == 0, stop=k == len(ks) - 1)
                    close(ins)

            def fo_dft():
                i = by_name["fo_dft"][0]
                await_chunk(i)
                for t in range(NT_X):
                    for g in range(4):
                        b = open_group(("fo_dft", t, g), 1, "act")
                        for k in range(2):
                            ins = nc.tensor.matmul(psum[:, b, :], HT[:, 2 * g + k, tiles(NT_C + t)], slot(i)[:, k],
                                                   start=k == 0, stop=k == 1)
                        close(ins)
                chunk_read[i] = (psum_full, state["g"])

            def fo_seq():
                i = by_name["fo_seq"][0]
                await_chunk(i)
                for d in range(KD):
                    b = open_group(("fo_seq", d), 1, "act")
                    for part in range(2):
                        for t in range(NT_X):
                            ins = nc.tensor.matmul(
                                psum[:, b, :], fo_AB[:, t, d // 2, part * 256 + (d % 2) * P:part * 256 + (d % 2) * P + P],
                                slot(i)[:, part * NT_X + t], start=part + t == 0, stop=part + t == NT_X)
                    close(ins)
                chunk_read[i] = (psum_full, state["g"])

            def route(m):
                def go():
                    wait_loads(pe, f"r{m}_route")
                    b = open_group(("logits", m))
                    for t in range(NT_X):
                        for k in range(KD):
                            ins = nc.tensor.matmul(psum[:, b, 36 * t:36 * t + 36], HT[:, k, tiles(NT_C + t)],
                                                   mo_wr[:, k], start=k == 0, stop=k == KD - 1)
                    close(ins)
                    pe.wait_ge(M(m, "picked"), 1)
                    b = open_group(("rank", m))
                    for t in range(NT_X):
                        for s in range(t + 1):
                            ins = nc.tensor.matmul(psum[:, b, NE * t:NE * t + NE], mo_before[:, int(s < t)],
                                                   mo_A[:, s], start=s == 0, stop=s == t)
                    for s in range(NT_X):
                        ins = nc.tensor.matmul(psum[:, b, NE * NT_X:NE * NT_X + NE], mo_before[:, 1], mo_A[:, s],
                                               start=s == 0, stop=s == NT_X - 1)
                    close(ins)
                return go

            def experts(m):
                def one_pass(p):
                    for e in range(NE):
                        pe.wait_ge(M(m, "sel_ready"), NE * p + e + 1)
                        for t in range(NT_X):
                            ins = nc.tensor.matmul(psum[:, 7, 4 * e:4 * e + 4], mo_sel[:, 4 * (e % 2) + t],
                                                   mo_F[:, t, e], start=t == 0, stop=t == NT_X - 1)
                        ins.then_inc(M(m, "sel_used"), 1)

                    def turn_x(xg_n, b):
                        pe.wait_ge(M(m, f"xg_ready{b}"), xg_n * 16)
                        for k in range(KD):
                            ins = nc.tensor.transpose(flat(2, D)[:, tiles(k)], mo_xg[:, b, tiles(k)], ident)
                        ins.then_inc(M(m, "xt_full"), 1)

                    turn_x(17 * p + 1, 0)
                    with pe.Fori(0, NE // 2) as i:
                        for b in range(2):
                            e = NE * p + i * 2 + b
                            pe.wait_ge(M(m, "xgT_ready"), (NE + 1) * p + i * 2 + b + 1)
                            pe.wait_ge(M(m, "gu_free"), e + 1)
                            for part in range(2):
                                w = region(MOE_RING_KB[3 * b + part], KD, 512)
                                pe.wait_ge(M(m, f"w_ready{3 * b + part}"), ((NE // 2) * p + i + 1) * 16)
                                for k in range(KD):
                                    ins = nc.tensor.matmul(psum[:, part, :], mo_xgT[:, k], w[:, k],
                                                           start=k == 0, stop=k == KD - 1)
                            ins.then_inc(M(m, "gu_full"), 1)
                            turn_x((17 * p + i + 2) if b == 1 else (16 * p + i + 1), 1 - b)
                            pe.wait_ge(M(m, "h_ready"), e + 1)
                            for k in range(4):
                                ins = nc.tensor.transpose(psum[:, 4, tiles(k)], mo_h[:, tiles(k)], ident)
                            ins.then_inc(M(m, "ht_full"), 1)
                            pe.wait_ge(M(m, "hT_ready"), e + 1)
                            pe.wait_ge(M(m, "y_free"), e + 1)
                            pe.wait_ge(M(m, f"w_ready{3 * b + 2}"), ((NE // 2) * p + i + 1) * 16)
                            w = region(MOE_RING_KB[3 * b + 2], 4, D)
                            for half in range(2):
                                for k in range(4):
                                    ins = nc.tensor.matmul(psum[:, 5 + half, :], mo_hT[:, k],
                                                           w[:, k, half * 512:half * 512 + 512],
                                                           start=k == 0, stop=k == 3)
                            ins.then_inc(M(m, "y_full"), 1)

                def go():
                    one_pass(0)
                    more_passes(pe, m, one_pass)
                return go

            def heads(name, t0):
                def then(t):
                    pe.wait_ge(sem(name + "_roped"), 1 + t - t0)
                    transposes(name, [t], lambda t, k: cd_tmp[:, t % 4, tiles(k)], 6)
                return then

            steps = {
                "mod0": mod(0), "modT0": mod_t(0), "mod1": mod(1), "modT1": mod_t(1),
                "ab_ht": lambda: transposes("ab_ht", ALL, lambda t, k: X[:, t, tiles(k)], KD),
                "ab_in": lambda: tile_products("ab_in", ALL, lambda t, k: HT[:, k, tiles(t)], "act"),
                "ab_tr": ab_tr, "ab_att": ab_att, "ab_pool": ab_pool,
                "ab_ot": lambda: transposes("ab_ot", ALL, lambda t, k: O_all[:, t, tiles(k)], KD),
                "ab_out": lambda: tile_products("ab_out", ALL, lambda t, k: OT_ab[:, k, tiles(t)], "dve",
                                                turn_x("ab_out_t")),
                **ffn("f0x", TILES_X), **ffn("f0c", TILES_C), **ffn("f1x", TILES_X, "f1x_out_t"),
                "cd_ht": lambda: transposes("cd_ht", ALL, lambda t, k: X[:, t, tiles(k)], KD),
                "cd_u": cd_u, "cd_conv": cd_conv_v,
                "cd_q": lambda: tile_products("cd_q", TILES_X, lambda t, k: HT[:, k, tiles(t)], "act",
                                              heads("cd_qt", NT_C)),
                "cd_k": lambda: tile_products("cd_k", ALL, lambda t, k: HT[:, k, tiles(t)], "act",
                                              heads("cd_kt", 0)),
                "cd_att": cd_att,
                "cd_ot": lambda: transposes("cd_ot", TILES_X, lambda t, k: O4[:, t - NT_C, tiles(k)], KD),
                "cd_out": lambda: tile_products("cd_out", TILES_X, lambda t, k: OT_cd[:, k, tiles(t - NT_C)], "dve",
                                                turn_x("cd_out_t")),
                "ev_in": lambda: products("ev_in", TILES_X, lambda t, k: HT[:, k, tiles(t)], "act"),
                "ev_tr": ev_tr, "ev_ret": ev_ret, "ev_win": ev_win,
                "ev_ot": lambda: transposes("ev_ot", TILES_X, lambda t, k: O4[:, t - NT_C, tiles(k)], KD),
                "ev_out": lambda: tile_products("ev_out", TILES_X, lambda t, k: OT_ev[:, k, tiles(t - NT_C)], "dve",
                                                turn_x("ev_out_t")),
                "fo_dft": fo_dft, "fo_seq": fo_seq,
                "fo_out": lambda: tile_products("fo_out", TILES_X, lambda t, k: fo_YT[:, k, tiles(t - NT_C)], "dve",
                                                turn_x("fo_out_t")),
                "r0_norm": lambda: [turn_x("r0_norm_t")(t) for t in TILES_X],
                "r1_norm": lambda: [turn_x(None)(t) for t in TILES_X],
            }
            for m in range(2):
                steps[f"r{m}_route"] = route(m)
                steps[f"r{m}_experts"] = experts(m)
            pe.wait_ge(sem("ident_loaded"), 16)
            pe.wait_ge(sem("x_loaded"), 16 * NT)
            run(pe, steps)

        @block.scalar
        def _(act):
            link = Link(act, act_chain)

            free = free_by["act"]

            def await_group(name):
                act.wait_ge(psum_full, groups[name][0] + 1)
                return groups[name][3], groups[name][1]

            def take(name, dst, n):
                g, b = await_group(name)
                src = flat(b, n)
                if len(dst.shape) == 3:
                    src = src.rearrange("p (a c) -> p a c", a=dst.shape[1])
                link(nc.scalar.activation(dst, src, ACT.Copy), free, g)

            def roots(n, times=1):
                def go():
                    for _ in range(times):
                        k = link.n.get("sqrt_done", 0)
                        act.wait_ge(stat_ready, k + 1)
                        v = n if not callable(n) else n()
                        link(nc.scalar.activation(v, v, ACT.Sqrt), sqrt_done)
                return go

            def mod(l):
                def go():
                    wait_loads(act, f"mod{l}")
                    for who in range(2):
                        link(nc.scalar.activation(c_silu[:, :, who], c_cols[:, who], ACT.Silu),
                             None if who == 0 else sem("c_ready"))
                return go

            def gate(name, func, sg, ntok, n):
                def go():
                    for j in range(n):
                        g, b = await_group((name, j))
                        if j >= 2:
                            await_read(act, (name, j - 2))
                        link(nc.scalar.activation(sg[:, j % 2, 0:ntok], psum[:, b + 1, 0:ntok], func), gate_done)
                return go

            def ab_in():
                for t in ALL:
                    for c in range(3):
                        take(("ab_in", c, t), ab_qk[:, t, 512 * c:512 * c + 512] if c < 2 else ab_vu[:, t], 512)
                    roots(rstd[:, t])()

            def ab_att():
                s = A_

                def exps(u):
                    if u >= len(AB_UNITS):
                        return
                    n = ab_keys(AB_UNITS[u][1]) * P
                    act.wait_ge(s["max_done"], u + 1)
                    link(nc.scalar.activation(att_P[:, u % 2, 0:n], flat(2 * (u % 2), n), ACT.Exp,
                                              bias=nmx[:, u % 4:u % 4 + 1], scale=HD ** -0.5,
                                              accum_out=esum[:, u % 4:u % 4 + 1]), s["exp_done"])

                exps(0)
                exps(1)
                for u, (h, t) in enumerate(AB_UNITS):
                    n = ab_keys(t) * P
                    act.wait_ge(s["pt_full"], u + 1)
                    link(nc.scalar.activation(att_PT[:, u % 2, 0:n], flat(4, n), ACT.Copy), s["pt_copied"])
                    exps(u + 2)

            def cd_att():
                s, n = C_, NT * P
                for i in range(2):
                    act.wait_ge(sem("lam_sum"), i + 1)
                    link(nc.scalar.activation(lam[:, i:i + 1], lam[:, i:i + 1], ACT.Exp), sem("lam_exp"))

                def exps(v):
                    if v >= 2 * len(CD_UNITS):
                        return
                    act.wait_ge(s["max_done"], v + 1)
                    link(nc.scalar.activation(cd_P[:, v % 4], flat(2 * (v % 2), n), ACT.Exp,
                                              bias=nmx[:, v % 8:v % 8 + 1], scale=HD ** -0.5,
                                              accum_out=esum[:, v % 8:v % 8 + 1]), s["exp_done"])

                exps(0)
                exps(1)
                for u in range(len(CD_UNITS)):
                    act.wait_ge(s["pt_full"], u + 1)
                    link(nc.scalar.activation(cd_PT[:, u % 2], flat(4, n), ACT.Copy), s["pt_copied"])
                    exps(2 * u + 2)
                    exps(2 * u + 3)

            def cd_conv_():
                for c, w in enumerate((512, 256)):
                    for t in ALL:
                        take(("cd_v", c, t), cd_v[:, t, 512 * c:512 * c + w], w)
                roots(rstd[:, 0:NT_X, 0])()
                act.wait_ge(sem("conv_normed"), 1)
                link(nc.scalar.activation(cd_conv, cd_conv, ACT.Silu))

            def cd_proj(name, tl, turned):
                def go():
                    for t in tl:
                        if t - tl[0] >= 4:
                            act.wait_ge(psum_full, groups[(turned, t - 4)][0] + 1)
                        for c, w in enumerate((512, 256)):
                            take((name, c, t), cd_tmp[:, t % 4, 512 * c:512 * c + w], w)
                return go

            def ev_in():
                for c, d in enumerate((ev_qa, ev_ka, ev_va, ev_ga, ev_qb, ev_kv)):
                    for t in range(NT_X):
                        take(("ev_in", c, NT_C + t), d[:, t], 512 if c < 5 else 256)

            def ev_ret():
                act.wait_ge(sem("decay_abs"), 1)
                link(nc.scalar.activation(lg[:, 1], lg[:, 0], ACT.Exp, scale=-1.0), sem("decay_exp"))
                for h in range(4):
                    act.wait_ge(sem("decay_arg"), h + 1)
                    link(nc.scalar.activation(ev_D, ev_D, ACT.Exp), sem("decay_done"))
                roots(rstd[:, 0:NT_X, 0:4])()
                link(nc.scalar.activation(ev_ga, ev_ga, ACT.Silu), sem("ret_gate"))

            def ev_win():
                for u, (h, t) in enumerate(WIN_UNITS):
                    n = len(win_keys(t)) * P
                    act.wait_ge(sem("win_max_done"), u + 1)
                    link(nc.scalar.activation(ev_P[:, u % 2, 0:n], ev_Sm[:, u % 2, 0:n], ACT.Exp,
                                              bias=nmx[:, u % 4:u % 4 + 1], accum_out=esum[:, u % 4:u % 4 + 1]))
                    link(nc.scalar.activation(esum[:, 4 + u % 4:5 + u % 4], ev_Sm[:, u % 2, n:n + 1], ACT.Exp,
                                              bias=nmx[:, u % 4:u % 4 + 1]), sem("win_exp_done"))

            def fo_dft():
                for t in range(NT_X):
                    for g in range(4):
                        take(("fo_dft", t, g), fo_AB[:, t, g], 512)

            def fo_seq():
                for d in range(KD):
                    take(("fo_seq", d), fo_YT[:, d], 512)

            def route(m):
                def go():
                    act.wait_ge(M(m, "coarse_shifted"), 1)
                    link(nc.scalar.activation(mo_C8[:, :, 0:4], mo_C8[:, :, 0:4], ACT.Exp), M(m, "coarse_exp"))
                    act.wait_ge(M(m, "fine_diff"), 1)
                    link(nc.scalar.activation(mo_s[:, 3], mo_s[:, 2], ACT.Exp), M(m, "fine_exp"))
                return go

            def experts(m):
                chain = Link(act, M(m, "act_chain"))

                def one_pass(p):
                    def turned_x():
                        chain(nc.scalar.activation(mo_xgT, flat(2, D).rearrange("p (a c) -> p a c", a=KD), ACT.Copy),
                              M(m, "xgT_ready"))

                    chain.n = {}
                    chain.at = {M(m, "xgT_ready").name: p * (NE + 1)}
                    act.wait_ge(M(m, "xt_full"), p * (NE + 1) + 1)
                    turned_x()
                    with act.Fori(0, NE // 2) as i:
                        chain.n = {}
                        chain.at = {M(m, "xgT_ready").name: p * (NE + 1) + i * 2 + 1,
                                    M(m, "sg_done").name: p * NE + i * 2, M(m, "hT_ready").name: p * NE + i * 2}
                        for b in range(2):
                            e = p * NE + i * 2 + b
                            act.wait_ge(M(m, "gu_full"), e + 1)
                            chain(nc.scalar.activation(mo_sg, psum[:, 0, :], ACT.Silu), M(m, "sg_done"))
                            act.wait_ge(M(m, "xt_full"), p * (NE + 1) + i * 2 + b + 2)
                            turned_x()
                            act.wait_ge(M(m, "ht_full"), e + 1)
                            chain(nc.scalar.activation(mo_hT, psum[:, 4, :].rearrange("p (a c) -> p a c", a=4),
                                                       ACT.Copy), M(m, "hT_ready"))

                def go():
                    one_pass(0)
                    more_passes(act, m, one_pass)
                return go

            def norms(tl):
                def go():
                    for j in range(len(tl)):
                        roots(rstd[:, j, 0:1])()
                return go

            steps = {
                "mod0": mod(0), "mod1": mod(1), "ab_in": ab_in, "ab_att": ab_att,
                "f0x_in": gate("f0x_in", ACT.Silu, ffn_sg, SEQ, KF), "f0c_in": gate("f0c_in", ACT.Silu, ffn_sg, CTX, KF),
                "f1x_in": gate("f1x_in", ACT.Silu, ffn_sg, SEQ, KF),
                "cd_u": gate("cd_u", ACT.Sigmoid, cd_sg, SEQ, 2), "cd_conv": cd_conv_,
                "cd_q": cd_proj("cd_q", TILES_X, "cd_qt"), "cd_k": cd_proj("cd_k", ALL, "cd_kt"),
                "cd_att": cd_att, "cd_sub": roots(rstd[:, 0:NT_X, 0:6]),
                "ev_in": ev_in, "ev_ret": ev_ret, "ev_win": ev_win,
                "fo_dft": fo_dft, "fo_seq": fo_seq,
                "r0_route": route(0), "r1_route": route(1), "r0_experts": experts(0), "r1_experts": experts(1),
                "ab_out": norms(ALL), "f0x_out": norms(TILES_X), "f0c_out": norms(TILES_C), "cd_out": norms(TILES_X),
                "f1x_out": norms(TILES_X), "ev_out": norms(TILES_X), "fo_out": norms(TILES_X),
                "r0_norm": norms(TILES_X), "r1_norm": norms(TILES_X),
            }
            run(act, steps, stage_act)

        @block.vector
        def _(dve):
            link = Link(dve, dve_chain)
            V = nc.vector

            free = free_by["dve"]

            def await_group(name):
                dve.wait_ge(psum_full, groups[name][0] + 1)
                return groups[name][3], groups[name][1]

            def over(v, n):
                return v.unsqueeze(1).broadcast_to([P, n, v.shape[1]])

            def per(v, n):
                return v.unsqueeze(2).broadcast_to([P, v.shape[1], n])

            def take(name, dst, n, parts=P):
                g, b = await_group(name)
                src = flat(b, n)[0:parts]
                if len(dst.shape) == 3:
                    src = src.rearrange("p (a c) -> p a c", a=dst.shape[1])
                link(V.tensor_copy(dst, src), free, g)

            def mod(l):
                def go():
                    wait_loads(dve, f"mod{l}")
                    for c in range(12):
                        g, b = await_group(("mod", l, c))
                        link(V.tensor_tensor(mod_rows[:, 512 * c:512 * c + 512], psum[0:2, b, :],
                                             ada_bias[:, 512 * c:512 * c + 512], ALU.add), free, g)
                return go

            def mod_t(l):
                def go():
                    take(("modT", l), mod_cols, 96)
                    for k in (8, 32):
                        link(V.tensor_scalar(mod_cols[:, k:k + 8], mod_cols[:, k:k + 8], 1.0, None, ALU.add))
                return go

            def modulate(name, shift):
                def one(t):
                    g, b = await_group((name, t))
                    who = int(t < NT_C)
                    for k in range(KD):
                        ins = V.tensor_scalar(HT[:, k, tiles(t)], flat(b, D)[:, tiles(k)],
                                              mod_cols[:, shift + 8 + k, who:who + 1],
                                              mod_cols[:, shift + k, who:who + 1], ALU.mult, ALU.add)
                    link(ins, free, g)
                return one

            def modulated(name, tl, shift):
                return lambda: [modulate(name, shift)(t) for t in tl]

            def copied(name):
                return lambda t: take((name, t), HT[:, :, tiles(t)], D)

            def plain(name, tl, dst, n, t0=0):
                def go():
                    for t in tl:
                        take((name, t), dst[:, :, tiles(t - t0)], n)
                return go

            def root_of(v, count, eps, src=None):
                link(V.tensor_scalar(v, v if src is None else src, 1.0 / count, eps, ALU.mult, ALU.add), stat_ready)
                dve.wait_ge(sqrt_done, link.n["stat_ready"])
                link(V.reciprocal(v, v))

            def statistics(src, slot_, n):
                for j in range(-(-n // 512)):
                    link(V.bn_stats(stat[:, slot_, j], src[:, 512 * j:min(512 * j + 512, n)]))
                link(V.bn_aggr(mv[:, slot_], stat[:, slot_, 0:-(-n // 512)]))

            def norm_tile(j, t, rows, eps):
                statistics(X[:, t], j, D)
                root_of(rstd[:, j, 0:1], 1.0, eps, mv[:, j, 1:2])
                link(V.tensor_scalar(X[:, t], X[:, t], mv[:, j, 0:1], rstd[:, j, 0:1], ALU.subtract, ALU.mult))
                link(V.tensor_tensor(X[:, t], X[:, t], rows.g, ALU.mult))
                link(V.tensor_tensor(X[:, t], X[:, t], rows.b, ALU.add), x_normed)

            def out_norm(name, tl, rows, eps, gates, by_tile, following=None):
                def residual(half, t, n):
                    g, b = await_group((name, half, t))
                    cols = slice(512 * half, 512 * half + 512)
                    if gates:
                        row_ = rows.gate[len(rows.gate) - 1 if t < NT_C else 0]
                        link(V.tensor_tensor(rows.tmp[:, n % 2], psum[:, b, :], row_[:, cols], ALU.mult), free, g)
                        link(V.scalar_tensor_tensor(X[:, t, cols], X[:, t, cols], ALPHA, rows.tmp[:, n % 2],
                                                    ALU.mult, ALU.add))
                    else:
                        link(V.scalar_tensor_tensor(X[:, t, cols], X[:, t, cols], ALPHA, psum[:, b, :],
                                                    ALU.mult, ALU.add), free, g)

                def go():
                    wait_loads(dve, name)
                    if not by_tile:
                        for j, t in enumerate(tl):
                            residual(0, t, j)
                    for j, t in enumerate(tl):
                        if by_tile:
                            residual(0, t, 0)
                        residual(1, t, 1)
                        norm_tile(j, t, rows, eps)
                        if following and by_tile and j:
                            following(tl[j - 1])
                    if following:
                        for t in tl[-1:] if by_tile else tl:
                            following(t)
                return go

            def product(f, n_tok):
                def go():
                    for j in range(KF):
                        g, b = await_group((f"{f}_in", j))
                        dve.wait_ge(gate_done, gate_base[f] + j + 1)
                        link(V.tensor_tensor(ffn_hT[:, j, 0:n_tok], psum[:, b, 0:n_tok], ffn_sg[:, j % 2, 0:n_tok],
                                             ALU.mult), free, g)
                return go

            gate_base = dict(f0x=0, f0c=KF, cd_u=2 * KF, f1x=2 * KF + 2)

            def rotate(x, table, heads, axes, half, ta, tb, signal=None):
                w = axes * 2 * half
                n = heads * w
                cos, sin = table[:, 0:w], table[:, w:2 * w]
                x3 = x.rearrange("p (h w) -> p h w", w=w)
                a3, b3 = (v[:, 0:n].rearrange("p (h w) -> p h w", w=w) for v in (ta, tb))
                link(V.tensor_tensor(a3, x3, over(cos, heads), ALU.mult))
                for ax in range(axes):
                    for s in range(2):
                        at = ax * 2 * half + s * half
                        of = ax * 2 * half + (1 - s) * half
                        link(V.tensor_tensor(b3[:, :, at:at + half], x3[:, :, of:of + half],
                                             over(sin[:, at:at + half], heads), ALU.mult))
                link(V.tensor_tensor(x, ta[:, 0:n], tb[:, 0:n], ALU.add), signal)

            def ab_rope():
                wait_loads(dve, "ab_in")
                for t in ALL:
                    await_read(dve, ("ab_in", 2, t))
                    link(V.tensor_tensor(tmp_a, ab_qk[:, t], ab_qk[:, t], ALU.mult))
                    link(V.reduce_sum(rstd[:, t], tmp_a.rearrange("p (h d) -> p h d", d=HD), axis=AX.X))
                    root_of(rstd[:, t], HD, EPS)
                    x3 = ab_qk[:, t].rearrange("p (h d) -> p h d", d=HD)
                    link(V.tensor_tensor(x3, x3, per(rstd[:, t], HD), ALU.mult))
                    link(V.tensor_tensor(x3[:, 0:12], x3[:, 0:12], over(qk_gain[:, 0], 12), ALU.mult))
                    link(V.tensor_tensor(x3[:, 12:16], x3[:, 12:16], over(qk_gain[:, 1], 4), ALU.mult))
                    if t >= NT_C:
                        rotate(ab_qk[:, t], rope_ax[:, t - NT_C], 16, 2, 16, tmp_a, tmp_b)
                    kd = ab_kd[:, t].rearrange("p (h c) -> p h c", h=4)
                    for j in range(2):
                        link(V.tensor_copy(kd[:, :, HD * j:HD * j + HD], x3[:, 12:16]))

            def two_halves(name, dst):
                g, b = await_group(name)
                src = flat(b, dst.shape[1] * P).rearrange("p (a c) -> p a c", c=P)
                link(V.tensor_copy(dst[0:64, :, 0], src[0:64]))
                link(V.tensor_copy(dst[64:128, :, 1], src[64:128]), free, g)

            def clear_others(dst):
                link(V.memset(dst[64:128, :, 0], 0.0))
                link(V.memset(dst[0:64, :, 1], 0.0))

            def ab_tr():
                for t in ALL:
                    take(("ab_q", t), ab_qT[:, :, tiles(t)], 768)
                clear_others(ab_kT)
                for t in ALL:
                    two_halves(("ab_k", t), ab_kT[:, :, :, tiles(t)])

            def max_of(s, u, m, n):
                dve.wait_ge(s["score_full"], u + 1)
                link(V.reduce_max(nmx[:, u % m:u % m + 1], flat(2 * (u % 2), n), axis=AX.X))
                link(V.tensor_scalar(nmx[:, u % m:u % m + 1], nmx[:, u % m:u % m + 1], -(HD ** -0.5), None, ALU.mult),
                     s["max_done"])

            def ab_att():
                s = A_

                def mx(u):
                    if u < len(AB_UNITS):
                        max_of(s, u, 4, ab_keys(AB_UNITS[u][1]) * P)

                mx(0)
                mx(1)
                for u, (h, t) in enumerate(AB_UNITS):
                    mx(u + 2)
                    dve.wait_ge(s["o_full"], u + 1)
                    link(V.reciprocal(rsum[:, u % 4:u % 4 + 1], esum[:, u % 4:u % 4 + 1]))
                    link(V.tensor_scalar(O_all[:, t, HD * h:HD * h + HD], psum[:, 6 + u % 2, 0:HD],
                                         rsum[:, u % 4:u % 4 + 1], None, ALU.mult), s["o_done"])

            def ab_pool():
                wait_loads(dve, "ab_pool")
                for who, tl in (("x", TILES_X), ("c", TILES_C)):
                    for g in range(4):
                        take(("pooled", who, g), pooledT[:, g, 0:len(tl) * P], len(tl) * P, 64)
                    for t in tl:
                        g, b = await_group(("mixed", t))
                        link(V.tensor_tensor(O_all[:, t, 768:1024], psum[:, b, 0:256], pool_scale, ALU.mult),
                             free, g)

            def cd_u():
                take("conv_w", cd_wcol, 64)
                link(V.memset(cd_z, 0.0))
                for j in range(2):
                    g, b = await_group(("cd_u", j))
                    dve.wait_ge(gate_done, gate_base["cd_u"] + j + 1)
                    link(V.tensor_tensor(cd_z[:, j, 15:15 + SEQ], psum[:, b, :], cd_sg[:, j], ALU.mult),
                         free, g)

            def cd_conv_():
                wait_loads(dve, "cd_u")
                for j in range(2):
                    link(V.tensor_scalar(cd_acc[:, j], cd_z[:, j, 0:SEQ], cd_wcol[:, j, 0:1], cd_wcol[:, j, 31:32],
                                         ALU.mult, ALU.add))
                    for k in range(1, 31):
                        ins = V.scalar_tensor_tensor(cd_acc[:, j], cd_z[:, j, k:k + SEQ], cd_wcol[:, j, k:k + 1],
                                                     cd_acc[:, j], ALU.mult, ALU.add)
                        link(ins, sem("conv_done") if j == 1 and k == 30 else None)
                for t in range(NT_X):
                    take(("conv", t), cd_conv[:, t], 256)
                    statistics(cd_conv[:, t], t, 256)
                link(V.tensor_copy(rstd[:, 0:NT_X, 0], mv[:, 0:NT_X, 1]))
                root_of(rstd[:, 0:NT_X, 0], 1.0, EPS)
                for t in range(NT_X):
                    link(V.tensor_scalar(cd_conv[:, t], cd_conv[:, t], mv[:, t, 0:1], rstd[:, t, 0:1],
                                         ALU.subtract, ALU.mult))
                    link(V.tensor_tensor(cd_conv[:, t], cd_conv[:, t], cd_lng, ALU.mult))
                    link(V.tensor_tensor(cd_conv[:, t], cd_conv[:, t], cd_lnb, ALU.add),
                         sem("conv_normed") if t == NT_X - 1 else None)

            def cd_heads(name, turned, tl, put):
                def go():
                    if name == "cd_q":
                        clear_others(cd_qT)
                    for j, t in enumerate(tl):
                        await_read(dve, (name, 1, t))
                        if t >= NT_C:
                            for part in range(2):
                                rotate(cd_tmp[:, t % 4, 384 * part:384 * part + 384], rope_ax[:, t - NT_C], 6, 2, 16,
                                       cd_ta, cd_tb, sem(turned + "_roped") if part else None)
                        else:
                            dve.sem_inc(sem(turned + "_roped"), 1)
                        if j:
                            put(tl[j - 1])
                    put(tl[-1])
                return go

            def cd_att():
                wait_loads(dve, "cd_att")
                for i in range(2):
                    link(V.tensor_tensor(lam_in[:, 2 * i], lam_in[:, 2 * i], lam_in[:, 2 * i + 1], ALU.mult))
                    link(V.reduce_sum(lam[:, i:i + 1], lam_in[:, 2 * i], axis=AX.X), sem("lam_sum"))
                dve.wait_ge(sem("lam_exp"), 2)
                link(V.tensor_tensor(lam[:, 2:3], lam[:, 1:2], lam[:, 0:1], ALU.subtract))
                link(V.tensor_scalar(lam[:, 2:3], lam[:, 2:3], -LAM_INIT, None, ALU.add))
                s, n = C_, 2 * len(CD_UNITS)

                def mx(v):
                    if v < n:
                        max_of(s, v, 8, NT * P)

                mx(0)
                mx(1)
                for u, (h, t) in enumerate(CD_UNITS):
                    v = 2 * u
                    dve.wait_ge(s["exp_done"], v + 2)
                    a = v % 8
                    link(V.reciprocal(rsum[:, a:a + 2], esum[:, a:a + 2]))
                    link(V.tensor_tensor(rsum[:, a + 1:a + 2], rsum[:, a + 1:a + 2], lam[:, 2:3], ALU.mult))
                    link(V.tensor_scalar(cd_P[:, v % 4], cd_P[:, v % 4], rsum[:, a:a + 1], None, ALU.mult))
                    link(V.scalar_tensor_tensor(cd_P[:, v % 4], cd_P[:, v % 4 + 1], rsum[:, a + 1:a + 2], cd_P[:, v % 4],
                                                ALU.mult, ALU.add), s["diff_done"])
                    mx(v + 2)
                    dve.wait_ge(s["o_full"], u + 1)
                    link(V.tensor_copy(O4[:, t, tiles(h)], psum[:, 6 + u % 2, 0:P]), s["o_done"])
                    mx(v + 3)

            def cd_sub():
                for t in range(NT_X):
                    link(V.tensor_tensor(cd_sq, O4[:, t, 0:768], O4[:, t, 0:768], ALU.mult))
                    link(V.reduce_sum(rstd[:, t, 0:6], cd_sq.rearrange("p (h d) -> p h d", h=6), axis=AX.X))
                root_of(rstd[:, 0:NT_X, 0:6], 128.0, EPS)
                link(V.tensor_scalar(sub_gain, sub_gain, 1.0 - LAM_INIT, None, ALU.mult))
                for t in range(NT_X):
                    x3 = O4[:, t, 0:768].rearrange("p (h d) -> p h d", h=6)
                    link(V.tensor_tensor(x3, x3, per(rstd[:, t, 0:6], P), ALU.mult))
                    link(V.tensor_tensor(x3, x3, over(sub_gain, 6), ALU.mult))
                    link(V.tensor_copy(O4[:, t, 768:1024], cd_conv[:, t]))

            def ev_rope():
                wait_loads(dve, "ev_in")
                for c, x, table, heads, half in ((0, ev_qa, rope_ret, 4, 64), (1, ev_ka, rope_ret, 4, 64),
                                                 (4, ev_qb, rope_win, 8, 32), (5, ev_kv, rope_win, 2, 32)):
                    for t in range(NT_X):
                        await_read(dve, ("ev_in", c, NT_C + t))
                        rotate(x[:, t] if c < 5 else x[:, t, 0:P], table[:, t], heads, 1, half, ev_ta, ev_tb)
                        if c == 5:
                            kd = ev_kbd[:, t].rearrange("p (h c) -> p h c", h=2)
                            for j in range(2):
                                link(V.tensor_copy(kd[:, :, HD * j:HD * j + HD],
                                                   ev_kv[:, t, 0:P].rearrange("p (h d) -> p h d", h=2)))

            def ev_tr():
                for name, dst, n in (("ev_qa", ev_qaT, 512), ("ev_ka", ev_kaT, 512), ("ev_qb", ev_qbT, 512),
                                     ("ev_kb", ev_kbT, 256)):
                    for t in range(NT_X):
                        take((name, t), dst[:, :, tiles(t)], n)

            def ev_ret():
                wait_loads(dve, "ev_ret")
                link(V.tensor_scalar(lg[:, 2], decay, -1.0, None, ALU.mult))
                link(V.tensor_tensor(lg[:, 0], decay, lg[:, 2], ALU.max), sem("decay_abs"))
                dve.wait_ge(sem("decay_exp"), 1)
                link(V.tensor_scalar(lg[:, 2], lg[:, 1], 2.0, None, ALU.add))
                link(V.reciprocal(lg[:, 2], lg[:, 2]))
                link(V.tensor_tensor(lg[:, 1], lg[:, 1], lg[:, 2], ALU.mult))
                link(V.tensor_tensor(lg[:, 2], lg[:, 1], lg[:, 1], ALU.mult))
                link(V.tensor_scalar(lg[:, 3], lg[:, 2], 1.0 / 17, 1.0 / 15, ALU.mult, ALU.add))
                for d in (13, 11, 9, 7, 5, 3, 1):
                    link(V.tensor_tensor(lg[:, 3], lg[:, 3], lg[:, 2], ALU.mult))
                    link(V.tensor_scalar(lg[:, 3], lg[:, 3], 1.0 / d, None, ALU.add))
                link(V.tensor_tensor(lg[:, 3], lg[:, 3], lg[:, 1], ALU.mult))
                link(V.tensor_scalar(lg[:, 3], lg[:, 3], -2.0, None, ALU.mult))
                link(V.tensor_scalar(lg[:, 2], decay, 0.0, None, ALU.min))
                link(V.tensor_tensor(lg[:, 4], lg[:, 3], lg[:, 2], ALU.add))
                for h in range(4):
                    for mt in range(NT_X):
                        at = 384 - P * mt
                        link(V.tensor_scalar(ev_D[:, mt], dist[:, 0, at:at + SEQ], lg[:, 4, 0, h:h + 1], None, ALU.mult))
                        link(V.scalar_tensor_tensor(ev_D[:, mt], dist[:, 1, at:at + SEQ], lg[:, 4, 1, h:h + 1],
                                                    ev_D[:, mt], ALU.mult, ALU.add),
                             sem("decay_arg") if mt == NT_X - 1 else None)
                    dve.wait_ge(sem("decay_done"), h + 1)
                    for mt in range(NT_X):
                        g, b = await_group(("ret_s", h, mt))
                        link(V.scalar_tensor_tensor(ev_ST[:, mt], psum[:, b, :], P ** -0.5, ev_D[:, mt],
                                                    ALU.mult, ALU.mult), free, g)
                    for t in range(NT_X):
                        take(("ret_y", h, t), O4[:, t, tiles(h)], P)
                for t in range(NT_X):
                    for h in range(4):
                        link(V.bn_stats(stat[:, 0, 0], O4[:, t, tiles(h)]))
                        link(V.bn_aggr(ret_mv[:, t, h], stat[:, 0, 0:1]))
                        link(V.tensor_copy(rstd[:, t, h:h + 1], ret_mv[:, t, h, 1:2]))
                root_of(rstd[:, 0:NT_X, 0:4], 1.0, GN_EPS)
                dve.wait_ge(sem("ret_gate"), 1)
                for t in range(NT_X):
                    for h in range(4):
                        link(V.tensor_scalar(O4[:, t, tiles(h)], O4[:, t, tiles(h)], ret_mv[:, t, h, 0:1],
                                             rstd[:, t, h:h + 1], ALU.subtract, ALU.mult))
                    link(V.tensor_tensor(O4[:, t, 0:512], O4[:, t, 0:512], gn_row, ALU.mult))
                    link(V.tensor_tensor(O4[:, t, 0:512], O4[:, t, 0:512], ev_ga[:, t], ALU.mult))

            def ev_win():
                wait_loads(dve, "ev_win")

                def masked(u):
                    if u >= len(WIN_UNITS):
                        return
                    h, t = WIN_UNITS[u]
                    ks = win_keys(t)
                    n = len(ks) * P
                    g, b = await_group(("win_s", u))
                    first = ks[0] - t + 1
                    link(V.scalar_tensor_tensor(ev_Sm[:, u % 2, 0:n], psum[:, b, 0:n], HD ** -0.5,
                                                band[:, first:first + len(ks)].rearrange("p a c -> p (a c)"),
                                                ALU.mult, ALU.add), free, g)
                    link(V.tensor_copy(ev_Sm[:, u % 2, n:n + 1], sinks[:, h:h + 1]))
                    link(V.reduce_max(nmx[:, u % 4:u % 4 + 1], ev_Sm[:, u % 2, 0:n + 1], axis=AX.X))
                    link(V.tensor_scalar(nmx[:, u % 4:u % 4 + 1], nmx[:, u % 4:u % 4 + 1], -1.0, None, ALU.mult),
                         sem("win_max_done"))

                masked(0)
                for u, (h, t) in enumerate(WIN_UNITS):
                    n = len(win_keys(t)) * P
                    masked(u + 1)
                    take(("win_pt", u), ev_PT[:, u % 2, 0:n], n)
                    g, b = await_group(("win_o", u))
                    a = slice(u % 4, u % 4 + 1)
                    link(V.tensor_tensor(rsum[:, a], esum[:, a], esum[:, 4 + u % 4:5 + u % 4], ALU.add))
                    link(V.reciprocal(rsum[:, a], rsum[:, a]))
                    link(V.tensor_scalar(O4[:, t, 512 + HD * h:576 + HD * h], psum[:, b, 0:HD], rsum[:, a], None,
                                         ALU.mult), free, g)

            def route(m):
                def go():
                    s = [mo_s[:, j] for j in range(16)]
                    wait_loads(dve, f"r{m}_route")
                    link(V.memset(mo_C8, -3e38))
                    link(V.memset(mo_idxf, BIG_IDX))
                    link(V.memset(mo_xg, 0.0))
                    g, b = await_group(("logits", m))
                    link(V.tensor_tensor(mo_L, psum[:, b, 0:144].rearrange("p (t c) -> p t c", c=36),
                                         over(mo_bias, NT_X), ALU.add), free, g)
                    link(V.tensor_copy(mo_C8[:, :, 0:4], mo_L[:, :, 0:4]))
                    for t in range(NT_X):
                        link(V.max(mo_m8[:, t], mo_C8[:, t]))
                        link(V.max_index(mo_ix[:, t], mo_m8[:, t], mo_C8[:, t]))
                    link(V.tensor_copy(mo_ixf, mo_ix))
                    link(V.tensor_copy(s[0], mo_ixf[:, :, 0]))
                    link(V.tensor_tensor(mo_C8[:, :, 0:4], mo_C8[:, :, 0:4], per(mo_m8[:, :, 0], 4), ALU.subtract),
                         M(m, "coarse_shifted"))
                    for t in range(NT_X):
                        link(V.tensor_scalar(mo_G[:, t], mo_iota[:, 0:4], s[0][:, t:t + 1], None, ALU.is_equal))
                    for q in range(4):
                        fine = mo_L[:, :, 4 + 8 * q:12 + 8 * q]
                        dst = mo_FS if q == 0 else mo_t8
                        link(V.tensor_tensor(dst, fine, per(mo_G[:, :, q], 8), ALU.mult))
                        if q:
                            link(V.tensor_tensor(mo_FS, mo_FS, mo_t8, ALU.add))
                    for t in range(NT_X):
                        link(V.max(mo_m8[:, t], mo_FS[:, t]))
                        link(V.max_index(mo_ix[:, t], mo_m8[:, t], mo_FS[:, t]))
                    link(V.tensor_copy(mo_ixf, mo_ix))
                    for j in range(2):
                        link(V.scalar_tensor_tensor(s[4 + j], s[0], 8.0, mo_ixf[:, :, j], ALU.mult, ALU.add))
                    link(V.tensor_tensor(s[2], mo_m8[:, :, 1], mo_m8[:, :, 0], ALU.subtract), M(m, "fine_diff"))
                    for t in range(NT_X):
                        link(V.tensor_scalar(mo_A1[:, t], mo_iota[:, 0:NE], s[4][:, t:t + 1], None, ALU.is_equal))
                        link(V.tensor_scalar(mo_A2[:, t], mo_iota[:, 0:NE], s[5][:, t:t + 1], None, ALU.is_equal))
                    link(V.tensor_tensor(mo_A, mo_A1, mo_A2, ALU.add), M(m, "picked"))
                    dve.wait_ge(M(m, "coarse_exp"), 1)
                    link(V.reduce_sum(s[6], mo_C8[:, :, 0:4], axis=AX.X))
                    link(V.reciprocal(s[6], s[6]))
                    dve.wait_ge(M(m, "fine_exp"), 1)
                    link(V.tensor_scalar(s[7], s[3], 1.0, None, ALU.add))
                    link(V.reciprocal(s[7], s[7]))
                    link(V.tensor_tensor(s[8], s[7], s[6], ALU.mult))
                    link(V.tensor_tensor(s[9], s[8], s[3], ALU.mult))
                    link(V.memset(mo_F[:, :, :, 0], 1.0))
                    for t in range(NT_X):
                        link(V.tensor_scalar(mo_F[:, t, :, 1], mo_F[:, t, :, 0], mo_tok[:, t:t + 1], None, ALU.mult))
                        link(V.tensor_scalar(mo_F[:, t, :, 2], mo_A2[:, t], float(SEQ), mo_tok[:, t:t + 1],
                                             ALU.mult, ALU.add))
                        link(V.tensor_scalar(mo_F[:, t, :, 3], mo_A1[:, t], s[8][:, t:t + 1], None, ALU.mult))
                        link(V.scalar_tensor_tensor(mo_F[:, t, :, 3], mo_A2[:, t], s[9][:, t:t + 1],
                                                    mo_F[:, t, :, 3], ALU.mult, ALU.add))
                    g, b = await_group(("rank", m))
                    link(V.scalar_tensor_tensor(mo_RK, psum[:, b, 0:P].rearrange("p (t e) -> p t e", t=NT_X), 1.0, mo_A,
                                                ALU.add, ALU.mult))
                    link(V.tensor_scalar(mo_RK, mo_RK, -1.0, None, ALU.add))
                    link(V.reduce_max(mo_np[:, 0:1], psum[:, b, P:P + NE], axis=AX.X), free, g)
                    for j in range(1, NT_X):
                        link(V.tensor_scalar(mo_np[:, j:j + 1], mo_np[:, 0:1], P * j + 0.5, None, ALU.is_ge))
                    for j in range(2, NT_X):
                        link(V.tensor_tensor(mo_np[:, 1:2], mo_np[:, 1:2], mo_np[:, j:j + 1], ALU.add))
                    link(V.tensor_scalar(mo_np[:, 1:2], mo_np[:, 1:2], 1.0, None, ALU.add))
                    link(V.tensor_copy(mo_npi[:, 0:1], mo_np[:, 1:2]))
                return go

            def experts(m):
                chain = Link(dve, M(m, "dve_chain"))

                def one_pass(p):
                    first = isinstance(p, int)
                    chain.n, chain.at = {}, {M(m, "dve_chain").name: p * DVE_PER_PASS,
                                             M(m, "sel_ready").name: p * NE}
                    if not first:
                        dve.wait_ge(M(m, "pass_done"), p)
                        chain(V.tensor_scalar(mo_RK, mo_RK, -float(P), None, ALU.add))
                    else:
                        chain(V.tensor_copy(mo_RK, mo_RK))
                    for e in range(NE):
                        if not first or e >= 2:
                            dve.wait_ge(M(m, "sel_used"), p * NE + e - 1)
                        for t in range(NT_X):
                            ins = V.tensor_scalar(mo_sel[:, 4 * (e % 2) + t], mo_iota, mo_RK[:, t, e:e + 1], None,
                                                  ALU.is_equal)
                        chain(ins, M(m, "sel_ready"))
                    dve.wait_ge(M(m, "sel_used"), p * NE + NE)
                    chain(V.tensor_copy(mo_meta, psum[:, 7, 0:P].rearrange("p (e f) -> p e f", f=4)))
                    for j in range(2):
                        chain(V.tensor_scalar(mo_idxf[:, j, 0:NE], mo_meta[:, :, 0], -BIG_IDX, BIG_IDX,
                                              ALU.mult, ALU.add))
                        chain(V.tensor_tensor(mo_idxf[:, j, 0:NE], mo_idxf[:, j, 0:NE], mo_meta[:, :, 1 + j], ALU.add))
                    chain(V.tensor_copy(mo_gate, mo_meta[:, :, 3]))
                    chain(V.tensor_copy(mo_idx, mo_idxf))
                    V.tensor_copy(mo_cnt[:, 0:1], mo_np[:, 0:1]).then_inc(M(m, "lists_ready"), 1)
                    with dve.Fori(0, NE // 2) as i:
                        chain.n, chain.at = {}, {M(m, n).name: p * NE + i * 2 + c for n, c in
                                                 (("h_ready", 0), ("gu_free", 1), ("y_free", 1), ("y_ready", 0))}
                        for b in range(2):
                            e = p * NE + i * 2 + b
                            dve.wait_ge(M(m, "sg_done"), e + 1)
                            chain(V.tensor_tensor(mo_h, psum[:, 1, :], mo_sg, ALU.mult), M(m, "h_ready"))
                            dve.sem_inc(M(m, "gu_free"), 1)
                            dve.wait_ge(M(m, "y_full"), e + 1)
                            dve.wait_ge(M(m, "y_buf_free"), e + 1)
                            chain(V.tensor_scalar(mo_y[:, b], flat(5, D), mo_gate[:, bass.ds(i * 2 + b, 1)], None,
                                                  ALU.mult), M(m, "y_ready"))
                            dve.sem_inc(M(m, "y_free"), 1)

                def go():
                    dve.sem_inc(M(m, "gu_free"), 1)
                    dve.sem_inc(M(m, "y_free"), 1)
                    one_pass(0)
                    more_passes(dve, m, one_pass)
                return go

            def moe_norm(m):
                def go():
                    wait_loads(dve, f"r{m}_norm")
                    for j, t in enumerate(TILES_X):
                        link(V.tensor_tensor(mo_y12[:, 0, j], mo_y12[:, 0, j], mo_y12[:, 1, j], ALU.add))
                        link(V.scalar_tensor_tensor(X[:, t], X[:, t], ALPHA, mo_y12[:, 0, j], ALU.mult, ALU.add))
                        norm_tile(j, t, rows_moe, LN_EPS2)
                        if m == 0 and j:
                            copied("r0_norm_t")(t - 1)
                    if m == 0:
                        copied("r0_norm_t")(TILES_X[-1])
                return go

            steps = {
                "mod0": mod(0), "modT0": mod_t(0), "mod1": mod(1), "modT1": mod_t(1),
                "ab_ht": modulated("ab_ht", ALL, 0), "ab_in": ab_rope, "ab_tr": ab_tr, "ab_att": ab_att,
                "ab_pool": ab_pool, "ab_ot": plain("ab_ot", ALL, OT_ab, D),
                "ab_out": out_norm("ab_out", ALL, rows_ab, EPS, True, True, modulate("ab_out_t", 24)),
                "cd_ht": modulated("cd_ht", ALL, 0), "cd_u": cd_u, "cd_conv": cd_conv_,
                "cd_q": cd_heads("cd_q", "cd_qt", TILES_X,
                                 lambda t: two_halves(("cd_qt", t), cd_qT[:, :, :, tiles(t - NT_C)])),
                "cd_k": cd_heads("cd_k", "cd_kt", ALL, lambda t: take(("cd_kt", t), cd_kT[:, :, tiles(t)], 768)),
                "cd_att": cd_att, "cd_sub": cd_sub, "cd_ot": plain("cd_ot", TILES_X, OT_cd, D, NT_C),
                "cd_out": out_norm("cd_out", TILES_X, rows_cd, EPS, True, True, modulate("cd_out_t", 24)),
                "ev_in": ev_rope, "ev_tr": ev_tr, "ev_ret": ev_ret,
                "ev_win": ev_win, "ev_ot": plain("ev_ot", TILES_X, OT_ev, D, NT_C),
                "ev_out": out_norm("ev_out", TILES_X, rows_ev, LN_EPS2, False, True, copied("ev_out_t")),
                "fo_out": out_norm("fo_out", TILES_X, rows_fo, LN_EPS2, False, True, copied("fo_out_t")),
                "f0x_in": product("f0x", SEQ), "f0c_in": product("f0c", CTX), "f1x_in": product("f1x", SEQ),
                "f0x_out": out_norm("f0x_out", TILES_X, rows_ffn, EPS, True, False),
                "f0c_out": out_norm("f0c_out", TILES_C, rows_ffn, EPS, True, False),
                "f1x_out": out_norm("f1x_out", TILES_X, rows_ffn, EPS, True, False, copied("f1x_out_t")),
            }
            for m in range(2):
                steps[f"r{m}_route"] = route(m)
                steps[f"r{m}_experts"] = experts(m)
                steps[f"r{m}_norm"] = moe_norm(m)
            run(dve, steps, stage_dve)

        @block.gpsimd
        def _(pool):
            def loads(stage):
                for dst, src in LOADS[stage]:
                    pool.dma_start(dst, src, allow_slow_non_contiguous=stage[:3] == "mod").then_inc(sem("loads_" + stage), 16)

            def store_mod(l):
                def go():
                    pool.dma_start(A["mod"][l], mod_rows).then_inc(sem("mod_stored"), 16)
                    pool.wait_ge(sem("mod_stored"), 16 * (l + 1))
                return go

            def route(m):
                def go():
                    loads(f"r{m}_route")
                    for t in range(NT_X):
                        pool.dma_start(A[f"xs{m}"][tiles(t)], X[:, NT_C + t]).then_inc(M(m, "x_stored"), 16)
                    pool.wait_ge(M(m, "x_stored"), 16 * NT_X)
                return go

            def await_count(s, value):
                pool.wait_ge(s, value)
                if not isinstance(value, int):
                    pool.sem_inc(sem("pool_steps"), 1)

            def experts(m):
                def one_pass(p):
                    await_count(M(m, "lists_ready"), p + 1)

                    def gather(e):
                        if e > NE:
                            return
                        if e >= 2:
                            await_count(M(m, "xt_full"), p * (NE + 1) + e - 1)
                        pool.indirect_dma_start(
                            out=mo_xg[:, e % 2], out_offset=None, in_=A[f"xs{m}"][:, :],
                            in_offset=bass.IndirectOffsetOnAxis(ap=mo_idx[:, 0, e:e + 1], axis=0),
                            bounds_check=SEQ - 1, oob_is_err=False).then_inc(M(m, f"xg_ready{e % 2}"), 16)

                    def buffer_free(e):
                        await_count(M(m, f"y_stored{e % 2}"), (p * (NE // 2) + e // 2 + 1) * 16)
                        pool.sem_inc(M(m, "y_buf_free"), 1)

                    gather(0)
                    gather(1)
                    for e in range(NE):
                        gather(e + 2)
                        await_count(M(m, "y_ready"), p * NE + e + 1)
                        pool.indirect_dma_start(
                            out=A[f"y{m}"][:, :], out_offset=bass.IndirectOffsetOnAxis(ap=mo_idx[:, 1, e:e + 1], axis=0),
                            in_=mo_y[:, e % 2], in_offset=None,
                            bounds_check=2 * SEQ - 1, oob_is_err=False).then_inc(M(m, f"y_stored{e % 2}"), 16)
                        if e >= 1:
                            buffer_free(e - 1)
                    buffer_free(NE - 1)
                    await_count(M(m, "xg_ready0"), p * (17 * 16) + 17 * 16)
                    pool.sem_inc(M(m, "pass_done"), 1)

                def go():
                    pool.sem_inc(M(m, "y_buf_free"), 2)
                    one_pass(0)
                    more_passes(pool, m, one_pass)
                return go

            steps = {s: (lambda s: lambda: loads(s))(s) for s in LOADS}
            steps["modT0"], steps["modT1"] = store_mod(0), store_mod(1)
            for m in range(2):
                steps[f"r{m}_route"], steps[f"r{m}_experts"] = route(m), experts(m)
            run(pool, steps)
            for t in range(NT_X):
                pool.dma_start(A["out"][0, tiles(t)], X[:, NT_C + t]).then_inc(sem("stored"), 16)
            pool.wait_ge(sem("stored"), 16 * NT_X)

        @block.sync
        def _(sp):
            sp.dma_start(ident, A["ident"]).then_inc(sem("ident_loaded"), 16)
            for t in range(NT_C):
                sp.dma_start(X[:, t], A["ctx"][0, tiles(t)]).then_inc(sem("x_loaded"), 16)
            for t in range(NT_X):
                sp.dma_start(X[:, NT_C + t], A["x"][0, tiles(t)]).then_inc(sem("x_loaded"), 16)
            used = [c for c in range(len(chunks)) if c in chunk_read]
            last_user = {}

            def load(i):
                ch = chunks[i]
                if ch["slot"] in last_user:
                    sp.wait_ge(*chunk_read[last_user[ch["slot"]]])
                last_user[ch["slot"]] = i
                for c0, src in ch["parts"]:
                    n = src.shape[2]
                    sp.dma_start(slot(i)[:, :, c0:c0 + n], src).then_inc(w_ready[ch["slot"]], 16)

            def expert_weights(m):
                first = STAGES.index(f"r{m}_experts")

                def one(p, i, b, part, wait=True):
                    if wait:
                        e1 = p * NE + i * 2 + b - 1
                        sp.wait_ge(M(m, "gu_full" if part < 2 else "y_full"), e1)
                    name = ("expert_w_gate_2", "expert_w_up_2", "expert_w_down_2")[part]
                    src = A[name][m, bass.ds(i * 2 + b, 1)].rearrange("o (k p) n -> p (o k) n", p=P)
                    dst = region(MOE_RING_KB[3 * b + part], KD if part < 2 else 4, 512 if part < 2 else D)
                    sp.dma_start(dst, src).then_inc(M(m, f"w_ready{3 * b + part}"), 16)

                for b in range(2):
                    for part in range(3):
                        s = 3 * b + part
                        if s < 5 and s in last_user:
                            sp.wait_ge(*chunk_read[last_user[s]])
                        else:
                            sp.wait_ge(stage_act, first)
                            sp.wait_ge(stage_dve, first)
                        one(0, 0, b, part, wait=False)
                with sp.Fori(1, NE // 2) as i:
                    for b in range(2):
                        for part in range(3):
                            one(0, i, b, part)

                def one_pass(p):
                    with sp.Fori(0, NE // 2) as i:
                        for b in range(2):
                            for part in range(3):
                                one(p, i, b, part)

                sp.wait_ge(stage_act, first)
                sp.wait_ge(stage_dve, first)
                more_passes(sp, m, one_pass)
                sp.wait_ge(stage_act, first + 1)
                sp.wait_ge(stage_dve, first + 1)
                last_user.clear()

            for i in used:
                if i == before_experts0 and "r0_experts" in STAGES:
                    expert_weights(0)
                load(i)
            if used and used[-1] < before_experts0 and "r0_experts" in STAGES:
                expert_weights(0)
            if "r1_experts" in STAGES:
                expert_weights(1)


_INS = """x c ctx c_ctx ab_w_in ab_q_gain ab_k_gain ab_w_pool ab_pool_scale ab_w_out cd_w_in cd_lambda_q1 cd_lambda_k1
    cd_lambda_q2 cd_lambda_k2 cd_subln_gain cd_conv_w cd_conv_b cd_conv_ln_g cd_conv_ln_b cd_w_out ada_w ada_b ln1_g
    ln1_b ln2_g ln2_b ffn_w_in ffn_w_out w_in_even_2 ret_decay_logit_2 ret_gn_gain_2 sink_logit_2 w_out_even_2
    w_out_fourier_2 ln1_gain_2 ln1_bias_2 ln2_gain_2 ln2_bias_2 router_coarse_w_2 router_coarse_b_2 router_fine_w_2
    router_fine_b_2 expert_w_gate_2 expert_w_up_2 expert_w_down_2""".split()
STOP = None


def kernel(**inputs):
    import concourse.bacc as bacc
    from concourse.bass_utils import run_bass_kernel_spmd

    nc = bacc.Bacc("TRN2", target_bir_lowering=False, num_devices=1)
    arrays = {n: np.ascontiguousarray(inputs[n]) for n in _INS}
    arrays.update(constants())
    aps = {n: nc.dram_tensor(f"in_{n}", a.shape, F32, kind="ExternalInput").ap() for n, a in arrays.items()}
    for n, shape in (("mod", (2, 2, 6 * D)), ("xs0", (SEQ, D)), ("xs1", (SEQ, D)), ("y0", (2 * SEQ, D)),
                     ("y1", (2 * SEQ, D))):
        aps[n] = nc.dram_tensor(n, shape, F32, kind="Internal").ap()
    aps["out"] = nc.dram_tensor("out", (1, SEQ, D), F32, kind="ExternalOutput").ap()
    build(nc, aps, STOP)
    r = run_bass_kernel_spmd(nc, [{f"in_{n}": a for n, a in arrays.items()}], core_ids=[0])
    return r.results[0]["out"]
```

```python
import math
from contextlib import ExitStack

import numpy as np
import concourse.bass as bass
from concourse import mybir

F32, I32, U32 = mybir.dt.float32, mybir.dt.int32, mybir.dt.uint32
F32R = mybir.dt.float32r
ACT, ALU, AX = mybir.ActivationFunctionType, mybir.AluOpType, mybir.AxisListType

P = 128
D = 1024
KD = D // P
SEQ, CTX = 512, 256
NT_C, NT_X = CTX // P, SEQ // P
NT = NT_C + NT_X
HD = 64
GRID_W = 64
FFN = 2816
KF = FFN // P
EPS, LN_EPS2, GN_EPS = 1e-6, 1e-5, 1e-6
ALPHA = (2.0 * 2) ** 0.25
LAM_INIT = 0.8 - 0.6 * math.exp(-0.3)
NE = 32
BIG_IDX = 4096.0
NEG = -1e30
DVE_PER_PASS = 8


def constants():
    f = np.float32
    c = {}
    c["ident"] = np.eye(P, dtype=f)
    t = np.arange(SEQ)
    row, col = (t // GRID_W).astype(f), (t % GRID_W).astype(f)
    fr = (10000.0 ** (-np.arange(0, 32, 2, dtype=f) / 32)).astype(f)
    cs, sn = [], []
    for pos in (row, col):
        a = (pos[:, None] * fr[None]).astype(f).astype(np.float64)
        cs += [np.cos(a), np.cos(a)]
        sn += [-np.sin(a), np.sin(a)]
    c["rope_ax"] = np.concatenate([np.concatenate(cs, 1), np.concatenate(sn, 1)], 1).astype(f)
    for name, half in (("rope_ret", 64), ("rope_win", 32)):
        inv = (10000.0 ** (-np.arange(half, dtype=f) / half)).astype(f)
        a = (t.astype(f)[:, None] * inv[None]).astype(f).astype(np.float64)
        c[name] = np.concatenate([np.cos(a), np.cos(a), -np.sin(a), np.sin(a)], 1).astype(f)

    def pool(n):
        out = np.zeros((4, n, n), np.float64)
        for g, w in enumerate((2, 4, 8, 16)):
            for i in range(n):
                lo, hi = max(i - w // 2, 0), min(i + (w - 1 - w // 2) + 1, n)
                out[g, lo:hi, i] += 1.0 / (hi - lo)
                out[g, i, i] -= 1.0
        return out

    c["pool_x"] = np.ascontiguousarray(pool(SEQ).reshape(4, NT_X, P, SEQ).transpose(2, 0, 1, 3)).astype(f)
    c["pool_c"] = np.ascontiguousarray(pool(CTX).reshape(4, NT_C, P, CTX).transpose(2, 0, 1, 3)).astype(f)
    j, p = np.arange(896)[None] - 384, np.arange(P)[:, None]
    c["dist"] = np.stack([np.maximum(j - p, 0), np.maximum(p - j, 0)], 1).astype(f)
    i, k = np.arange(P)[:, None], np.arange(P)[None]
    c["band"] = np.stack([np.where(i <= k, 0, NEG), np.zeros((P, P)), np.where(k <= i, 0, NEG)], 1).astype(f)
    kk = np.outer(np.arange(256), np.arange(256)) % 256 * (2 * np.pi / 256)
    c["dft_c"] = np.ascontiguousarray(
        np.concatenate([np.cos(kk), np.sin(kk)], 1).reshape(2, P, 512).transpose(1, 0, 2)).astype(f)
    kk = np.outer(np.arange(SEQ), np.arange(SEQ)) % SEQ * (2 * np.pi / SEQ)
    s = 1.0 / math.sqrt(SEQ * 256)
    c["dft_s"] = np.ascontiguousarray(
        np.stack([np.cos(kk) * s, -np.sin(kk) * s]).reshape(2, NT_X, P, SEQ).transpose(2, 0, 1, 3)).astype(f)
    c["before"] = np.concatenate([np.triu(np.ones((P, P)), 1), np.ones((P, P))], 1).astype(f)
    c["iota"] = np.tile(np.arange(P, dtype=f), (P, 1))
    c["tok"] = (np.arange(NT_X)[None] * P + np.arange(P)[:, None]).astype(f)
    return c


def build(nc, A, stop):
    ctx = ExitStack()
    with ctx:
        KB = 256
        RING_END, SBUF_END = 80, 207
        with nc.sbuf_tensor("ring_rounded", [P, RING_END * KB], F32R) as ring_rounded:
            pass
        ring = ctx.enter_context(nc.sbuf_tensor("ring", [P, RING_END * KB], F32))
        with nc.sbuf_tensor("below_low", [P, (104 - RING_END) * KB], F32), \
             nc.sbuf_tensor("low_rounded", [P, 68 * KB], F32R) as low_rounded, \
             nc.sbuf_tensor("below_high", [P, 8 * KB], F32), \
             nc.sbuf_tensor("high_rounded", [P, 20 * KB], F32R) as high_rounded:
            pass
        arena = ctx.enter_context(nc.sbuf_tensor("arena", [P, (SBUF_END - RING_END) * KB], F32))
        PLACES = {False: [(0, RING_END, ring), (RING_END, SBUF_END - RING_END, arena)],
                  True: [(0, RING_END, ring_rounded), (104, 68, low_rounded), (180, 20, high_rounded)]}

        def region(kb, *shape, parts=P, rounded=False):
            n = int(np.prod(shape))
            first, size, tensor = [pl for pl in PLACES[rounded] if pl[0] <= kb < pl[0] + pl[1]][0]
            at = int(round((kb - first) * KB))
            assert at + n <= size * KB, (kb, shape)
            v = tensor[0:parts, at:at + n]
            if len(shape) == 1:
                return v
            names = "abcde"[:len(shape)]
            return v.rearrange(f"p ({' '.join(names)}) -> p {' '.join(names)}",
                               **{n_: s for n_, s in zip(names[1:], shape[1:])})

        RING_KB = [0, 16, 32, 48, 64]
        MOE_RING_KB = RING_KB + [128]
        X = region(80, NT, D)
        HT = region(104, KD, NT * P)
        BIG, MISC = 128, 200

        ident = ctx.enter_context(nc.sbuf_tensor("ident", [P, P], F32))[:, :]
        mod_cols = region(MISC, 48, 2)
        stat = region(MISC + 0.5, NT, 2, 6)
        mv = region(MISC + 1, NT, 2)
        rstd = region(MISC + 1.0625, NT, 16)
        nmx = region(MISC + 3.5, 8)
        esum = region(MISC + 3.75, 8)
        rsum = region(MISC + 4, 8)
        lam = region(MISC + 4.25, 8)
        psum = ctx.enter_context(nc.psum_tensor("psum", [P, 8, 512], F32))

        sems = {}

        def sem(name):
            if name not in sems:
                sems[name] = ctx.enter_context(nc.semaphore(name))
            return sems[name]

        psum_full = sem("psum_full")
        free_by = {"act": sem("psum_free_act"), "dve": sem("psum_free_dve")}
        x_normed = sem("x_normed")
        w_used = sem("w_used")
        split_high, split_low = sem("split_high"), sem("split_low")
        act_chain, dve_chain = sem("act_chain"), sem("dve_chain")
        stage_act, stage_dve = sem("stage_act"), sem("stage_dve")
        gate_done = sem("gate_done")
        stat_ready, sqrt_done = sem("stat_ready"), sem("sqrt_done")
        w_ready = [sem(f"w_ready{i}") for i in range(5)]

        mod_rows, ada_bias = region(BIG, 6 * D, parts=2), region(BIG + 24, 6 * D, parts=2)
        c_cols, c_silu = region(BIG + 48, 2, KD), region(BIG + 49, KD, 2)
        ab_qk, ab_vu = region(BIG, NT, 1024), region(BIG + 24, NT, 512)
        ab_qT = region(BIG + 36, 6, NT * P)
        ab_kT = region(BIG, 4, 2, NT * P)
        ab_kd = region(BIG + 60, NT, 512)
        tmp_a, tmp_b = region(BIG + 52, 1024), region(BIG + 56, 1024)
        qk_gain = region(MISC + 5, 2, HD)
        rope_ax = region(MISC + 1.5, NT_X, 128)
        att_P, att_PT = region(BIG + 54, 2, 768), region(BIG + 60, 2, 768)
        pooledT, w_pool = region(BIG + 54, 4, 512, parts=64), region(BIG + 62, 4, 64, parts=64)
        pool_scale = region(BIG + 63, 256)
        O_all = region(104, NT, D)
        cd_conv = region(80, NT_X, 256)
        cd_qT = region(BIG, 6, 2, SEQ)
        cd_kT, cd_v = region(BIG + 24, 6, NT * P), region(BIG + 42, NT, 768)
        cd_tmp = region(BIG + 60, 4, 768)
        cd_z, cd_acc, cd_sg = region(BIG, 2, 544), region(BIG + 5, 2, SEQ), region(BIG + 9, 2, SEQ)
        cd_wrow, cd_wcol = region(BIG + 13, 256, parts=32), region(BIG + 14, 2, 32)
        cd_lng, cd_lnb = region(BIG + 15, 256), region(BIG + 16, 256)
        cd_ta, cd_tb = region(84, 384), region(85.5, 384)
        cd_P, cd_PT = region(BIG + 60, 4, 768), region(120, 2, 768)
        cd_sq = region(BIG + 60, 768)
        O4 = region(104, NT_X, D)
        lam_in, sub_gain = region(126, 4, HD), region(127, 128)
        ev_qa, ev_ka, ev_va, ev_ga, ev_qb = (region(BIG + 8 * i, NT_X, 512) for i in range(5))
        ev_kv = region(BIG + 40, NT_X, 256)
        ev_qaT, ev_kaT = region(BIG + 44, 4, SEQ), region(BIG + 52, 4, SEQ)
        ev_qbT, ev_kbT = region(BIG + 60, 4, SEQ), region(124, 2, SEQ)
        rope_ret, rope_win = region(BIG + 44, NT_X, 256), region(BIG + 48, NT_X, 128)
        ev_ta, ev_tb, ev_kbd = region(80, 512), region(82, 512), region(BIG + 68, NT_X, 256)
        ev_D, ev_ST = [region(BIG, 4, SEQ), region(80, 4, SEQ)], region(BIG + 8, 4, SEQ)
        dist = region(BIG + 32, 2, 896)
        gn_row = region(120, 512)
        decay = region(122, 2, 4)
        lg = region(122.25, 8, 2, 4)
        sinks = region(122.75, 8)
        ev_Sm, ev_P, ev_PT = region(BIG, 2, 388), region(BIG + 4, 2, 384), region(BIG + 8, 2, 384)
        band = region(BIG + 12, 3, P)
        fo_AB, fo_YT = region(BIG, NT_X, 4, 512), region(BIG + 32, KD, SEQ)
        ffn_hT, ffn_sg = region(BIG, KF, SEQ), region(BIG + 44, 2, SEQ)
        ffn_xH, ffn_hH = region(180, KD, SEQ, rounded=True), region(192, 4, SEQ, rounded=True)
        ffn_xL, ffn_hL = region(104, KD, NT * P, rounded=True), region(BIG, KF, SEQ, rounded=True)
        HIGH_KB = RING_KB[3:]
        OT_ab, OT_cd, OT_ev = region(BIG + 36, KD, NT * P), region(BIG, KD, SEQ), region(BIG + 44, KD, SEQ)

        class Rows:

            def __init__(self, kb, gates):
                self.gate = [region(kb + 4 * i, D) for i in range(gates)]
                kb += 4 * gates
                self.g, self.b, self.tmp = region(kb, D), region(kb + 4, D), region(kb + 8, 2, 512)

        rows_ab, rows_cd, rows_ev, rows_fo = Rows(BIG, 2), Rows(BIG + 24, 1), Rows(BIG, 0), Rows(BIG + 48, 0)
        rows_ffn = Rows(BIG + 48, 1)
        mo_xg, mo_xgT = region(144, 2, D), region(152, KD, P)
        mo_sg, mo_h, mo_hT, mo_y = region(156, 512), region(158, 512), region(160, 4, P), region(162, 2, D)
        mo_sel, mo_F = region(170, 8, P), region(174, NT_X, NE, 4)
        mo_RK, mo_cnt = region(176, NT_X, NE), region(176.5, 8)
        mo_idxf, mo_gate = region(176.75, 2, NE + 1), region(177.25, NE)
        mo_idx = region(177.5, 2, NE + 1).bitcast(I32)
        mo_np, mo_npi = region(178, 8), region(178.125, 8).bitcast(I32)
        mo_L, mo_C8 = region(178.25, NT_X, 36), region(179, NT_X, 8)
        mo_m8, mo_ix, mo_ixf = region(179.25, NT_X, 8), region(179.5, NT_X, 8).bitcast(U32), region(179.75, NT_X, 8)
        mo_G, mo_FS, mo_t8 = region(180, NT_X, 4), region(180.25, NT_X, 8), region(180.5, NT_X, 8)
        mo_A1, mo_A2, mo_A = region(180.75, NT_X, NE), region(181.25, NT_X, NE), region(181.75, NT_X, NE)
        mo_s = region(182.25, 16, NT_X)
        mo_wr, mo_bias = region(183, KD, 36), region(184.25, 36)
        mo_before, mo_iota, mo_tok = region(184.5, 2, P), region(185.5, P), region(186, NT_X)
        mo_meta = region(186.25, NE, 4)
        mo_y12 = region(144, 2, NT_X, D)
        rows_moe = Rows(187, 0)

        def ffn_stages(f):
            return [f"{f}_in", f"{f}_out"]

        def moe_stages(m):
            return [f"r{m}_route", f"r{m}_experts", f"r{m}_norm"]

        STAGES = (["mod0", "modT0", "ab_ht", "ab_in", "ab_tr", "ab_att", "ab_pool", "ab_ot", "ab_out"]
                  + ffn_stages("f0x") + ffn_stages("f0c")
                  + ["mod1", "modT1", "cd_ht", "cd_u", "cd_conv", "cd_q", "cd_k", "cd_att", "cd_sub", "cd_ot",
                     "cd_out"] + ffn_stages("f1x")
                  + ["ev_in", "ev_tr", "ev_ret", "ev_win", "ev_ot", "ev_out"]
                  + moe_stages(0) + ["fo_dft", "fo_seq", "fo_out"] + moe_stages(1))
        if stop:
            STAGES = STAGES[:STAGES.index(stop) + 1]

        TILES_X, TILES_C = list(range(NT_C, NT)), list(range(NT_C))
        ALL = TILES_C + TILES_X

        def row(v):
            return v.partition_broadcast(P)

        def norm_rows(rows, l, n, gates=()):
            out = [(rows.gate[i], row(A["mod"][l, who, at * D:at * D + D])) for i, (who, at) in enumerate(gates)]
            sfx = "" if n[:2] == "ln" else ""
            g, b = (f"{n}_g", f"{n}_b") if not n.endswith("_2") else (n.replace("_2", "_gain_2"), n.replace("_2", "_bias_2"))
            return out + [(rows.g, row(A[g][l])), (rows.b, row(A[b][l]))]

        def mod_loads(l):
            return [(c_cols[:, 0], A["c"][0].rearrange("(k p) -> p k", p=P)),
                    (c_cols[:, 1], A["c_ctx"].rearrange("(k p) -> p k", p=P)),
                    (ada_bias, A["ada_b"][l].partition_broadcast(2))]

        def route_loads(m):
            return [(mo_wr[:, :, 0:4], A["router_coarse_w_2"][m].rearrange("(k p) n -> p k n", p=P)),
                    (mo_wr[:, :, 4:36], A["router_fine_w_2"][m].rearrange("(k p) n -> p k n", p=P)),
                    (mo_bias[:, 0:4], row(A["router_coarse_b_2"][m])), (mo_bias[:, 4:36], row(A["router_fine_b_2"][m])),
                    (mo_before, A["before"].rearrange("p (a n) -> p a n", a=2)), (mo_iota, A["iota"]),
                    (mo_tok, A["tok"])]

        LOADS = {
            "mod0": mod_loads(0), "mod1": mod_loads(1),
            "ab_in": [(qk_gain[:, 0], row(A["ab_q_gain"][0])), (qk_gain[:, 1], row(A["ab_k_gain"][0])),
                        (rope_ax, A["rope_ax"].rearrange("(t p) n -> p t n", p=P))],
            "ab_pool": [(w_pool, A["ab_w_pool"][0].rearrange("g c d -> c g d")),
                        (pool_scale, row(A["ab_pool_scale"][0]))],
            "ab_out": norm_rows(rows_ab, 0, "ln1", [(0, 2), (1, 2)]),
            "f0x_out": norm_rows(rows_ffn, 0, "ln2", [(0, 5)]),
            "f0c_out": norm_rows(rows_ffn, 0, "ln2", [(1, 5)]),
            "cd_u": [(cd_wrow[0:31], A["cd_conv_w"][0]), (cd_wrow[31:32], A["cd_conv_b"]),
                     (cd_lng, row(A["cd_conv_ln_g"][0])), (cd_lnb, row(A["cd_conv_ln_b"][0]))],
            "cd_att": [(lam_in[:, i], row(A[n][0])) for i, n in
                     enumerate(("cd_lambda_q1", "cd_lambda_k1", "cd_lambda_q2", "cd_lambda_k2"))]
            + [(sub_gain, row(A["cd_subln_gain"][0]))],
            "cd_out": norm_rows(rows_cd, 1, "ln1", [(0, 2)]),
            "f1x_out": norm_rows(rows_ffn, 1, "ln2", [(0, 5)]),
            "ev_in": [(rope_ret, A["rope_ret"].rearrange("(t p) n -> p t n", p=P)),
                        (rope_win, A["rope_win"].rearrange("(t p) n -> p t n", p=P))],
            "ev_ret": [(dist, A["dist"]), (gn_row, row(A["ret_gn_gain_2"][0])),
                       (decay[:, 0], row(A["ret_decay_logit_2"][0, 0])), (decay[:, 1], row(A["ret_decay_logit_2"][0, 1])),
                       (sinks, row(A["sink_logit_2"][0]))],
            "ev_win": [(band, A["band"])],
            "ev_out": norm_rows(rows_ev, 0, "ln1_2"),
            "fo_out": norm_rows(rows_fo, 1, "ln1_2"),
        }
        Y_LOADS = {}
        for m in range(2):
            LOADS[f"r{m}_route"] = route_loads(m) + norm_rows(rows_moe, m, "ln2_2")
            Y_LOADS[f"r{m}_norm"] = [
                (mo_y12[:, j, t], A[f"y{m}"][j * SEQ + t * P:j * SEQ + t * P + P]) for j in range(2) for t in range(NT_X)]

        def wait_loads(eng, stage):
            eng.wait_ge(sem("loads_" + stage), 16 * len({**LOADS, **Y_LOADS}[stage]))

        chunks, by_name = [], {}

        def add_chunk(name, parts, k, n, split=False):
            i = len(chunks)
            n_split = sum(c["split"] for c in chunks)
            chunks.append(dict(parts=parts, k=k, n=n, slot=n_split % 3 if split else i % 5, split=split,
                               high=n_split % 2, name=name))
            by_name.setdefault(name, []).append(i)

        def chunk_loaded(i):
            return w_ready[chunks[i]["slot"]], 16 * sum(
                len(c["parts"]) for c in chunks[:i + 1] if c["slot"] == chunks[i]["slot"])

        def kpn(w, c0, c1, k0, k):
            return w[k0 * P:(k0 + k) * P, c0:c1].rearrange("(k p) n -> p k n", p=P)

        def weight_chunks(name, w, bounds, kblocks=KD, split=False):
            for c0, c1 in bounds:
                for k0 in range(0, kblocks, 8):
                    k = min(8, kblocks - k0)
                    add_chunk(name, [(0, kpn(w, c0, c1, k0, k))], k, c1 - c0, split)

        def ffn_chunks(f, l):
            w = A["ffn_w_in"][l]
            for j in range(0, FFN, 256):
                add_chunk(f"{f}_in", [(0, kpn(w, j, j + 256, 0, KD)), (256, kpn(w, FFN + j, FFN + j + 256, 0, KD))],
                          KD, 512, split=True)
            for k0 in range(0, KF, 4):
                k = min(4, KF - k0)
                add_chunk(f"{f}_out", [(0, kpn(A["ffn_w_out"][l], 0, D, k0, k))], k, D, split=True)

        HALVES = [(0, 512), (512, 1024)]
        weight_chunks("mod0", A["ada_w"][0], [(i * 512, i * 512 + 512) for i in range(12)])
        weight_chunks("ab_in", A["ab_w_in"][0], [(0, 512), (512, 1024), (1024, 1536)])
        for i in range(2):
            add_chunk("ab_pool", [(0, A["pool_x"][:, 2 * i:2 * i + 2].rearrange("p g t n -> p (g t) n"))], 8, 512)
        add_chunk("ab_pool", [(0, A["pool_c"].rearrange("p g t n -> p (g t) n"))], 8, 256)
        weight_chunks("ab_out", A["ab_w_out"][0], HALVES)
        ffn_chunks("f0x", 0)
        ffn_chunks("f0c", 0)
        weight_chunks("mod1", A["ada_w"][1], [(i * 512, i * 512 + 512) for i in range(12)])
        cw = A["cd_w_in"][0]
        weight_chunks("cd_u", cw, [(2304, 2816)])
        weight_chunks("cd_v", cw, [(1536, 2048), (2048, 2304)])
        weight_chunks("cd_q", cw, [(0, 512), (512, 768)])
        weight_chunks("cd_k", cw, [(768, 1280), (1280, 1536)])
        weight_chunks("cd_out", A["cd_w_out"][0], HALVES)
        ffn_chunks("f1x", 1)
        weight_chunks("ev_in", A["w_in_even_2"][0], [(i * 512, min(i * 512 + 512, 2816)) for i in range(6)],
                      split=True)
        weight_chunks("ev_out", A["w_out_even_2"][0], HALVES)
        before_experts0 = len(chunks)
        add_chunk("fo_dft", [(0, A["dft_c"])], 2, 512)
        add_chunk("fo_seq", [(0, A["dft_s"].rearrange("p s t n -> p (s t) n"))], 8, 512)
        weight_chunks("fo_out", A["w_out_fourier_2"][0], HALVES)
        chunk_read = {}
        hidden_read = {}
        groups = {}

        def slot(i, rounded=False):
            ch = chunks[i]
            return region(RING_KB[ch["slot"]], ch["k"], ch["n"], rounded=rounded)

        def slot_high(i):
            ch = chunks[i]
            return region(HIGH_KB[ch["high"]], ch["k"], ch["n"], rounded=True)

        split_at, split_order = {}, {}

        def input_order(ids, work_per_chunk):
            order = []
            for k in range(KD):
                order += [("x", k), ("w", ids[0], k)]
            order.append(("w", ids[1], None))
            for c in range(len(ids)):
                order += [("work", work_per_chunk * c + j) for j in range(work_per_chunk)]
                if c + 2 < len(ids):
                    order.append(("w", ids[c + 2], None))
            return order

        def hidden_order(ids):
            order = []
            for c, i in enumerate(ids):
                order.append(("w", i, None))
                order += [("h", k) for k in range(4 * c, min(4 * c + 4, KF))]
            return order

        for stage in ("f0x_in", "f0x_out", "f0c_in", "f0c_out", "f1x_in", "f1x_out", "ev_in"):
            split_order[stage] = (hidden_order(by_name[stage]) if stage[-3:] == "out" else
                                  input_order(by_name[stage], 1 if stage == "ev_in" else 2))
            for piece in split_order[stage]:
                if piece[0] != "work":
                    split_at[stage, piece] = len(split_at) + 1

        def piece_views(stage, piece):
            ntok, col0 = (CTX, 0) if stage[:3] == "f0c" else (SEQ, NT_C * P)
            if piece[0] == "x":
                k, cols = piece[1], slice(col0, col0 + ntok)
                return HT[:, k, cols], ffn_xH[:, k, 0:ntok], ffn_xL[:, k, cols]
            if piece[0] == "h":
                k = piece[1]
                return ffn_hT[:, k, 0:ntok], ffn_hH[:, k % 4, 0:ntok], ffn_hL[:, k, 0:ntok]
            views = slot(piece[1]), slot_high(piece[1]), slot(piece[1], rounded=True)
            return views if piece[2] is None else [v[:, piece[2]] for v in views]

        class Link:

            def __init__(self, eng, chain):
                self.eng, self.chain, self.n, self.at = eng, chain, {}, {}

            def __call__(self, ins, s=None, upto=None):
                s = self.chain if s is None else s
                self.n[s.name] = self.n.get(s.name, 0) + 1
                ins.then_inc(s, 1)
                self.eng.wait_ge(s, upto if upto is not None else self.at.get(s.name, 0) + self.n[s.name])

        def run(eng, steps, me=None):
            for n, name in enumerate(STAGES):
                if name in ("ab_ht", "cd_ht"):
                    eng.wait_ge(sem("mod_stored"), 16 if name == "ab_ht" else 32)
                if name in ("r0_norm", "r1_norm"):
                    eng.wait_ge(M(int(name[1]), "x_stored"), 16 * NT_X)
                if name in steps:
                    steps[name]()
                if me is not None:
                    eng.sem_inc(me, 1)
                eng.wait_ge(stage_act, n + 1)
                eng.wait_ge(stage_dve, n + 1)

        def await_read(eng, name):
            _, _, by, n = groups[name]
            eng.wait_ge(free_by[by], n)

        def tiles(t, n=1):
            return slice(t * P, (t + n) * P)

        def flat(bank, n):
            return psum[:, bank:bank + -(-n // 512), :].rearrange("p b n -> p (b n)")[:, 0:n]

        AB_UNITS = [(h, t) for h in range(12) for t in TILES_X] + [(h, t) for h in range(12) for t in TILES_C]
        CD_UNITS = [(h, t) for h in range(6) for t in range(NT_X)]
        WIN_UNITS = [(h, t) for h in range(8) for t in range(NT_X)]

        def win_keys(t):
            return [k for k in (t - 1, t, t + 1) if 0 <= k < NT_X]

        def ab_keys(t):
            return NT if t >= NT_C else NT_C

        A_, C_ = {}, {}
        for nm in ("score_full", "max_done", "exp_done", "pt_full", "pt_copied", "o_full", "o_done", "diff_done"):
            A_[nm], C_[nm] = sem("ab_" + nm), sem("cd_" + nm)

        ret_mv = region(MISC + 4.5, NT_X, 4, 2)

        def M(m, name):
            return sem(f"moe{m}_{name}")

        def more_passes(eng, m, one_pass):
            eng.wait_ge(stage_dve, STAGES.index(f"r{m}_experts"))
            n = eng.value_load(mo_npi[0:1, 0:1], min_val=1, max_val=NT_X)
            with eng.If(n > 1):
                with eng.Fori(1, n) as p:
                    one_pass(p)

        block = ctx.enter_context(nc.Block())

        @block.tensor
        def _(pe):
            state = dict(g=0, bank=0, mid=0, x_normed=0)
            read_n = {"act": 0, "dve": 0}
            last_group = [None] * 8

            def open_group(name, nb=1, by="dve"):
                if state["bank"] + nb > 8:
                    state["bank"] = 0
                b = state["bank"]
                state["bank"] = (b + nb) % 8
                for reader, s in free_by.items():
                    before = [g[1] for g in last_group[b:b + nb] if g and g[0] == reader]
                    if before:
                        pe.wait_ge(s, max(before))
                read_n[by] += 1
                for i in range(b, b + nb):
                    last_group[i] = (by, read_n[by])
                groups[name] = (state["g"], b, by, read_n[by])
                state["g"] += 1
                return b

            def close(ins):
                ins.then_inc(psum_full, 1)
                return ins

            def await_chunk(i):
                pe.wait_ge(*chunk_loaded(i))

            def read_group(name):
                await_read(pe, name)

            def await_x(n=1):
                state["x_normed"] += n
                pe.wait_ge(x_normed, state["x_normed"])

            def one_product(name, c, i, t, lhs, by):
                w, k, n = slot(i), chunks[i]["k"], chunks[i]["n"]
                b = open_group((name, c, t), 1, by)
                for kk in range(k):
                    ins = nc.tensor.matmul(psum[:, b, 0:n], lhs(t, kk), w[:, kk, :],
                                           start=kk == 0, stop=kk == k - 1)
                close(ins)

            def products(name, tl, lhs, by="dve"):
                for c, i in enumerate(by_name[name]):
                    await_chunk(i)
                    for t in tl:
                        one_product(name, c, i, t, lhs, by)
                    chunk_read[i] = (psum_full, state["g"])

            def tile_products(name, tl, lhs, by="dve", then=None):
                ids = by_name[name]
                for j, t in enumerate(tl):
                    for c, i in enumerate(ids):
                        if j == 0:
                            await_chunk(i)
                        one_product(name, c, i, t, lhs, by)
                        if j == len(tl) - 1:
                            chunk_read[i] = (psum_full, state["g"])
                    if then and j:
                        then(tl[j - 1])
                if then:
                    then(tl[-1])

            def turn_x(name):
                def then(t):
                    await_x()
                    if name:
                        transposes(name, [t], lambda t, k: X[:, t, tiles(k)], KD)
                return then

            def transposes(name, tl, src, n, per=8):
                for t in tl:
                    b = open_group((name, t), -(-n // 4))
                    for k in range(n):
                        ins = nc.tensor.transpose(flat(b, n * P)[:, tiles(k)], src(t, k), ident)
                    close(ins)

            def mod(l):
                def go():
                    pe.wait_ge(gate_ready := sem("c_ready"), l + 1)
                    for c, i in enumerate(by_name[f"mod{l}"]):
                        await_chunk(i)
                        b = open_group(("mod", l, c))
                        for k in range(KD):
                            ins = nc.tensor.matmul(psum[0:2, b, :], c_silu[:, k], slot(i)[:, k],
                                                   start=k == 0, stop=k == KD - 1)
                        close(ins)
                        chunk_read[i] = (psum_full, state["g"])
                return go

            def mod_t(l):
                def go():
                    b = open_group(("modT", l))
                    for j in range(48):
                        ins = nc.tensor.transpose(psum[:, b, 2 * j:2 * j + 2], mod_rows[:, tiles(j)], ident[0:2, 0:2])
                    close(ins)
                return go

            def gated(name, w_cols, ntok, col0):
                for c, i in enumerate(by_name[name]):
                    await_chunk(i)
                    w = slot(i)
                    for j in range(2):
                        b = open_group((name, 2 * c + j), 2)
                        for part in range(2):
                            for k in range(KD):
                                ins = nc.tensor.matmul(psum[:, b + part, 0:ntok],
                                                       w[:, k, part * 256 + j * P:part * 256 + j * P + P],
                                                       HT[:, k, col0:col0 + ntok], start=k == 0, stop=k == KD - 1)
                        close(ins)
                    chunk_read[i] = (psum_full, state["g"])

            def three_passes(out, aL, aH, bL, bH, start, stop):
                nc.tensor.matmul(out, aH, bH, start=start, stop=False)
                nc.tensor.matmul(out, aH, bL, start=False, stop=False)
                return nc.tensor.matmul(out, aL, bH, start=False, stop=stop)

            def gated_split(name, ntok, col0):
                for c, i in enumerate(by_name[name]):
                    if c:
                        pe.wait_ge(split_low, split_at[name, ("w", i, None)])
                    w, wH = slot(i, rounded=True), slot_high(i)
                    for j in range(2):
                        b = open_group((name, 2 * c + j), 2)
                        for part in range(2):
                            cols = slice(part * 256 + j * P, part * 256 + j * P + P)
                            for k in range(KD):
                                if c == j == part == 0:
                                    pe.wait_ge(split_low, split_at[name, ("w", i, k)])
                                ins = three_passes(psum[:, b + part, 0:ntok], w[:, k, cols], wH[:, k, cols],
                                                   ffn_xL[:, k, col0:col0 + ntok], ffn_xH[:, k, 0:ntok],
                                                   k == 0, k == KD - 1)
                        close(ins)
                    chunk_read[i] = (psum_full, state["g"])

            def products_split(name, tl, by):
                for c, i in enumerate(by_name[name]):
                    if c:
                        pe.wait_ge(split_low, split_at[name, ("w", i, None)])
                    w, wH, n = slot(i, rounded=True), slot_high(i), chunks[i]["n"]
                    for t in tl:
                        b = open_group((name, c, t), 1, by)
                        for k in range(KD):
                            if c == 0 and t == tl[0]:
                                pe.wait_ge(split_low, split_at[name, ("w", i, k)])
                            ins = three_passes(psum[:, b, 0:n], ffn_xL[:, k, tiles(t)],
                                               ffn_xH[:, k, tiles(t - NT_C)], w[:, k], wH[:, k], k == 0, k == KD - 1)
                        close(ins)
                    chunk_read[i] = (psum_full, state["g"])

            def summed(name, tl, then):
                banks = [(j, half, open_group((name, half, t))) for j, t in enumerate(tl) for half in range(2)]
                k = 0
                for i in by_name[name]:
                    pe.wait_ge(split_low, split_at[name, ("w", i, None)])
                    w, wH = slot(i, rounded=True), slot_high(i)
                    for kk in range(chunks[i]["k"]):
                        pe.wait_ge(split_low, split_at[name, ("h", k)])
                        for j, half, b in banks:
                            cols = slice(512 * half, 512 * half + 512)
                            ins = three_passes(psum[:, b, :], ffn_hL[:, k, tiles(j)], ffn_hH[:, k % 4, tiles(j)],
                                               w[:, kk, cols], wH[:, kk, cols], k == 0, k == KF - 1)
                            if k == KF - 1:
                                close(ins)
                        if k < KF - 1:
                            ins.then_inc(w_used, 1)
                            state["mid"] += 1
                        hidden_read[name, k] = (w_used, state["mid"])
                        k += 1
                    chunk_read[i] = (psum_full, state["g"]) if k == KF else (w_used, state["mid"])
                for t in tl:
                    then(t)

            def ffn(f, tl, following=None):
                return {
                    f"{f}_in": lambda: gated_split(f"{f}_in", len(tl) * P, tl[0] * P),
                    f"{f}_out": lambda: summed(f"{f}_out", tl, turn_x(following)),
                }

            def ab_tr():
                transposes("ab_q", ALL, lambda t, k: ab_qk[:, t, tiles(k)], 6)
                transposes("ab_k", ALL, lambda t, k: ab_kd[:, t, tiles(k)], 4)

            def ab_att():
                s, n = A_, len(AB_UNITS)

                def scores(u):
                    if u >= n:
                        return
                    h, t = AB_UNITS[u]
                    kv, nk = h // 3, ab_keys(t) * P
                    if u >= 2:
                        pe.wait_ge(s["exp_done"], u - 1)
                    for c0 in range(0, nk, 512):
                        c1 = min(c0 + 512, nk)
                        ins = nc.tensor.matmul(flat(2 * (u % 2), nk)[:, c0:c1], ab_qT[:, h // 2, tiles(t)],
                                               ab_kT[:, kv, h % 2, c0:c1], start=True, stop=True)
                    ins.then_inc(s["score_full"], 1)

                scores(0)
                scores(1)
                for u, (h, t) in enumerate(AB_UNITS):
                    nk = ab_keys(t)
                    pe.wait_ge(s["exp_done"], u + 1)
                    if u >= 1:
                        pe.wait_ge(s["pt_copied"], u)
                    for k in range(nk):
                        ins = nc.tensor.transpose(flat(4, 768)[:, tiles(k)], att_P[:, u % 2, tiles(k)], ident)
                    ins.then_inc(s["pt_full"], 1)
                    scores(u + 2)
                    pe.wait_ge(s["pt_copied"], u + 1)
                    if u >= 2:
                        pe.wait_ge(s["o_done"], u - 1)
                    for k in range(nk):
                        ins = nc.tensor.matmul(psum[:, 6 + u % 2, 0:HD], att_PT[:, u % 2, tiles(k)],
                                               ab_vu[:, k, HD * (h // 3):HD * (h // 3) + HD],
                                               start=k == 0, stop=k == nk - 1)
                    ins.then_inc(s["o_full"], 1)

            def ab_pool():
                wait_loads(pe, "ab_pool")
                ids = by_name["ab_pool"]
                for who, tl, cs in (("x", TILES_X, ids[:2]), ("c", TILES_C, ids[2:])):
                    nt = len(tl)
                    for g in range(4):
                        i = cs[g * len(cs) // 4]
                        if g % (4 // len(cs)) == 0:
                            await_chunk(i)
                        b = open_group(("pooled", who, g))
                        for kt in range(nt):
                            ins = nc.tensor.matmul(psum[0:64, b, 0:nt * P],
                                                   ab_vu[:, tl[0] + kt, 256 + g * 64:320 + g * 64],
                                                   slot(i)[:, (g % (4 // len(cs))) * nt + kt, :],
                                                   start=kt == 0, stop=kt == nt - 1)
                        close(ins)
                        chunk_read[i] = (psum_full, state["g"])
                    for g in range(4):
                        read_group(("pooled", who, g))
                    for t in tl:
                        b = open_group(("mixed", t))
                        for g in range(4):
                            ins = nc.tensor.matmul(psum[:, b, g * 64:g * 64 + 64], pooledT[:, g, tiles(t - tl[0])],
                                                   w_pool[:, g], start=True, stop=True)
                        close(ins)

            def cd_u():
                wait_loads(pe, "cd_u")
                b = open_group("conv_w")
                for j in range(2):
                    ins = nc.tensor.transpose(psum[:, b, 32 * j:32 * j + 32], cd_wrow[:, tiles(j)], ident[0:32, 0:32])
                close(ins)
                gated("cd_u", None, SEQ, NT_C * P)

            def cd_conv_v():
                products("cd_v", ALL, lambda t, k: HT[:, k, tiles(t)], "act")
                pe.wait_ge(sem("conv_done"), 1)
                for t in range(NT_X):
                    b = open_group(("conv", t))
                    for j in range(2):
                        ins = nc.tensor.transpose(psum[:, b, tiles(j)], cd_acc[:, j, tiles(t)], ident)
                    close(ins)

            def cd_att():
                s, n = C_, 2 * len(CD_UNITS)
                NK = NT * P

                def scores(v):
                    if v >= n:
                        return
                    h, t = CD_UNITS[v // 2]
                    if v >= 2:
                        pe.wait_ge(s["exp_done"], v - 1)
                    for c0 in range(0, NK, 512):
                        c1 = min(c0 + 512, NK)
                        ins = nc.tensor.matmul(flat(2 * (v % 2), NK)[:, c0:c1], cd_qT[:, h, v % 2, tiles(t)],
                                               cd_kT[:, h, c0:c1], start=True, stop=True)
                    ins.then_inc(s["score_full"], 1)

                scores(0)
                scores(1)
                for u, (h, t) in enumerate(CD_UNITS):
                    scores(2 * u + 2)
                    pe.wait_ge(s["diff_done"], u + 1)
                    if u >= 1:
                        pe.wait_ge(s["pt_copied"], u)
                    for k in range(NT):
                        ins = nc.tensor.transpose(flat(4, 768)[:, tiles(k)], cd_P[:, 2 * u % 4, tiles(k)], ident)
                    ins.then_inc(s["pt_full"], 1)
                    scores(2 * u + 3)
                    pe.wait_ge(s["pt_copied"], u + 1)
                    if u >= 2:
                        pe.wait_ge(s["o_done"], u - 1)
                    for k in range(NT):
                        ins = nc.tensor.matmul(psum[:, 6 + u % 2, 0:P], cd_PT[:, u % 2, tiles(k)],
                                               cd_v[:, k, tiles(h)], start=k == 0, stop=k == NT - 1)
                    ins.then_inc(s["o_full"], 1)

            def ev_tr():
                R = range(NT_X)
                transposes("ev_qa", R, lambda t, k: ev_qa[:, t, tiles(k)], 4)
                transposes("ev_ka", R, lambda t, k: ev_ka[:, t, tiles(k)], 4)
                transposes("ev_qb", R, lambda t, k: ev_qb[:, t, tiles(k)], 4)
                transposes("ev_kb", R, lambda t, k: ev_kbd[:, t, tiles(k)], 2)

            def ev_ret():
                for h in range(4):
                    for mt in range(NT_X):
                        b = open_group(("ret_s", h, mt))
                        close(nc.tensor.matmul(psum[:, b, :], ev_kaT[:, h, tiles(mt)], ev_qaT[:, h, :],
                                               start=True, stop=True))
                    read_group(("ret_s", h, NT_X - 1))
                    for t in range(NT_X):
                        b = open_group(("ret_y", h, t))
                        for mt in range(NT_X):
                            ins = nc.tensor.matmul(psum[:, b, 0:P], ev_ST[:, mt, tiles(t)], ev_va[:, mt, tiles(h)],
                                                   start=mt == 0, stop=mt == NT_X - 1)
                        close(ins)

            def ev_win():
                def scores(u):
                    if u >= len(WIN_UNITS):
                        return
                    h, t = WIN_UNITS[u]
                    ks, lo = win_keys(t), 64 * (h % 2)
                    b = open_group(("win_s", u))
                    close(nc.tensor.matmul(psum[:, b, 0:len(ks) * P], ev_qbT[lo:lo + 64, h // 2, tiles(t)],
                                           ev_kbT[lo:lo + 64, h // 4, tiles(ks[0], len(ks))], start=True, stop=True))

                def output(u):
                    h, t = WIN_UNITS[u]
                    ks = win_keys(t)
                    read_group(("win_pt", u))
                    b = open_group(("win_o", u))
                    for k, kt in enumerate(ks):
                        ins = nc.tensor.matmul(psum[:, b, 0:HD], ev_PT[:, u % 2, tiles(k)],
                                               ev_kv[:, kt, P + HD * (h // 4):P + HD * (h // 4) + HD],
                                               start=k == 0, stop=k == len(ks) - 1)
                    close(ins)

                scores(0)
                scores(1)
                for u, (h, t) in enumerate(WIN_UNITS):
                    ks = win_keys(t)
                    pe.wait_ge(sem("win_exp_done"), u + 1)
                    b = open_group(("win_pt", u))
                    for k in range(len(ks)):
                        ins = nc.tensor.transpose(psum[:, b, tiles(k)], ev_P[:, u % 2, tiles(k)], ident)
                    close(ins)
                    scores(u + 2)
                    if u:
                        output(u - 1)
                output(len(WIN_UNITS) - 1)

            def fo_dft():
                i = by_name["fo_dft"][0]
                await_chunk(i)
                for t in range(NT_X):
                    for g in range(4):
                        b = open_group(("fo_dft", t, g), 1, "act")
                        for k in range(2):
                            ins = nc.tensor.matmul(psum[:, b, :], HT[:, 2 * g + k, tiles(NT_C + t)], slot(i)[:, k],
                                                   start=k == 0, stop=k == 1)
                        close(ins)
                chunk_read[i] = (psum_full, state["g"])

            def fo_seq():
                i = by_name["fo_seq"][0]
                await_chunk(i)
                for d in range(KD):
                    b = open_group(("fo_seq", d), 1, "act")
                    for part in range(2):
                        for t in range(NT_X):
                            ins = nc.tensor.matmul(
                                psum[:, b, :], fo_AB[:, t, d // 2, part * 256 + (d % 2) * P:part * 256 + (d % 2) * P + P],
                                slot(i)[:, part * NT_X + t], start=part + t == 0, stop=part + t == NT_X)
                    close(ins)
                chunk_read[i] = (psum_full, state["g"])

            def route(m):
                def go():
                    wait_loads(pe, f"r{m}_route")
                    b = open_group(("logits", m))
                    for t in range(NT_X):
                        for k in range(KD):
                            ins = nc.tensor.matmul(psum[:, b, 36 * t:36 * t + 36], HT[:, k, tiles(NT_C + t)],
                                                   mo_wr[:, k], start=k == 0, stop=k == KD - 1)
                    close(ins)
                    pe.wait_ge(M(m, "picked"), 1)
                    b = open_group(("rank", m))
                    for t in range(NT_X):
                        for s in range(t + 1):
                            ins = nc.tensor.matmul(psum[:, b, NE * t:NE * t + NE], mo_before[:, int(s < t)],
                                                   mo_A[:, s], start=s == 0, stop=s == t)
                    for s in range(NT_X):
                        ins = nc.tensor.matmul(psum[:, b, NE * NT_X:NE * NT_X + NE], mo_before[:, 1], mo_A[:, s],
                                               start=s == 0, stop=s == NT_X - 1)
                    close(ins)
                return go

            def experts(m):
                def one_pass(p):
                    for e in range(NE):
                        pe.wait_ge(M(m, "sel_ready"), NE * p + e + 1)
                        for t in range(NT_X):
                            ins = nc.tensor.matmul(psum[:, 7, 4 * e:4 * e + 4], mo_sel[:, 4 * (e % 2) + t],
                                                   mo_F[:, t, e], start=t == 0, stop=t == NT_X - 1)
                        ins.then_inc(M(m, "sel_used"), 1)

                    def turn_x(xg_n, b):
                        pe.wait_ge(M(m, f"xg_ready{b}"), xg_n * 16)
                        for k in range(KD):
                            ins = nc.tensor.transpose(flat(2, D)[:, tiles(k)], mo_xg[:, b, tiles(k)], ident)
                        ins.then_inc(M(m, "xt_full"), 1)

                    def gate_or_value(i, b, part):
                        w = region(MOE_RING_KB[3 * b + part], KD, 512)
                        pe.wait_ge(M(m, f"w_ready{3 * b + part}"), ((NE // 2) * p + i + 1) * 16)
                        for k in range(KD):
                            ins = nc.tensor.matmul(psum[:, part, :], mo_xgT[:, k], w[:, k],
                                                   start=k == 0, stop=k == KD - 1)
                        ins.then_inc(M(m, ("g_full", "gu_full")[part]), 1)

                    def gate(i, b):
                        pe.wait_ge(M(m, "xgT_ready"), (NE + 1) * p + i * 2 + b + 1)
                        pe.wait_ge(M(m, "gu_free"), NE * p + i * 2 + b + 1)
                        gate_or_value(i, b, 0)

                    def two_experts(i, last):
                        for b in range(2):
                            e = NE * p + i * 2 + b
                            gate_or_value(i, b, 1)
                            turn_x((17 * p + i + 2) if b == 1 else (16 * p + i + 1), 1 - b)
                            pe.wait_ge(M(m, "h_ready"), e + 1)
                            for k in range(4):
                                ins = nc.tensor.transpose(psum[:, 4, tiles(k)], mo_h[:, tiles(k)], ident)
                            ins.then_inc(M(m, "ht_full"), 1)
                            if b == 0:
                                gate(i, 1)
                            elif not last:
                                gate(i + 1, 0)
                            pe.wait_ge(M(m, "hT_ready"), e + 1)
                            pe.wait_ge(M(m, "y_free"), e + 1)
                            pe.wait_ge(M(m, f"w_ready{3 * b + 2}"), ((NE // 2) * p + i + 1) * 16)
                            w = region(MOE_RING_KB[3 * b + 2], 4, D)
                            for half in range(2):
                                for k in range(4):
                                    ins = nc.tensor.matmul(psum[:, 5 + half, :], mo_hT[:, k],
                                                           w[:, k, half * 512:half * 512 + 512],
                                                           start=k == 0, stop=k == 3)
                            ins.then_inc(M(m, "y_full"), 1)

                    turn_x(17 * p + 1, 0)
                    gate(0, 0)
                    with pe.Fori(0, NE // 2 - 1) as i:
                        two_experts(i, False)
                    two_experts(NE // 2 - 1, True)

                def go():
                    one_pass(0)
                    more_passes(pe, m, one_pass)
                return go

            def heads(name, t0):
                def then(t):
                    pe.wait_ge(sem(name + "_roped"), 1 + t - t0)
                    transposes(name, [t], lambda t, k: cd_tmp[:, t % 4, tiles(k)], 6)
                return then

            steps = {
                "mod0": mod(0), "modT0": mod_t(0), "mod1": mod(1), "modT1": mod_t(1),
                "ab_ht": lambda: transposes("ab_ht", ALL, lambda t, k: X[:, t, tiles(k)], KD),
                "ab_in": lambda: tile_products("ab_in", ALL, lambda t, k: HT[:, k, tiles(t)], "act"),
                "ab_tr": ab_tr, "ab_att": ab_att, "ab_pool": ab_pool,
                "ab_ot": lambda: transposes("ab_ot", ALL, lambda t, k: O_all[:, t, tiles(k)], KD),
                "ab_out": lambda: tile_products("ab_out", ALL, lambda t, k: OT_ab[:, k, tiles(t)], "dve",
                                                turn_x("ab_out_t")),
                **ffn("f0x", TILES_X), **ffn("f0c", TILES_C), **ffn("f1x", TILES_X, "f1x_out_t"),
                "cd_ht": lambda: transposes("cd_ht", ALL, lambda t, k: X[:, t, tiles(k)], KD),
                "cd_u": cd_u, "cd_conv": cd_conv_v,
                "cd_q": lambda: tile_products("cd_q", TILES_X, lambda t, k: HT[:, k, tiles(t)], "act",
                                              heads("cd_qt", NT_C)),
                "cd_k": lambda: tile_products("cd_k", ALL, lambda t, k: HT[:, k, tiles(t)], "act",
                                              heads("cd_kt", 0)),
                "cd_att": cd_att,
                "cd_ot": lambda: transposes("cd_ot", TILES_X, lambda t, k: O4[:, t - NT_C, tiles(k)], KD),
                "cd_out": lambda: tile_products("cd_out", TILES_X, lambda t, k: OT_cd[:, k, tiles(t - NT_C)], "dve",
                                                turn_x("cd_out_t")),
                "ev_in": lambda: products_split("ev_in", TILES_X, "act"),
                "ev_tr": ev_tr, "ev_ret": ev_ret, "ev_win": ev_win,
                "ev_ot": lambda: transposes("ev_ot", TILES_X, lambda t, k: O4[:, t - NT_C, tiles(k)], KD),
                "ev_out": lambda: tile_products("ev_out", TILES_X, lambda t, k: OT_ev[:, k, tiles(t - NT_C)], "dve",
                                                turn_x("ev_out_t")),
                "fo_dft": fo_dft, "fo_seq": fo_seq,
                "fo_out": lambda: tile_products("fo_out", TILES_X, lambda t, k: fo_YT[:, k, tiles(t - NT_C)], "dve",
                                                turn_x("fo_out_t")),
                "r0_norm": lambda: [turn_x("r0_norm_t")(t) for t in TILES_X],
                "r1_norm": lambda: [turn_x(None)(t) for t in TILES_X],
            }
            for m in range(2):
                steps[f"r{m}_route"] = route(m)
                steps[f"r{m}_experts"] = experts(m)
            pe.wait_ge(sem("ident_loaded"), 16)
            pe.wait_ge(sem("x_loaded"), 16 * NT)
            run(pe, steps)

        @block.scalar
        def _(act):
            link = Link(act, act_chain)

            free = free_by["act"]

            def await_group(name):
                act.wait_ge(psum_full, groups[name][0] + 1)
                return groups[name][3], groups[name][1]

            def take(name, dst, n):
                g, b = await_group(name)
                src = flat(b, n)
                if len(dst.shape) == 3:
                    src = src.rearrange("p (a c) -> p a c", a=dst.shape[1])
                link(nc.scalar.activation(dst, src, ACT.Copy), free, g)

            def roots(n, times=1):
                def go():
                    for _ in range(times):
                        k = link.n.get("sqrt_done", 0)
                        act.wait_ge(stat_ready, k + 1)
                        v = n if not callable(n) else n()
                        link(nc.scalar.activation(v, v, ACT.Sqrt), sqrt_done)
                return go

            def mod(l):
                def go():
                    wait_loads(act, f"mod{l}")
                    for who in range(2):
                        link(nc.scalar.activation(c_silu[:, :, who], c_cols[:, who], ACT.Silu),
                             None if who == 0 else sem("c_ready"))
                return go

            def gate_of(name, func, sg, ntok, j):
                g, b = await_group((name, j))
                if j >= 2:
                    await_read(act, (name, j - 2))
                link(nc.scalar.activation(sg[:, j % 2, 0:ntok], psum[:, b + 1, 0:ntok], func), gate_done)

            def gate(name, func, sg, ntok, n):
                return lambda: [gate_of(name, func, sg, ntok, j) for j in range(n)]

            def high_part(stage, piece):
                if piece[0] == "w" and not piece[2]:
                    i = piece[1]
                    act.wait_ge(*chunk_loaded(i))
                    before = [c for c in by_name[stage] if c < i and chunks[c]["high"] == chunks[i]["high"]]
                    if before:
                        act.wait_ge(*chunk_read[before[-1]])
                if piece[0] == "h" and piece[1] >= 4:
                    act.wait_ge(*hidden_read[stage, piece[1] - 4])
                full, high, _ = piece_views(stage, piece)
                link(nc.scalar.activation(high, full, ACT.Copy), split_high)

            def ffn_in(name, ntok):
                def go():
                    for piece in split_order[name]:
                        if piece[0] == "work":
                            gate_of(name, ACT.Silu, ffn_sg, ntok, piece[1])
                        else:
                            high_part(name, piece)
                return go

            def ffn_out(name, tl):
                def go():
                    for piece in split_order[name]:
                        high_part(name, piece)
                    norms(tl)()
                return go

            def ab_in():
                for t in ALL:
                    for c in range(3):
                        take(("ab_in", c, t), ab_qk[:, t, 512 * c:512 * c + 512] if c < 2 else ab_vu[:, t], 512)
                    roots(rstd[:, t])()

            def ab_att():
                s = A_

                def exps(u):
                    if u >= len(AB_UNITS):
                        return
                    n = ab_keys(AB_UNITS[u][1]) * P
                    act.wait_ge(s["max_done"], u + 1)
                    link(nc.scalar.activation(att_P[:, u % 2, 0:n], flat(2 * (u % 2), n), ACT.Exp,
                                              bias=nmx[:, u % 4:u % 4 + 1], scale=HD ** -0.5,
                                              accum_out=esum[:, u % 4:u % 4 + 1]), s["exp_done"])

                exps(0)
                exps(1)
                for u, (h, t) in enumerate(AB_UNITS):
                    n = ab_keys(t) * P
                    act.wait_ge(s["pt_full"], u + 1)
                    link(nc.scalar.activation(att_PT[:, u % 2, 0:n], flat(4, n), ACT.Copy), s["pt_copied"])
                    exps(u + 2)

            def cd_att():
                s, n = C_, NT * P
                for i in range(2):
                    act.wait_ge(sem("lam_sum"), i + 1)
                    link(nc.scalar.activation(lam[:, i:i + 1], lam[:, i:i + 1], ACT.Exp), sem("lam_exp"))

                def exps(v):
                    if v >= 2 * len(CD_UNITS):
                        return
                    act.wait_ge(s["max_done"], v + 1)
                    link(nc.scalar.activation(cd_P[:, v % 4], flat(2 * (v % 2), n), ACT.Exp,
                                              bias=nmx[:, v % 8:v % 8 + 1], scale=HD ** -0.5,
                                              accum_out=esum[:, v % 8:v % 8 + 1]), s["exp_done"])

                exps(0)
                exps(1)
                for u in range(len(CD_UNITS)):
                    act.wait_ge(s["pt_full"], u + 1)
                    link(nc.scalar.activation(cd_PT[:, u % 2], flat(4, n), ACT.Copy), s["pt_copied"])
                    exps(2 * u + 2)
                    exps(2 * u + 3)

            def cd_conv_():
                for c, w in enumerate((512, 256)):
                    for t in ALL:
                        take(("cd_v", c, t), cd_v[:, t, 512 * c:512 * c + w], w)
                roots(rstd[:, 0:NT_X, 0])()
                act.wait_ge(sem("conv_normed"), 1)
                link(nc.scalar.activation(cd_conv, cd_conv, ACT.Silu))

            def cd_proj(name, tl, turned):
                def go():
                    for t in tl:
                        if t - tl[0] >= 4:
                            act.wait_ge(psum_full, groups[(turned, t - 4)][0] + 1)
                        for c, w in enumerate((512, 256)):
                            take((name, c, t), cd_tmp[:, t % 4, 512 * c:512 * c + w], w)
                return go

            def ev_in():
                for piece in split_order["ev_in"]:
                    if piece[0] != "work":
                        high_part("ev_in", piece)
                        continue
                    c = piece[1]
                    for t in range(NT_X):
                        take(("ev_in", c, NT_C + t), (ev_qa, ev_ka, ev_va, ev_ga, ev_qb, ev_kv)[c][:, t],
                             512 if c < 5 else 256)

            def ev_ret():
                act.wait_ge(sem("decay_abs"), 1)
                link(nc.scalar.activation(lg[:, 1], lg[:, 0], ACT.Exp, scale=-1.0), sem("decay_exp"))
                for h in range(4):
                    act.wait_ge(sem("decay_arg"), h + 1)
                    link(nc.scalar.activation(ev_D[h % 2], ev_D[h % 2], ACT.Exp), sem("decay_done"))
                roots(rstd[:, 0:NT_X, 0:4])()
                link(nc.scalar.activation(ev_ga, ev_ga, ACT.Silu), sem("ret_gate"))

            def ev_win():
                for u, (h, t) in enumerate(WIN_UNITS):
                    n = len(win_keys(t)) * P
                    act.wait_ge(sem("win_max_done"), u + 1)
                    link(nc.scalar.activation(ev_P[:, u % 2, 0:n], ev_Sm[:, u % 2, 0:n], ACT.Exp,
                                              bias=nmx[:, u % 4:u % 4 + 1], accum_out=esum[:, u % 4:u % 4 + 1]))
                    link(nc.scalar.activation(esum[:, 4 + u % 4:5 + u % 4], ev_Sm[:, u % 2, n:n + 1], ACT.Exp,
                                              bias=nmx[:, u % 4:u % 4 + 1]), sem("win_exp_done"))

            def fo_dft():
                for t in range(NT_X):
                    for g in range(4):
                        take(("fo_dft", t, g), fo_AB[:, t, g], 512)

            def fo_seq():
                for d in range(KD):
                    take(("fo_seq", d), fo_YT[:, d], 512)

            def route(m):
                def go():
                    act.wait_ge(M(m, "coarse_shifted"), 1)
                    link(nc.scalar.activation(mo_C8[:, :, 0:4], mo_C8[:, :, 0:4], ACT.Exp), M(m, "coarse_exp"))
                    act.wait_ge(M(m, "fine_diff"), 1)
                    link(nc.scalar.activation(mo_s[:, 3], mo_s[:, 2], ACT.Exp), M(m, "fine_exp"))
                return go

            def experts(m):
                chain = Link(act, M(m, "act_chain"))

                def one_pass(p):
                    def turned_x():
                        chain(nc.scalar.activation(mo_xgT, flat(2, D).rearrange("p (a c) -> p a c", a=KD), ACT.Copy),
                              M(m, "xgT_ready"))

                    chain.n = {}
                    chain.at = {M(m, "xgT_ready").name: p * (NE + 1)}
                    act.wait_ge(M(m, "xt_full"), p * (NE + 1) + 1)
                    turned_x()
                    with act.Fori(0, NE // 2) as i:
                        chain.n = {}
                        chain.at = {M(m, "xgT_ready").name: p * (NE + 1) + i * 2 + 1,
                                    M(m, "sg_done").name: p * NE + i * 2, M(m, "hT_ready").name: p * NE + i * 2}
                        for b in range(2):
                            e = p * NE + i * 2 + b
                            act.wait_ge(M(m, "g_full"), e + 1)
                            chain(nc.scalar.activation(mo_sg, psum[:, 0, :], ACT.Silu), M(m, "sg_done"))
                            act.wait_ge(M(m, "xt_full"), p * (NE + 1) + i * 2 + b + 2)
                            turned_x()
                            act.wait_ge(M(m, "ht_full"), e + 1)
                            chain(nc.scalar.activation(mo_hT, psum[:, 4, :].rearrange("p (a c) -> p a c", a=4),
                                                       ACT.Copy), M(m, "hT_ready"))

                def go():
                    one_pass(0)
                    more_passes(act, m, one_pass)
                return go

            def norms(tl):
                def go():
                    for j in range(len(tl)):
                        roots(rstd[:, j, 0:1])()
                return go

            steps = {
                "mod0": mod(0), "mod1": mod(1), "ab_in": ab_in, "ab_att": ab_att,
                "f0x_in": ffn_in("f0x_in", SEQ), "f0c_in": ffn_in("f0c_in", CTX), "f1x_in": ffn_in("f1x_in", SEQ),
                "cd_u": gate("cd_u", ACT.Sigmoid, cd_sg, SEQ, 2), "cd_conv": cd_conv_,
                "cd_q": cd_proj("cd_q", TILES_X, "cd_qt"), "cd_k": cd_proj("cd_k", ALL, "cd_kt"),
                "cd_att": cd_att, "cd_sub": roots(rstd[:, 0:NT_X, 0:6]),
                "ev_in": ev_in, "ev_ret": ev_ret, "ev_win": ev_win,
                "fo_dft": fo_dft, "fo_seq": fo_seq,
                "r0_route": route(0), "r1_route": route(1), "r0_experts": experts(0), "r1_experts": experts(1),
                "ab_out": norms(ALL), "f0x_out": ffn_out("f0x_out", TILES_X), "f0c_out": ffn_out("f0c_out", TILES_C), "cd_out": norms(TILES_X),
                "f1x_out": ffn_out("f1x_out", TILES_X), "ev_out": norms(TILES_X), "fo_out": norms(TILES_X),
                "r0_norm": norms(TILES_X), "r1_norm": norms(TILES_X),
            }
            run(act, steps, stage_act)

        @block.vector
        def _(dve):
            link = Link(dve, dve_chain)
            V = nc.vector

            free = free_by["dve"]

            def await_group(name):
                dve.wait_ge(psum_full, groups[name][0] + 1)
                return groups[name][3], groups[name][1]

            def over(v, n):
                return v.unsqueeze(1).broadcast_to([P, n, v.shape[1]])

            def per(v, n):
                return v.unsqueeze(2).broadcast_to([P, v.shape[1], n])

            def take(name, dst, n, parts=P):
                g, b = await_group(name)
                src = flat(b, n)[0:parts]
                if len(dst.shape) == 3:
                    src = src.rearrange("p (a c) -> p a c", a=dst.shape[1])
                link(V.tensor_copy(dst, src), free, g)

            def mod(l):
                def go():
                    wait_loads(dve, f"mod{l}")
                    for c in range(12):
                        g, b = await_group(("mod", l, c))
                        link(V.tensor_tensor(mod_rows[:, 512 * c:512 * c + 512], psum[0:2, b, :],
                                             ada_bias[:, 512 * c:512 * c + 512], ALU.add), free, g)
                return go

            def mod_t(l):
                def go():
                    take(("modT", l), mod_cols, 96)
                    for k in (8, 32):
                        link(V.tensor_scalar(mod_cols[:, k:k + 8], mod_cols[:, k:k + 8], 1.0, None, ALU.add))
                return go

            def modulate(name, shift):
                def one(t):
                    g, b = await_group((name, t))
                    who = int(t < NT_C)
                    for k in range(KD):
                        ins = V.tensor_scalar(HT[:, k, tiles(t)], flat(b, D)[:, tiles(k)],
                                              mod_cols[:, shift + 8 + k, who:who + 1],
                                              mod_cols[:, shift + k, who:who + 1], ALU.mult, ALU.add)
                    link(ins, free, g)
                return one

            def modulated(name, tl, shift):
                return lambda: [modulate(name, shift)(t) for t in tl]

            def copied(name):
                return lambda t: take((name, t), HT[:, :, tiles(t)], D)

            def plain(name, tl, dst, n, t0=0):
                def go():
                    for t in tl:
                        take((name, t), dst[:, :, tiles(t - t0)], n)
                return go

            def root_of(v, count, eps, src=None):
                link(V.tensor_scalar(v, v if src is None else src, 1.0 / count, eps, ALU.mult, ALU.add), stat_ready)
                dve.wait_ge(sqrt_done, link.n["stat_ready"])
                link(V.reciprocal(v, v))

            def statistics(src, slot_, n):
                for j in range(-(-n // 512)):
                    link(V.bn_stats(stat[:, slot_, j], src[:, 512 * j:min(512 * j + 512, n)]))
                link(V.bn_aggr(mv[:, slot_], stat[:, slot_, 0:-(-n // 512)]))

            def norm_tile(j, t, rows, eps):
                statistics(X[:, t], j, D)
                root_of(rstd[:, j, 0:1], 1.0, eps, mv[:, j, 1:2])
                link(V.tensor_scalar(X[:, t], X[:, t], mv[:, j, 0:1], rstd[:, j, 0:1], ALU.subtract, ALU.mult))
                link(V.tensor_tensor(X[:, t], X[:, t], rows.g, ALU.mult))
                link(V.tensor_tensor(X[:, t], X[:, t], rows.b, ALU.add), x_normed)

            def out_norm(name, tl, rows, eps, gates, following=None):
                def residual(half, t, n):
                    g, b = await_group((name, half, t))
                    cols = slice(512 * half, 512 * half + 512)
                    if gates:
                        row_ = rows.gate[len(rows.gate) - 1 if t < NT_C else 0]
                        link(V.tensor_tensor(rows.tmp[:, n % 2], psum[:, b, :], row_[:, cols], ALU.mult), free, g)
                        link(V.scalar_tensor_tensor(X[:, t, cols], X[:, t, cols], ALPHA, rows.tmp[:, n % 2],
                                                    ALU.mult, ALU.add))
                    else:
                        link(V.scalar_tensor_tensor(X[:, t, cols], X[:, t, cols], ALPHA, psum[:, b, :],
                                                    ALU.mult, ALU.add), free, g)

                def go():
                    for piece in split_order.get(name, []):
                        low_part(name, piece)
                    wait_loads(dve, name)
                    split = name in split_order
                    for t in tl if split else []:
                        residual(0, t, 0)
                        residual(1, t, 1)
                    for j, t in enumerate(tl):
                        if not split:
                            residual(0, t, 0)
                            residual(1, t, 1)
                        norm_tile(j, t, rows, eps)
                        if following and j:
                            following(tl[j - 1])
                    if following:
                        following(tl[-1])
                return go

            def low_part(stage, piece):
                full, high, low = piece_views(stage, piece)
                dve.wait_ge(split_high, split_at[stage, piece])
                link(V.tensor_tensor(low, full, high.bitcast(F32), ALU.subtract), split_low)

            def product(f, n_tok):
                def go():
                    for piece in split_order[f"{f}_in"]:
                        if piece[0] != "work":
                            low_part(f"{f}_in", piece)
                            continue
                        j = piece[1]
                        g, b = await_group((f"{f}_in", j))
                        dve.wait_ge(gate_done, gate_base[f] + j + 1)
                        link(V.tensor_tensor(ffn_hT[:, j, 0:n_tok], psum[:, b, 0:n_tok], ffn_sg[:, j % 2, 0:n_tok],
                                             ALU.mult), free, g)
                return go

            gate_base = dict(f0x=0, f0c=KF, cd_u=2 * KF, f1x=2 * KF + 2)

            def rotate(x, table, heads, axes, half, ta, tb, signal=None):
                w = axes * 2 * half
                n = heads * w
                cos, sin = table[:, 0:w], table[:, w:2 * w]
                x3 = x.rearrange("p (h w) -> p h w", w=w)
                a3, b3 = (v[:, 0:n].rearrange("p (h w) -> p h w", w=w) for v in (ta, tb))
                link(V.tensor_tensor(a3, x3, over(cos, heads), ALU.mult))
                for ax in range(axes):
                    for s in range(2):
                        at = ax * 2 * half + s * half
                        of = ax * 2 * half + (1 - s) * half
                        link(V.tensor_tensor(b3[:, :, at:at + half], x3[:, :, of:of + half],
                                             over(sin[:, at:at + half], heads), ALU.mult))
                link(V.tensor_tensor(x, ta[:, 0:n], tb[:, 0:n], ALU.add), signal)

            def ab_rope():
                wait_loads(dve, "ab_in")
                for t in ALL:
                    await_read(dve, ("ab_in", 2, t))
                    link(V.tensor_tensor(tmp_a, ab_qk[:, t], ab_qk[:, t], ALU.mult))
                    link(V.reduce_sum(rstd[:, t], tmp_a.rearrange("p (h d) -> p h d", d=HD), axis=AX.X))
                    root_of(rstd[:, t], HD, EPS)
                    x3 = ab_qk[:, t].rearrange("p (h d) -> p h d", d=HD)
                    link(V.tensor_tensor(x3, x3, per(rstd[:, t], HD), ALU.mult))
                    link(V.tensor_tensor(x3[:, 0:12], x3[:, 0:12], over(qk_gain[:, 0], 12), ALU.mult))
                    link(V.tensor_tensor(x3[:, 12:16], x3[:, 12:16], over(qk_gain[:, 1], 4), ALU.mult))
                    if t >= NT_C:
                        rotate(ab_qk[:, t], rope_ax[:, t - NT_C], 16, 2, 16, tmp_a, tmp_b)
                    kd = ab_kd[:, t].rearrange("p (h c) -> p h c", h=4)
                    for j in range(2):
                        link(V.tensor_copy(kd[:, :, HD * j:HD * j + HD], x3[:, 12:16]))

            def two_halves(name, dst):
                g, b = await_group(name)
                src = flat(b, dst.shape[1] * P).rearrange("p (a c) -> p a c", c=P)
                link(V.tensor_copy(dst[0:64, :, 0], src[0:64]))
                link(V.tensor_copy(dst[64:128, :, 1], src[64:128]), free, g)

            def clear_others(dst):
                link(V.memset(dst[64:128, :, 0], 0.0))
                link(V.memset(dst[0:64, :, 1], 0.0))

            def ab_tr():
                for t in ALL:
                    take(("ab_q", t), ab_qT[:, :, tiles(t)], 768)
                clear_others(ab_kT)
                for t in ALL:
                    two_halves(("ab_k", t), ab_kT[:, :, :, tiles(t)])

            def max_of(s, u, m, n):
                dve.wait_ge(s["score_full"], u + 1)
                link(V.reduce_max(nmx[:, u % m:u % m + 1], flat(2 * (u % 2), n), axis=AX.X))
                link(V.tensor_scalar(nmx[:, u % m:u % m + 1], nmx[:, u % m:u % m + 1], -(HD ** -0.5), None, ALU.mult),
                     s["max_done"])

            def ab_att():
                s = A_

                def mx(u):
                    if u < len(AB_UNITS):
                        max_of(s, u, 4, ab_keys(AB_UNITS[u][1]) * P)

                def output(u):
                    h, t = AB_UNITS[u]
                    dve.wait_ge(s["o_full"], u + 1)
                    link(V.reciprocal(rsum[:, u % 4:u % 4 + 1], esum[:, u % 4:u % 4 + 1]))
                    link(V.tensor_scalar(O_all[:, t, HD * h:HD * h + HD], psum[:, 6 + u % 2, 0:HD],
                                         rsum[:, u % 4:u % 4 + 1], None, ALU.mult), s["o_done"])

                mx(0)
                mx(1)
                for u in range(len(AB_UNITS) + 1):
                    mx(u + 2)
                    if u:
                        output(u - 1)

            def ab_pool():
                wait_loads(dve, "ab_pool")
                for who, tl in (("x", TILES_X), ("c", TILES_C)):
                    for g in range(4):
                        take(("pooled", who, g), pooledT[:, g, 0:len(tl) * P], len(tl) * P, 64)
                    for t in tl:
                        g, b = await_group(("mixed", t))
                        link(V.tensor_tensor(O_all[:, t, 768:1024], psum[:, b, 0:256], pool_scale, ALU.mult),
                             free, g)

            def cd_u():
                take("conv_w", cd_wcol, 64)
                link(V.memset(cd_z, 0.0))
                for j in range(2):
                    g, b = await_group(("cd_u", j))
                    dve.wait_ge(gate_done, gate_base["cd_u"] + j + 1)
                    link(V.tensor_tensor(cd_z[:, j, 15:15 + SEQ], psum[:, b, :], cd_sg[:, j], ALU.mult),
                         free, g)

            def cd_conv_():
                wait_loads(dve, "cd_u")
                for j in range(2):
                    link(V.tensor_scalar(cd_acc[:, j], cd_z[:, j, 0:SEQ], cd_wcol[:, j, 0:1], cd_wcol[:, j, 31:32],
                                         ALU.mult, ALU.add))
                    for k in range(1, 31):
                        ins = V.scalar_tensor_tensor(cd_acc[:, j], cd_z[:, j, k:k + SEQ], cd_wcol[:, j, k:k + 1],
                                                     cd_acc[:, j], ALU.mult, ALU.add)
                        link(ins, sem("conv_done") if j == 1 and k == 30 else None)
                for t in range(NT_X):
                    take(("conv", t), cd_conv[:, t], 256)
                    statistics(cd_conv[:, t], t, 256)
                link(V.tensor_copy(rstd[:, 0:NT_X, 0], mv[:, 0:NT_X, 1]))
                root_of(rstd[:, 0:NT_X, 0], 1.0, EPS)
                for t in range(NT_X):
                    link(V.tensor_scalar(cd_conv[:, t], cd_conv[:, t], mv[:, t, 0:1], rstd[:, t, 0:1],
                                         ALU.subtract, ALU.mult))
                    link(V.tensor_tensor(cd_conv[:, t], cd_conv[:, t], cd_lng, ALU.mult))
                    link(V.tensor_tensor(cd_conv[:, t], cd_conv[:, t], cd_lnb, ALU.add),
                         sem("conv_normed") if t == NT_X - 1 else None)

            def cd_heads(name, turned, tl, put):
                def go():
                    if name == "cd_q":
                        clear_others(cd_qT)
                    for j, t in enumerate(tl):
                        await_read(dve, (name, 1, t))
                        if t >= NT_C:
                            for part in range(2):
                                rotate(cd_tmp[:, t % 4, 384 * part:384 * part + 384], rope_ax[:, t - NT_C], 6, 2, 16,
                                       cd_ta, cd_tb, sem(turned + "_roped") if part else None)
                        else:
                            dve.sem_inc(sem(turned + "_roped"), 1)
                        if j:
                            put(tl[j - 1])
                    put(tl[-1])
                return go

            def cd_att():
                wait_loads(dve, "cd_att")
                for i in range(2):
                    link(V.tensor_tensor(lam_in[:, 2 * i], lam_in[:, 2 * i], lam_in[:, 2 * i + 1], ALU.mult))
                    link(V.reduce_sum(lam[:, i:i + 1], lam_in[:, 2 * i], axis=AX.X), sem("lam_sum"))
                dve.wait_ge(sem("lam_exp"), 2)
                link(V.tensor_tensor(lam[:, 2:3], lam[:, 1:2], lam[:, 0:1], ALU.subtract))
                link(V.tensor_scalar(lam[:, 2:3], lam[:, 2:3], -LAM_INIT, None, ALU.add))
                s, n = C_, 2 * len(CD_UNITS)

                def mx(v):
                    if v < n:
                        max_of(s, v, 8, NT * P)

                def output(u):
                    h, t = CD_UNITS[u]
                    dve.wait_ge(s["o_full"], u + 1)
                    link(V.tensor_copy(O4[:, t, tiles(h)], psum[:, 6 + u % 2, 0:P]), s["o_done"])

                mx(0)
                mx(1)
                for u in range(len(CD_UNITS)):
                    v = 2 * u
                    dve.wait_ge(s["exp_done"], v + 2)
                    a = v % 8
                    link(V.reciprocal(rsum[:, a:a + 2], esum[:, a:a + 2]))
                    link(V.tensor_tensor(rsum[:, a + 1:a + 2], rsum[:, a + 1:a + 2], lam[:, 2:3], ALU.mult))
                    link(V.tensor_scalar(cd_P[:, v % 4], cd_P[:, v % 4], rsum[:, a:a + 1], None, ALU.mult))
                    link(V.scalar_tensor_tensor(cd_P[:, v % 4], cd_P[:, v % 4 + 1], rsum[:, a + 1:a + 2], cd_P[:, v % 4],
                                                ALU.mult, ALU.add), s["diff_done"])
                    mx(v + 2)
                    mx(v + 3)
                    if u:
                        output(u - 1)
                output(len(CD_UNITS) - 1)

            def cd_sub():
                for t in range(NT_X):
                    link(V.tensor_tensor(cd_sq, O4[:, t, 0:768], O4[:, t, 0:768], ALU.mult))
                    link(V.reduce_sum(rstd[:, t, 0:6], cd_sq.rearrange("p (h d) -> p h d", h=6), axis=AX.X))
                root_of(rstd[:, 0:NT_X, 0:6], 128.0, EPS)
                link(V.tensor_scalar(sub_gain, sub_gain, 1.0 - LAM_INIT, None, ALU.mult))
                for t in range(NT_X):
                    x3 = O4[:, t, 0:768].rearrange("p (h d) -> p h d", h=6)
                    link(V.tensor_tensor(x3, x3, per(rstd[:, t, 0:6], P), ALU.mult))
                    link(V.tensor_tensor(x3, x3, over(sub_gain, 6), ALU.mult))
                    link(V.tensor_copy(O4[:, t, 768:1024], cd_conv[:, t]))

            def ev_rope():
                wait_loads(dve, "ev_in")
                rotated = {0: (ev_qa, rope_ret, 4, 64), 1: (ev_ka, rope_ret, 4, 64), 4: (ev_qb, rope_win, 8, 32),
                           5: (ev_kv, rope_win, 2, 32)}
                for piece in split_order["ev_in"]:
                    if piece[0] != "work":
                        low_part("ev_in", piece)
                        continue
                    c = piece[1]
                    if c not in rotated:
                        continue
                    x, table, heads, half = rotated[c]
                    for t in range(NT_X):
                        await_read(dve, ("ev_in", c, NT_C + t))
                        rotate(x[:, t] if c < 5 else x[:, t, 0:P], table[:, t], heads, 1, half, ev_ta, ev_tb)
                        if c == 5:
                            kd = ev_kbd[:, t].rearrange("p (h c) -> p h c", h=2)
                            for j in range(2):
                                link(V.tensor_copy(kd[:, :, HD * j:HD * j + HD],
                                                   ev_kv[:, t, 0:P].rearrange("p (h d) -> p h d", h=2)))

            def ev_tr():
                for name, dst, n in (("ev_qa", ev_qaT, 512), ("ev_ka", ev_kaT, 512), ("ev_qb", ev_qbT, 512),
                                     ("ev_kb", ev_kbT, 256)):
                    for t in range(NT_X):
                        take((name, t), dst[:, :, tiles(t)], n)

            def ev_ret():
                wait_loads(dve, "ev_ret")
                link(V.tensor_scalar(lg[:, 2], decay, -1.0, None, ALU.mult))
                link(V.tensor_tensor(lg[:, 0], decay, lg[:, 2], ALU.max), sem("decay_abs"))
                dve.wait_ge(sem("decay_exp"), 1)
                link(V.tensor_scalar(lg[:, 2], lg[:, 1], 2.0, None, ALU.add))
                link(V.reciprocal(lg[:, 2], lg[:, 2]))
                link(V.tensor_tensor(lg[:, 1], lg[:, 1], lg[:, 2], ALU.mult))
                link(V.tensor_tensor(lg[:, 2], lg[:, 1], lg[:, 1], ALU.mult))
                link(V.tensor_scalar(lg[:, 3], lg[:, 2], 1.0 / 17, 1.0 / 15, ALU.mult, ALU.add))
                for d in (13, 11, 9, 7, 5, 3, 1):
                    link(V.tensor_tensor(lg[:, 3], lg[:, 3], lg[:, 2], ALU.mult))
                    link(V.tensor_scalar(lg[:, 3], lg[:, 3], 1.0 / d, None, ALU.add))
                link(V.tensor_tensor(lg[:, 3], lg[:, 3], lg[:, 1], ALU.mult))
                link(V.tensor_scalar(lg[:, 3], lg[:, 3], -2.0, None, ALU.mult))
                link(V.tensor_scalar(lg[:, 2], decay, 0.0, None, ALU.min))
                link(V.tensor_tensor(lg[:, 4], lg[:, 3], lg[:, 2], ALU.add))

                def decay_of(h):
                    if h >= 4:
                        return
                    D_ = ev_D[h % 2]
                    for mt in range(NT_X):
                        at = 384 - P * mt
                        link(V.tensor_scalar(D_[:, mt], dist[:, 0, at:at + SEQ], lg[:, 4, 0, h:h + 1], None, ALU.mult))
                        link(V.scalar_tensor_tensor(D_[:, mt], dist[:, 1, at:at + SEQ], lg[:, 4, 1, h:h + 1],
                                                    D_[:, mt], ALU.mult, ALU.add),
                             sem("decay_arg") if mt == NT_X - 1 else None)

                decay_of(0)
                decay_of(1)
                for h in range(4):
                    dve.wait_ge(sem("decay_done"), h + 1)
                    for mt in range(NT_X):
                        g, b = await_group(("ret_s", h, mt))
                        link(V.scalar_tensor_tensor(ev_ST[:, mt], psum[:, b, :], P ** -0.5, ev_D[h % 2][:, mt],
                                                    ALU.mult, ALU.mult), free, g)
                    decay_of(h + 2)
                    for t in range(NT_X):
                        take(("ret_y", h, t), O4[:, t, tiles(h)], P)
                for t in range(NT_X):
                    for h in range(4):
                        link(V.bn_stats(stat[:, 0, 0], O4[:, t, tiles(h)]))
                        link(V.bn_aggr(ret_mv[:, t, h], stat[:, 0, 0:1]))
                        link(V.tensor_copy(rstd[:, t, h:h + 1], ret_mv[:, t, h, 1:2]))
                root_of(rstd[:, 0:NT_X, 0:4], 1.0, GN_EPS)
                dve.wait_ge(sem("ret_gate"), 1)
                for t in range(NT_X):
                    for h in range(4):
                        link(V.tensor_scalar(O4[:, t, tiles(h)], O4[:, t, tiles(h)], ret_mv[:, t, h, 0:1],
                                             rstd[:, t, h:h + 1], ALU.subtract, ALU.mult))
                    link(V.tensor_tensor(O4[:, t, 0:512], O4[:, t, 0:512], gn_row, ALU.mult))
                    link(V.tensor_tensor(O4[:, t, 0:512], O4[:, t, 0:512], ev_ga[:, t], ALU.mult))

            def ev_win():
                wait_loads(dve, "ev_win")

                def masked(u):
                    if u >= len(WIN_UNITS):
                        return
                    h, t = WIN_UNITS[u]
                    ks = win_keys(t)
                    n = len(ks) * P
                    g, b = await_group(("win_s", u))
                    first = ks[0] - t + 1
                    link(V.scalar_tensor_tensor(ev_Sm[:, u % 2, 0:n], psum[:, b, 0:n], HD ** -0.5,
                                                band[:, first:first + len(ks)].rearrange("p a c -> p (a c)"),
                                                ALU.mult, ALU.add), free, g)
                    link(V.tensor_copy(ev_Sm[:, u % 2, n:n + 1], sinks[:, h:h + 1]))
                    link(V.reduce_max(nmx[:, u % 4:u % 4 + 1], ev_Sm[:, u % 2, 0:n + 1], axis=AX.X))
                    link(V.tensor_scalar(nmx[:, u % 4:u % 4 + 1], nmx[:, u % 4:u % 4 + 1], -1.0, None, ALU.mult),
                         sem("win_max_done"))

                def output(u):
                    h, t = WIN_UNITS[u]
                    g, b = await_group(("win_o", u))
                    a = slice(u % 4, u % 4 + 1)
                    link(V.tensor_tensor(rsum[:, a], esum[:, a], esum[:, 4 + u % 4:5 + u % 4], ALU.add))
                    link(V.reciprocal(rsum[:, a], rsum[:, a]))
                    link(V.tensor_scalar(O4[:, t, 512 + HD * h:576 + HD * h], psum[:, b, 0:HD], rsum[:, a], None,
                                         ALU.mult), free, g)

                masked(0)
                masked(1)
                for u, (h, t) in enumerate(WIN_UNITS):
                    take(("win_pt", u), ev_PT[:, u % 2, 0:P * len(win_keys(t))], P * len(win_keys(t)))
                    masked(u + 2)
                    if u:
                        output(u - 1)
                output(len(WIN_UNITS) - 1)

            def route(m):
                def go():
                    s = [mo_s[:, j] for j in range(16)]
                    wait_loads(dve, f"r{m}_route")
                    link(V.memset(mo_C8, -3e38))
                    link(V.memset(mo_idxf, BIG_IDX))
                    link(V.memset(mo_xg, 0.0))
                    g, b = await_group(("logits", m))
                    link(V.tensor_tensor(mo_L, psum[:, b, 0:144].rearrange("p (t c) -> p t c", c=36),
                                         over(mo_bias, NT_X), ALU.add), free, g)
                    link(V.tensor_copy(mo_C8[:, :, 0:4], mo_L[:, :, 0:4]))
                    for t in range(NT_X):
                        link(V.max(mo_m8[:, t], mo_C8[:, t]))
                        link(V.max_index(mo_ix[:, t], mo_m8[:, t], mo_C8[:, t]))
                    link(V.tensor_copy(mo_ixf, mo_ix))
                    link(V.tensor_copy(s[0], mo_ixf[:, :, 0]))
                    link(V.tensor_tensor(mo_C8[:, :, 0:4], mo_C8[:, :, 0:4], per(mo_m8[:, :, 0], 4), ALU.subtract),
                         M(m, "coarse_shifted"))
                    for t in range(NT_X):
                        link(V.tensor_scalar(mo_G[:, t], mo_iota[:, 0:4], s[0][:, t:t + 1], None, ALU.is_equal))
                    for q in range(4):
                        fine = mo_L[:, :, 4 + 8 * q:12 + 8 * q]
                        dst = mo_FS if q == 0 else mo_t8
                        link(V.tensor_tensor(dst, fine, per(mo_G[:, :, q], 8), ALU.mult))
                        if q:
                            link(V.tensor_tensor(mo_FS, mo_FS, mo_t8, ALU.add))
                    for t in range(NT_X):
                        link(V.max(mo_m8[:, t], mo_FS[:, t]))
                        link(V.max_index(mo_ix[:, t], mo_m8[:, t], mo_FS[:, t]))
                    link(V.tensor_copy(mo_ixf, mo_ix))
                    for j in range(2):
                        link(V.scalar_tensor_tensor(s[4 + j], s[0], 8.0, mo_ixf[:, :, j], ALU.mult, ALU.add))
                    link(V.tensor_tensor(s[2], mo_m8[:, :, 1], mo_m8[:, :, 0], ALU.subtract), M(m, "fine_diff"))
                    for t in range(NT_X):
                        link(V.tensor_scalar(mo_A1[:, t], mo_iota[:, 0:NE], s[4][:, t:t + 1], None, ALU.is_equal))
                        link(V.tensor_scalar(mo_A2[:, t], mo_iota[:, 0:NE], s[5][:, t:t + 1], None, ALU.is_equal))
                    link(V.tensor_tensor(mo_A, mo_A1, mo_A2, ALU.add), M(m, "picked"))
                    dve.wait_ge(M(m, "coarse_exp"), 1)
                    link(V.reduce_sum(s[6], mo_C8[:, :, 0:4], axis=AX.X))
                    link(V.reciprocal(s[6], s[6]))
                    dve.wait_ge(M(m, "fine_exp"), 1)
                    link(V.tensor_scalar(s[7], s[3], 1.0, None, ALU.add))
                    link(V.reciprocal(s[7], s[7]))
                    link(V.tensor_tensor(s[8], s[7], s[6], ALU.mult))
                    link(V.tensor_tensor(s[9], s[8], s[3], ALU.mult))
                    link(V.memset(mo_F[:, :, :, 0], 1.0))
                    for t in range(NT_X):
                        link(V.tensor_scalar(mo_F[:, t, :, 1], mo_F[:, t, :, 0], mo_tok[:, t:t + 1], None, ALU.mult))
                        link(V.tensor_scalar(mo_F[:, t, :, 2], mo_A2[:, t], float(SEQ), mo_tok[:, t:t + 1],
                                             ALU.mult, ALU.add))
                        link(V.tensor_scalar(mo_F[:, t, :, 3], mo_A1[:, t], s[8][:, t:t + 1], None, ALU.mult))
                        link(V.scalar_tensor_tensor(mo_F[:, t, :, 3], mo_A2[:, t], s[9][:, t:t + 1],
                                                    mo_F[:, t, :, 3], ALU.mult, ALU.add))
                    g, b = await_group(("rank", m))
                    link(V.scalar_tensor_tensor(mo_RK, psum[:, b, 0:P].rearrange("p (t e) -> p t e", t=NT_X), 1.0, mo_A,
                                                ALU.add, ALU.mult))
                    link(V.tensor_scalar(mo_RK, mo_RK, -1.0, None, ALU.add))
                    link(V.reduce_max(mo_np[:, 0:1], psum[:, b, P:P + NE], axis=AX.X), free, g)
                    for j in range(1, NT_X):
                        link(V.tensor_scalar(mo_np[:, j:j + 1], mo_np[:, 0:1], P * j + 0.5, None, ALU.is_ge))
                    for j in range(2, NT_X):
                        link(V.tensor_tensor(mo_np[:, 1:2], mo_np[:, 1:2], mo_np[:, j:j + 1], ALU.add))
                    link(V.tensor_scalar(mo_np[:, 1:2], mo_np[:, 1:2], 1.0, None, ALU.add))
                    link(V.tensor_copy(mo_npi[:, 0:1], mo_np[:, 1:2]))
                return go

            def experts(m):
                chain = Link(dve, M(m, "dve_chain"))

                def one_pass(p):
                    first = isinstance(p, int)
                    chain.n, chain.at = {}, {M(m, "dve_chain").name: p * DVE_PER_PASS,
                                             M(m, "sel_ready").name: p * NE}
                    if not first:
                        dve.wait_ge(M(m, "pass_done"), p)
                        chain(V.tensor_scalar(mo_RK, mo_RK, -float(P), None, ALU.add))
                    else:
                        chain(V.tensor_copy(mo_RK, mo_RK))
                    for e in range(NE):
                        if not first or e >= 2:
                            dve.wait_ge(M(m, "sel_used"), p * NE + e - 1)
                        for t in range(NT_X):
                            ins = V.tensor_scalar(mo_sel[:, 4 * (e % 2) + t], mo_iota, mo_RK[:, t, e:e + 1], None,
                                                  ALU.is_equal)
                        chain(ins, M(m, "sel_ready"))
                    dve.wait_ge(M(m, "sel_used"), p * NE + NE)
                    chain(V.tensor_copy(mo_meta, psum[:, 7, 0:P].rearrange("p (e f) -> p e f", f=4)))
                    for j in range(2):
                        chain(V.tensor_scalar(mo_idxf[:, j, 0:NE], mo_meta[:, :, 0], -BIG_IDX, BIG_IDX,
                                              ALU.mult, ALU.add))
                        chain(V.tensor_tensor(mo_idxf[:, j, 0:NE], mo_idxf[:, j, 0:NE], mo_meta[:, :, 1 + j], ALU.add))
                    chain(V.tensor_copy(mo_gate, mo_meta[:, :, 3]))
                    chain(V.tensor_copy(mo_idx, mo_idxf))
                    V.tensor_copy(mo_cnt[:, 0:1], mo_np[:, 0:1]).then_inc(M(m, "lists_ready"), 1)
                    with dve.Fori(0, NE // 2) as i:
                        chain.n, chain.at = {}, {M(m, n).name: p * NE + i * 2 + c for n, c in
                                                 (("h_ready", 0), ("gu_free", 1), ("y_free", 1), ("y_ready", 0))}
                        for b in range(2):
                            e = p * NE + i * 2 + b
                            dve.wait_ge(M(m, "sg_done"), e + 1)
                            dve.wait_ge(M(m, "gu_full"), e + 1)
                            chain(V.tensor_tensor(mo_h, psum[:, 1, :], mo_sg, ALU.mult), M(m, "h_ready"))
                            dve.sem_inc(M(m, "gu_free"), 1)
                            dve.wait_ge(M(m, "y_full"), e + 1)
                            dve.wait_ge(M(m, "y_buf_free"), e + 1)
                            chain(V.tensor_scalar(mo_y[:, b], flat(5, D), mo_gate[:, bass.ds(i * 2 + b, 1)], None,
                                                  ALU.mult), M(m, "y_ready"))
                            dve.sem_inc(M(m, "y_free"), 1)

                def go():
                    dve.sem_inc(M(m, "gu_free"), 1)
                    dve.sem_inc(M(m, "y_free"), 1)
                    one_pass(0)
                    more_passes(dve, m, one_pass)
                return go

            def moe_norm(m):
                def go():
                    wait_loads(dve, f"r{m}_norm")
                    for j, t in enumerate(TILES_X):
                        link(V.tensor_tensor(mo_y12[:, 0, j], mo_y12[:, 0, j], mo_y12[:, 1, j], ALU.add))
                        link(V.scalar_tensor_tensor(X[:, t], X[:, t], ALPHA, mo_y12[:, 0, j], ALU.mult, ALU.add))
                        norm_tile(j, t, rows_moe, LN_EPS2)
                        if m == 0 and j:
                            copied("r0_norm_t")(t - 1)
                    if m == 0:
                        copied("r0_norm_t")(TILES_X[-1])
                return go

            steps = {
                "mod0": mod(0), "modT0": mod_t(0), "mod1": mod(1), "modT1": mod_t(1),
                "ab_ht": modulated("ab_ht", ALL, 0), "ab_in": ab_rope, "ab_tr": ab_tr, "ab_att": ab_att,
                "ab_pool": ab_pool, "ab_ot": plain("ab_ot", ALL, OT_ab, D),
                "ab_out": out_norm("ab_out", ALL, rows_ab, EPS, True, modulate("ab_out_t", 24)),
                "cd_ht": modulated("cd_ht", ALL, 0), "cd_u": cd_u, "cd_conv": cd_conv_,
                "cd_q": cd_heads("cd_q", "cd_qt", TILES_X,
                                 lambda t: two_halves(("cd_qt", t), cd_qT[:, :, :, tiles(t - NT_C)])),
                "cd_k": cd_heads("cd_k", "cd_kt", ALL, lambda t: take(("cd_kt", t), cd_kT[:, :, tiles(t)], 768)),
                "cd_att": cd_att, "cd_sub": cd_sub, "cd_ot": plain("cd_ot", TILES_X, OT_cd, D, NT_C),
                "cd_out": out_norm("cd_out", TILES_X, rows_cd, EPS, True, modulate("cd_out_t", 24)),
                "ev_in": ev_rope, "ev_tr": ev_tr, "ev_ret": ev_ret,
                "ev_win": ev_win, "ev_ot": plain("ev_ot", TILES_X, OT_ev, D, NT_C),
                "ev_out": out_norm("ev_out", TILES_X, rows_ev, LN_EPS2, False, copied("ev_out_t")),
                "fo_out": out_norm("fo_out", TILES_X, rows_fo, LN_EPS2, False, copied("fo_out_t")),
                "f0x_in": product("f0x", SEQ), "f0c_in": product("f0c", CTX), "f1x_in": product("f1x", SEQ),
                "f0x_out": out_norm("f0x_out", TILES_X, rows_ffn, EPS, True),
                "f0c_out": out_norm("f0c_out", TILES_C, rows_ffn, EPS, True),
                "f1x_out": out_norm("f1x_out", TILES_X, rows_ffn, EPS, True, copied("f1x_out_t")),
            }
            for m in range(2):
                steps[f"r{m}_route"] = route(m)
                steps[f"r{m}_experts"] = experts(m)
                steps[f"r{m}_norm"] = moe_norm(m)
            run(dve, steps, stage_dve)

        @block.gpsimd
        def _(pool):
            def loads(stage):
                for dst, src in LOADS[stage]:
                    pool.dma_start(dst, src, allow_slow_non_contiguous=stage[:3] == "mod").then_inc(sem("loads_" + stage), 16)

            def store_mod(l):
                def go():
                    pool.dma_start(A["mod"][l], mod_rows).then_inc(sem("mod_stored"), 16)
                    pool.wait_ge(sem("mod_stored"), 16 * (l + 1))
                return go

            def route(m):
                def go():
                    loads(f"r{m}_route")
                    for t in range(NT_X):
                        pool.dma_start(A[f"xs{m}"][tiles(t)], X[:, NT_C + t]).then_inc(M(m, "x_stored"), 16)
                    pool.wait_ge(M(m, "x_stored"), 16 * NT_X)
                return go

            def await_count(s, value):
                pool.wait_ge(s, value)
                if not isinstance(value, int):
                    pool.sem_inc(sem("pool_steps"), 1)

            def experts(m):
                def one_pass(p):
                    await_count(M(m, "lists_ready"), p + 1)

                    def gather(e):
                        if e > NE:
                            return
                        if e >= 2:
                            await_count(M(m, "xt_full"), p * (NE + 1) + e - 1)
                        pool.indirect_dma_start(
                            out=mo_xg[:, e % 2], out_offset=None, in_=A[f"xs{m}"][:, :],
                            in_offset=bass.IndirectOffsetOnAxis(ap=mo_idx[:, 0, e:e + 1], axis=0),
                            bounds_check=SEQ - 1, oob_is_err=False).then_inc(M(m, f"xg_ready{e % 2}"), 16)

                    def buffer_free(e):
                        await_count(M(m, f"y_stored{e % 2}"), (p * (NE // 2) + e // 2 + 1) * 16)
                        pool.sem_inc(M(m, "y_buf_free"), 1)

                    gather(0)
                    gather(1)
                    for e in range(NE):
                        gather(e + 2)
                        await_count(M(m, "y_ready"), p * NE + e + 1)
                        pool.indirect_dma_start(
                            out=A[f"y{m}"][:, :], out_offset=bass.IndirectOffsetOnAxis(ap=mo_idx[:, 1, e:e + 1], axis=0),
                            in_=mo_y[:, e % 2], in_offset=None,
                            bounds_check=2 * SEQ - 1, oob_is_err=False).then_inc(M(m, f"y_stored{e % 2}"), 16)
                        if e >= 1:
                            buffer_free(e - 1)
                    buffer_free(NE - 1)
                    await_count(M(m, "xg_ready0"), p * (17 * 16) + 17 * 16)
                    pool.sem_inc(M(m, "pass_done"), 1)

                def go():
                    pool.sem_inc(M(m, "y_buf_free"), 2)
                    one_pass(0)
                    more_passes(pool, m, one_pass)
                    pool.sem_inc(M(m, "y_complete"), 1)
                return go

            steps = {s: (lambda s: lambda: loads(s))(s) for s in LOADS}
            steps["modT0"], steps["modT1"] = store_mod(0), store_mod(1)
            for m in range(2):
                steps[f"r{m}_route"], steps[f"r{m}_experts"] = route(m), experts(m)
            run(pool, steps)
            for t in range(NT_X):
                pool.dma_start(A["out"][0, tiles(t)], X[:, NT_C + t]).then_inc(sem("stored"), 16)
            pool.wait_ge(sem("stored"), 16 * NT_X)

        @block.sync
        def _(sp):
            sp.dma_start(ident, A["ident"]).then_inc(sem("ident_loaded"), 16)
            for t in range(NT_C):
                sp.dma_start(X[:, t], A["ctx"][0, tiles(t)]).then_inc(sem("x_loaded"), 16)
            for t in range(NT_X):
                sp.dma_start(X[:, NT_C + t], A["x"][0, tiles(t)]).then_inc(sem("x_loaded"), 16)
            used = [c for c in range(len(chunks)) if c in chunk_read]
            last_user = {}

            def load(i):
                ch = chunks[i]
                if ch["slot"] in last_user:
                    sp.wait_ge(*chunk_read[last_user[ch["slot"]]])
                last_user[ch["slot"]] = i
                if ch["split"]:
                    last_user[3 + ch["high"]] = i
                for c0, src in ch["parts"]:
                    n = src.shape[2]
                    sp.dma_start(slot(i)[:, :, c0:c0 + n], src).then_inc(w_ready[ch["slot"]], 16)

            def expert_weights(m):
                first = STAGES.index(f"r{m}_experts")

                def one(p, i, b, part, wait=True):
                    if wait:
                        e1 = p * NE + i * 2 + b - 1
                        sp.wait_ge(M(m, "gu_full" if part < 2 else "y_full"), e1)
                    name = ("expert_w_gate_2", "expert_w_up_2", "expert_w_down_2")[part]
                    src = A[name][m, bass.ds(i * 2 + b, 1)].rearrange("o (k p) n -> p (o k) n", p=P)
                    dst = region(MOE_RING_KB[3 * b + part], KD if part < 2 else 4, 512 if part < 2 else D)
                    sp.dma_start(dst, src).then_inc(M(m, f"w_ready{3 * b + part}"), 16)

                for b in range(2):
                    for part in range(3):
                        s = 3 * b + part
                        if s < 5 and s in last_user:
                            sp.wait_ge(*chunk_read[last_user[s]])
                        else:
                            sp.wait_ge(stage_act, first)
                            sp.wait_ge(stage_dve, first)
                        one(0, 0, b, part, wait=False)
                with sp.Fori(1, NE // 2) as i:
                    for b in range(2):
                        for part in range(3):
                            one(0, i, b, part)

                def one_pass(p):
                    with sp.Fori(0, NE // 2) as i:
                        for b in range(2):
                            for part in range(3):
                                one(p, i, b, part)

                sp.wait_ge(stage_act, first)
                sp.wait_ge(stage_dve, first)
                more_passes(sp, m, one_pass)
                sp.wait_ge(stage_act, first + 1)
                sp.wait_ge(stage_dve, first + 1)
                last_user.clear()
                if f"r{m}_norm" in STAGES:
                    sp.wait_ge(M(m, "y_complete"), 1)
                    for dst, src in Y_LOADS[f"r{m}_norm"]:
                        sp.dma_start(dst, src).then_inc(sem(f"loads_r{m}_norm"), 16)

            for i in used:
                if i == before_experts0 and "r0_experts" in STAGES:
                    expert_weights(0)
                load(i)
            if used and used[-1] < before_experts0 and "r0_experts" in STAGES:
                expert_weights(0)
            if "r1_experts" in STAGES:
                expert_weights(1)


_INS = """x c ctx c_ctx ab_w_in ab_q_gain ab_k_gain ab_w_pool ab_pool_scale ab_w_out cd_w_in cd_lambda_q1 cd_lambda_k1
    cd_lambda_q2 cd_lambda_k2 cd_subln_gain cd_conv_w cd_conv_b cd_conv_ln_g cd_conv_ln_b cd_w_out ada_w ada_b ln1_g
    ln1_b ln2_g ln2_b ffn_w_in ffn_w_out w_in_even_2 ret_decay_logit_2 ret_gn_gain_2 sink_logit_2 w_out_even_2
    w_out_fourier_2 ln1_gain_2 ln1_bias_2 ln2_gain_2 ln2_bias_2 router_coarse_w_2 router_coarse_b_2 router_fine_w_2
    router_fine_b_2 expert_w_gate_2 expert_w_up_2 expert_w_down_2""".split()
STOP = None


def kernel(**inputs):
    import concourse.bacc as bacc
    from concourse.bass_utils import run_bass_kernel_spmd

    nc = bacc.Bacc("TRN2", target_bir_lowering=False, num_devices=1)
    arrays = {n: np.ascontiguousarray(inputs[n]) for n in _INS}
    arrays.update(constants())
    aps = {n: nc.dram_tensor(f"in_{n}", a.shape, F32, kind="ExternalInput").ap() for n, a in arrays.items()}
    for n, shape in (("mod", (2, 2, 6 * D)), ("xs0", (SEQ, D)), ("xs1", (SEQ, D)), ("y0", (2 * SEQ, D)),
                     ("y1", (2 * SEQ, D))):
        aps[n] = nc.dram_tensor(n, shape, F32, kind="Internal").ap()
    aps["out"] = nc.dram_tensor("out", (1, SEQ, D), F32, kind="ExternalOutput").ap()
    build(nc, aps, STOP)
    r = run_bass_kernel_spmd(nc, [{f"in_{n}": a for n, a in arrays.items()}], core_ids=[0])
    return r.results[0]["out"]
```
